# Optimizing a Trainium2 kernel written in Bass

```python
import jax, jax.numpy as jnp
from jax import lax
import numpy as np

D_MODEL = 1024
BATCH = 1
SEQ = 512
DEPTH = 2

N_MIXERS = 2
N_LAYERS_A = (DEPTH + 1) // 2
N_LAYERS_B = DEPTH // 2
FOX_HEADS = 16
FOX_HEAD_DIM = D_MODEL // FOX_HEADS
Q_BLOCK = 128
FOX_IN = 4 * D_MODEL + FOX_HEADS
RET_HEADS = 4
RET_QK_DIM = D_MODEL // RET_HEADS
RET_V_DIM = 2 * D_MODEL // RET_HEADS
RET_CHUNK = 128
RET_IN = 2 * RET_HEADS * RET_QK_DIM + 2 * RET_HEADS * RET_V_DIM
N_GROUPS = 4
EXPERTS_PER_GROUP = 8
N_EXPERTS = N_GROUPS * EXPERTS_PER_GROUP
TOP_K = 2
EXPERT_FF = D_MODEL // 2
MOE_BLOCK = 128

EPS = 1e-6
NEG_INF = -1e30
ROPE_BASE = 10000.0


F32 = jnp.float32

def rms_norm(x, g):
    xf = x.astype(F32)
    y = xf * lax.rsqrt(jnp.mean(xf * xf, axis=-1, keepdims=True) + EPS)
    return (y * g.astype(F32)).astype(x.dtype)

def forgetting_attention(h, w_in, b_f, w_out):
    B, S, _ = h.shape
    H, dh = FOX_HEADS, FOX_HEAD_DIM
    proj = h @ w_in
    q, k, v, gate = jnp.split(proj[..., :4 * D_MODEL], 4, axis=-1)
    f_logit = (proj[..., 4 * D_MODEL:] + b_f).astype(F32)
    cum = jnp.cumsum(jax.nn.log_sigmoid(f_logit), axis=1).transpose(0, 2, 1)
    heads = lambda t: t.reshape(B, S, H, dh).transpose(0, 2, 1, 3)
    q, k, v = heads(q), heads(k), heads(v)
    scale = dh ** -0.5
    k_pos = jnp.arange(S)

    def query_block(i):
        start = i * Q_BLOCK
        q_b = lax.dynamic_slice_in_dim(q, start, Q_BLOCK, axis=2)
        c_b = lax.dynamic_slice_in_dim(cum, start, Q_BLOCK, axis=2)
        s = jnp.einsum('bhqd,bhkd->bhqk', q_b, k).astype(F32) * scale
        s = s + c_b[..., :, None] - cum[..., None, :]
        q_pos = start + jnp.arange(Q_BLOCK)
        s = jnp.where(k_pos[None, :] <= q_pos[:, None], s, NEG_INF)
        p = jax.nn.softmax(s, axis=-1)
        return jnp.einsum('bhqk,bhkd->bhqd', p.astype(v.dtype), v)

    o = lax.map(query_block, jnp.arange(S // Q_BLOCK))
    o = o.transpose(1, 0, 3, 2, 4).reshape(B, S, D_MODEL)
    o = o * jax.nn.sigmoid(gate)
    return o @ w_out

def rotary(t, pos):
    d = t.shape[-1]
    inv = 1.0 / (ROPE_BASE ** jnp.linspace(0.0, 1.0, d // 2, dtype=F32))
    ang = pos.astype(F32)[:, None] * inv[None, :]
    cos, sin = jnp.cos(ang), jnp.sin(ang)
    t1, t2 = t[..., :d // 2].astype(F32), t[..., d // 2:].astype(F32)
    return jnp.concatenate([t1 * cos - t2 * sin, t1 * sin + t2 * cos], axis=-1)

def retention(h, w_in, gn_gain, w_out):
    B, S, _ = h.shape
    H, dk, dv, C = RET_HEADS, RET_QK_DIM, RET_V_DIM, RET_CHUNK
    proj = h @ w_in
    q, k, v, gate = jnp.split(proj, [H * dk, 2 * H * dk, 2 * H * dk + H * dv], axis=-1)
    heads = lambda t, d: t.reshape(B, S, H, d).transpose(0, 2, 1, 3)
    pos = jnp.arange(S)
    q = rotary(heads(q, dk), pos)
    k = rotary(heads(k, dk), pos) * (dk ** -0.5)
    v = heads(v, dv).astype(F32)

    log_g = jnp.log(1.0 - 2.0 ** (-5.0 - jnp.arange(H, dtype=F32)))
    idx = jnp.arange(C, dtype=F32)
    rel = idx[:, None] - idx[None, :]
    intra = jnp.where(rel >= 0, jnp.exp(log_g[:, None, None] * jnp.maximum(rel, 0.0)), 0.0)
    q_decay = jnp.exp(log_g[:, None] * (idx + 1.0))[None, :, :, None]
    k_decay = jnp.exp(log_g[:, None] * (C - 1.0 - idx))[None, :, :, None]
    chunk_decay = jnp.exp(log_g * C)[None, :, None, None]

    n_chunks = S // C
    to_chunks = lambda t: t.reshape(B, H, n_chunks, C, t.shape[-1]).transpose(2, 0, 1, 3, 4)

    def step(R, qkv):
        q_n, k_n, v_n = qkv
        s = jnp.einsum('bhid,bhjd->bhij', q_n, k_n) * intra
        o = jnp.einsum('bhij,bhje->bhie', s, v_n)
        o = o + jnp.einsum('bhid,bhde->bhie', q_n, R) * q_decay
        R = R * chunk_decay + jnp.einsum('bhjd,bhje->bhde', k_n * k_decay, v_n)
        return R, o

    R0 = jnp.zeros((B, H, dk, dv), F32)
    _, o = lax.scan(step, R0, (to_chunks(q), to_chunks(k), to_chunks(v)))
    o = o.transpose(1, 0, 3, 2, 4).reshape(B, S, H, dv)
    mu = jnp.mean(o, axis=-1, keepdims=True)
    var = jnp.mean(jnp.square(o - mu), axis=-1, keepdims=True)
    o = ((o - mu) * lax.rsqrt(var + EPS)).reshape(B, S, H * dv) * gn_gain.astype(F32)
    o = jax.nn.silu(gate.astype(F32)) * o
    return o.astype(h.dtype) @ w_out

def grouped_experts(xf, expert_id, gates, w_gu, w_down):
    T, D = xf.shape
    A = T * TOP_K
    flat_e = expert_id.reshape(A)
    order = jnp.argsort(flat_e)
    sorted_e = flat_e[order]
    counts = jnp.bincount(flat_e, length=N_EXPERTS)
    padded = (counts + MOE_BLOCK - 1) // MOE_BLOCK * MOE_BLOCK
    pad_end = jnp.cumsum(padded)
    pad_start = pad_end - padded
    start = jnp.cumsum(counts) - counts
    dest = pad_start[sorted_e] + jnp.arange(A) - start[sorted_e]
    n_blocks = (A + N_EXPERTS * (MOE_BLOCK - 1) + MOE_BLOCK - 1) // MOE_BLOCK
    n_rows = n_blocks * MOE_BLOCK
    tok_sorted = (order // TOP_K).astype(jnp.int32)
    row_tok = jnp.full((n_rows,), T, jnp.int32).at[dest].set(tok_sorted)
    x_pad = jnp.concatenate([xf, jnp.zeros((1, D), xf.dtype)], axis=0)
    x_rows = x_pad[row_tok].reshape(n_blocks, MOE_BLOCK, D)
    block_e = jnp.minimum(jnp.searchsorted(pad_end, jnp.arange(n_blocks) * MOE_BLOCK, side='right'),
                          N_EXPERTS - 1)

    def expert_block(args):
        xb, e = args
        a, b = jnp.split(xb @ w_gu[e], 2, axis=-1)
        return (jax.nn.silu(a) * b) @ w_down[e]

    y_rows = lax.map(expert_block, (x_rows, block_e)).reshape(n_rows, D)
    w_sorted = gates.reshape(A)[order].astype(y_rows.dtype)
    return jax.ops.segment_sum(y_rows[dest] * w_sorted[:, None], tok_sorted, num_segments=T)

def hier_moe(h, wr_g, br_g, wr_e, br_e, w_gu, w_down):
    B, S, D = h.shape
    T = B * S
    xf = h.reshape(T, D)
    p_group = jax.nn.softmax((xf @ wr_g).astype(F32) + br_g.astype(F32), axis=-1)
    pg, gi = lax.top_k(p_group, 1)
    e_logits = ((xf @ wr_e).astype(F32) + br_e.astype(F32)).reshape(T, N_GROUPS, EXPERTS_PER_GROUP)
    e_in = jnp.einsum('tge,tg->te', e_logits, jax.nn.one_hot(gi[:, 0], N_GROUPS, dtype=F32))
    pv, pi = lax.top_k(jax.nn.softmax(e_in, axis=-1), TOP_K)
    gates = pg * pv / jnp.sum(pv, axis=-1, keepdims=True)
    expert_id = gi * EXPERTS_PER_GROUP + pi
    return grouped_experts(xf, expert_id, gates, w_gu, w_down).reshape(B, S, D)

def first_inputs(seed: int = 0) -> dict:
    key = jax.random.key(seed)
    ks = jax.random.split(key, 17)
    nrm = lambda k, shape, fan_in: jax.random.normal(k, shape, F32) * (fan_in ** -0.5)
    out_scale = (2.0 * DEPTH) ** -0.5
    return {
        "x": jax.random.normal(ks[0], (BATCH, SEQ, D_MODEL), F32),
        "fox_w_in": nrm(ks[1], (N_LAYERS_A, D_MODEL, FOX_IN), D_MODEL),
        "fox_b_f": 3.0 + 0.5 * jax.random.normal(ks[2], (N_LAYERS_A, FOX_HEADS), F32),
        "fox_w_out": nrm(ks[3], (N_LAYERS_A, D_MODEL, D_MODEL), D_MODEL) * out_scale,
        "ret_w_in": nrm(ks[4], (N_LAYERS_B, D_MODEL, RET_IN), D_MODEL),
        "ret_gn_gain": 1.0 + 0.02 * jax.random.normal(ks[5], (N_LAYERS_B, RET_HEADS * RET_V_DIM), F32),
        "ret_w_out": nrm(ks[6], (N_LAYERS_B, RET_HEADS * RET_V_DIM, D_MODEL), RET_HEADS * RET_V_DIM) * out_scale,
        "norm_mix": 1.0 + 0.02 * jax.random.normal(ks[7], (DEPTH, D_MODEL), F32),
        "norm_ffn": 1.0 + 0.02 * jax.random.normal(ks[8], (DEPTH, D_MODEL), F32),
        "router_group_w": nrm(ks[9], (DEPTH, D_MODEL, N_GROUPS), D_MODEL),
        "router_group_b": 0.01 * jax.random.normal(ks[10], (DEPTH, N_GROUPS), F32),
        "router_expert_w": nrm(ks[11], (DEPTH, D_MODEL, N_EXPERTS), D_MODEL),
        "router_expert_b": 0.01 * jax.random.normal(ks[12], (DEPTH, N_EXPERTS), F32),
        "expert_w_gu": nrm(ks[13], (DEPTH, N_EXPERTS, D_MODEL, 2 * EXPERT_FF), D_MODEL),
        "expert_w_down": nrm(ks[14], (DEPTH, N_EXPERTS, EXPERT_FF, D_MODEL), EXPERT_FF) * out_scale,
        "norm_final": 1.0 + 0.02 * jax.random.normal(ks[15], (D_MODEL,), F32),
    }

def first_block(x, fox_w_in, fox_b_f, fox_w_out, ret_w_in, ret_gn_gain, ret_w_out,
              norm_mix, norm_ffn, router_group_w, router_group_b, router_expert_w,
              router_expert_b, expert_w_gu, expert_w_down, norm_final):
    h = x
    for i in range(DEPTH):
        hn = rms_norm(h, norm_mix[i])
        j = i // N_MIXERS
        if i % N_MIXERS == 0:
            h = h + forgetting_attention(hn, fox_w_in[j], fox_b_f[j], fox_w_out[j])
        else:
            h = h + retention(hn, ret_w_in[j], ret_gn_gain[j], ret_w_out[j])
        hn = rms_norm(h, norm_ffn[i])
        h = h + hier_moe(hn, router_group_w[i], router_group_b[i], router_expert_w[i],
                         router_expert_b[i], expert_w_gu[i], expert_w_down[i])
    return rms_norm(h, norm_final)


GRID_W = 64
CTX_LEN = 256
ROPE_THETA = 10000.0
NORM_EPS = 1e-6
HEAD_DIM = 64

A_HEADS = 8
A_KV_HEADS = 2
A_WINDOW = 128
A_BLOCK = 128
B_HEADS = 8
B_Q_LORA = 384
B_KV_LORA = 256
B_NOPE = 64
B_ROPE = 32
B_V = 64
B_BLOCK = 128
C_HEADS = 16
C_KH = 8
C_KW = 16

A_WIDTH = A_HEADS * HEAD_DIM
A_KV_WIDTH = A_KV_HEADS * HEAD_DIM
B_WIDTH = B_HEADS * B_V
AB_MIX = A_WIDTH + B_WIDTH
AB_SPLITS = (
    A_WIDTH,
    A_WIDTH + A_KV_WIDTH,
    A_WIDTH + 2 * A_KV_WIDTH,
    2 * A_WIDTH + 2 * A_KV_WIDTH,
    2 * A_WIDTH + 2 * A_KV_WIDTH + B_Q_LORA,
    2 * A_WIDTH + 2 * A_KV_WIDTH + B_Q_LORA + B_KV_LORA,
    2 * A_WIDTH + 2 * A_KV_WIDTH + B_Q_LORA + B_KV_LORA + B_ROPE,
)
AB_IN = 2 * A_WIDTH + 2 * A_KV_WIDTH + B_Q_LORA + B_KV_LORA + B_ROPE + B_WIDTH
C_WIDTH = C_HEADS * HEAD_DIM
C_IN = 4 * C_WIDTH
N_EVEN = (DEPTH + 1) // 2
N_ODD = DEPTH // 2


def rms_norm_2(x, g):
    xf = x.astype(jnp.float32)
    y = xf * lax.rsqrt(jnp.mean(xf * xf, axis=-1, keepdims=True) + NORM_EPS)
    return (y * g.astype(jnp.float32)).astype(x.dtype)

def axial_rope_angles(n_tokens, rot_dim):
    t = jnp.arange(n_tokens, dtype=jnp.int32)
    row = (t // GRID_W).astype(jnp.float32)
    col = (t % GRID_W).astype(jnp.float32)
    pairs_per_axis = rot_dim // 4
    inv = ROPE_THETA ** (-jnp.arange(pairs_per_axis, dtype=jnp.float32) / pairs_per_axis)
    ang = jnp.concatenate([row[:, None] * inv, col[:, None] * inv], axis=-1)
    return jnp.cos(ang), jnp.sin(ang)

def apply_rope(x, cos, sin):
    d = x.shape[-1]
    xr = x.reshape(x.shape[:-1] + (d // 2, 2)).astype(jnp.float32)
    x1, x2 = xr[..., 0], xr[..., 1]
    out = jnp.stack([x1 * cos - x2 * sin, x1 * sin + x2 * cos], axis=-1)
    return out.reshape(x.shape).astype(x.dtype)

def gqa_sink_dense(q, k, v, sink):
    bn, n, _, d = q.shape
    grp = A_HEADS // A_KV_HEADS
    qg = q.reshape(bn, n, A_KV_HEADS, grp, d)
    s = jnp.einsum('bqhgd,bkhd->bhgqk', qg, k).astype(jnp.float32) * (d ** -0.5)
    s_sink = jnp.broadcast_to(sink.astype(jnp.float32).reshape(A_KV_HEADS, grp)[None, :, :, None, None], s.shape[:-1] + (1,))
    p = jax.nn.softmax(jnp.concatenate([s, s_sink], axis=-1), axis=-1)[..., :-1].astype(v.dtype)
    return jnp.einsum('bhgqk,bkhd->bqhgd', p, v).reshape(bn, n, A_HEADS * d)

def window_gqa_latent(q, k, v, kc, vc, sink):
    bn, s_len, _, d = q.shape
    nb = s_len // A_BLOCK
    grp = A_HEADS // A_KV_HEADS
    scale = d ** -0.5
    pad = [(0, 0), (A_BLOCK, A_BLOCK), (0, 0), (0, 0)]

    def band(t):
        tb = jnp.pad(t, pad).reshape(bn, nb + 2, A_BLOCK, A_KV_HEADS, d)
        w = jnp.concatenate([tb[:, :-2], tb[:, 1:-1], tb[:, 2:]], axis=2)
        return jnp.moveaxis(w, 1, 0)

    kw, vw = band(k), band(v)
    qb = jnp.moveaxis(q.reshape(bn, nb, A_BLOCK, A_KV_HEADS, grp, d), 1, 0)
    qi = jnp.arange(A_BLOCK)[:, None]
    kj = jnp.arange(3 * A_BLOCK)[None, :] - A_BLOCK
    band_ok = jnp.abs(kj - qi) <= A_WINDOW
    sink_g = sink.astype(jnp.float32).reshape(A_KV_HEADS, grp)[None, :, :, None, None]

    def block(args):
        n, qn, kn, vn = args
        kpos = n * A_BLOCK + kj
        mask = band_ok & (kpos >= 0) & (kpos < s_len)
        s_loc = jnp.einsum('bqhgd,bkhd->bhgqk', qn, kn).astype(jnp.float32) * scale
        s_loc = jnp.where(mask, s_loc, -jnp.inf)
        s_ctx = jnp.einsum('bqhgd,blhd->bhgql', qn, kc).astype(jnp.float32) * scale
        s_sink = jnp.broadcast_to(sink_g, s_loc.shape[:-1] + (1,))
        p = jax.nn.softmax(jnp.concatenate([s_loc, s_ctx, s_sink], axis=-1), axis=-1)
        p_loc = p[..., :3 * A_BLOCK].astype(vn.dtype)
        p_ctx = p[..., 3 * A_BLOCK:-1].astype(vc.dtype)
        return (jnp.einsum('bhgqk,bkhd->bqhgd', p_loc, vn)
                + jnp.einsum('bhgql,blhd->bqhgd', p_ctx, vc))

    o = lax.map(block, (jnp.arange(nb), qb, kw, vw))
    return jnp.moveaxis(o, 0, 1).reshape(bn, s_len, A_HEADS * d)

def mla_dense(qn, qr, kn, kr, v):
    scale = (B_NOPE + B_ROPE) ** -0.5
    s = (jnp.einsum('bqhd,bkhd->bhqk', qn, kn) + jnp.einsum('bqhr,bkr->bhqk', qr, kr)).astype(jnp.float32) * scale
    p = jax.nn.softmax(s, axis=-1).astype(v.dtype)
    return jnp.einsum('bhqk,bkhd->bqhd', p, v)

def mla_latent(qn, qr, kn, kr, v, kn_c, kr_c, v_c):
    bn, s_len = qn.shape[0], qn.shape[1]
    nb = s_len // B_BLOCK
    k_n = jnp.concatenate([kn_c, kn], axis=1)
    k_r = jnp.concatenate([kr_c, kr], axis=1)
    v_all = jnp.concatenate([v_c, v], axis=1)
    qn_b = jnp.moveaxis(qn.reshape(bn, nb, B_BLOCK, B_HEADS, B_NOPE), 1, 0)
    qr_b = jnp.moveaxis(qr.reshape(bn, nb, B_BLOCK, B_HEADS, B_ROPE), 1, 0)
    o = lax.map(lambda a: mla_dense(a[0], a[1], k_n, k_r, v_all), (qn_b, qr_b))
    return jnp.moveaxis(o, 0, 1).reshape(bn, s_len, B_HEADS * B_V)

def ab_project(u, in_w, qn_g, w_uq, kvn_g, w_ukv):
    bn, n, _ = u.shape
    p = u @ in_w
    qa, ka, va, za, cq, ckv, kr, zb = jnp.split(p, AB_SPLITS, axis=-1)
    qa = qa.reshape(bn, n, A_HEADS, HEAD_DIM)
    ka = ka.reshape(bn, n, A_KV_HEADS, HEAD_DIM)
    va = va.reshape(bn, n, A_KV_HEADS, HEAD_DIM)
    qb = (rms_norm_2(cq, qn_g) @ w_uq).reshape(bn, n, B_HEADS, B_NOPE + B_ROPE)
    kvb = (rms_norm_2(ckv, kvn_g) @ w_ukv).reshape(bn, n, B_HEADS, B_NOPE + B_V)
    return (qa, ka, va, za, qb[..., :B_NOPE], qb[..., B_NOPE:],
            kvb[..., :B_NOPE], kr, kvb[..., B_NOPE:], zb)

def ab_mixer(u, uc, in_w, out_w, sink, qn_g, w_uq, kvn_g, w_ukv, rope_a, rope_b, need_ctx):
    qa, ka, va, za, qbn, qbr, kbn, kbr, vb, zb = ab_project(u, in_w, qn_g, w_uq, kvn_g, w_ukv)
    qa_c, ka_c, va_c, za_c, qbn_c, qbr_c, kbn_c, kbr_c, vb_c, zb_c = ab_project(uc, in_w, qn_g, w_uq, kvn_g, w_ukv)
    cos_a, sin_a = rope_a
    cos_b, sin_b = rope_b
    qa = apply_rope(qa, cos_a[:, None, :], sin_a[:, None, :])
    ka = apply_rope(ka, cos_a[:, None, :], sin_a[:, None, :])
    qbr = apply_rope(qbr, cos_b[:, None, :], sin_b[:, None, :])
    kbr = apply_rope(kbr, cos_b, sin_b)
    oa = window_gqa_latent(qa, ka, va, ka_c, va_c, sink)
    ob = mla_latent(qbn, qbr, kbn, kbr, vb, kbn_c, kbr_c, vb_c)
    y = jnp.concatenate([oa * jax.nn.silu(za), ob * jax.nn.silu(zb)], axis=-1) @ out_w
    if not need_ctx:
        return y, None
    bn, n = uc.shape[0], uc.shape[1]
    oa_c = gqa_sink_dense(qa_c, ka_c, va_c, sink)
    ob_c = mla_dense(qbn_c, qbr_c, kbn_c, kbr_c, vb_c).reshape(bn, n, B_WIDTH)
    yc = jnp.concatenate([oa_c * jax.nn.silu(za_c), ob_c * jax.nn.silu(zb_c)], axis=-1) @ out_w
    return y, yc

def mha_dense(q, k, v):
    bn, n, h, d = q.shape
    s = jnp.einsum('bqhd,bkhd->bhqk', q, k).astype(jnp.float32) * (d ** -0.5)
    p = jax.nn.softmax(s, axis=-1).astype(v.dtype)
    return jnp.einsum('bhqk,bkhd->bqhd', p, v).reshape(bn, n, h * d)

def neighbourhood_latent(q, k, v, kc, vc, rpb):
    bn, s_len, h, d = q.shape
    rows = s_len // GRID_W
    kh = min(C_KH, rows)
    scale = d ** -0.5
    qg = jnp.moveaxis(q.reshape(bn, rows, GRID_W, h, d), 1, 0)
    kg = k.reshape(bn, rows, GRID_W, h, d)
    vg = v.reshape(bn, rows, GRID_W, h, d)
    col = jnp.arange(GRID_W)
    cs = jnp.clip(col - C_KW // 2, 0, GRID_W - C_KW)
    col_ok = (col[None, :] >= cs[:, None]) & (col[None, :] < cs[:, None] + C_KW)
    col_idx = jnp.clip(col[None, :] - col[:, None] + (C_KW - 1), 0, 2 * C_KW - 2)
    rpb_col = rpb[:, :, col_idx]
    mask = jnp.broadcast_to(col_ok[:, None, :], (GRID_W, kh, GRID_W)).reshape(GRID_W, kh * GRID_W)

    def row_block(args):
        r, qr = args
        rs = jnp.clip(r - kh // 2, 0, rows - kh)
        kr = lax.dynamic_slice_in_dim(kg, rs, kh, axis=1).reshape(bn, kh * GRID_W, h, d)
        vr = lax.dynamic_slice_in_dim(vg, rs, kh, axis=1).reshape(bn, kh * GRID_W, h, d)
        row_idx = rs + jnp.arange(kh) - r + (C_KH - 1)
        bias = jnp.take(rpb_col, row_idx, axis=1)
        bias = jnp.transpose(bias, (0, 2, 1, 3)).reshape(h, GRID_W, kh * GRID_W)
        s_loc = jnp.einsum('bqhd,bkhd->bhqk', qr, kr).astype(jnp.float32) * scale + bias.astype(jnp.float32)
        s_loc = jnp.where(mask, s_loc, -jnp.inf)
        s_ctx = jnp.einsum('bqhd,blhd->bhql', qr, kc).astype(jnp.float32) * scale
        p = jax.nn.softmax(jnp.concatenate([s_loc, s_ctx], axis=-1), axis=-1)
        p_loc = p[..., :kh * GRID_W].astype(vr.dtype)
        p_ctx = p[..., kh * GRID_W:].astype(vc.dtype)
        return jnp.einsum('bhqk,bkhd->bqhd', p_loc, vr) + jnp.einsum('bhql,blhd->bqhd', p_ctx, vc)

    o = lax.map(row_block, (jnp.arange(rows), qg))
    return jnp.moveaxis(o, 0, 1).reshape(bn, s_len, h * d)

def c_mixer(u, uc, in_w, out_w, rpb, need_ctx):
    def proj(t):
        bn, n, _ = t.shape
        q, k, v, z = jnp.split(t @ in_w, 4, axis=-1)
        shp = (bn, n, C_HEADS, HEAD_DIM)
        return q.reshape(shp), k.reshape(shp), v.reshape(shp), z
    q, k, v, z = proj(u)
    q_c, k_c, v_c, z_c = proj(uc)
    o = neighbourhood_latent(q, k, v, k_c, v_c, rpb)
    y = (o * jax.nn.silu(z)) @ out_w
    if not need_ctx:
        return y, None
    yc = (mha_dense(q_c, k_c, v_c) * jax.nn.silu(z_c)) @ out_w
    return y, yc

def second_inputs(seed: int = 0) -> dict:
    key = jax.random.key(seed)
    ks = jax.random.split(key, 20)
    f32 = jnp.float32

    def w(k, shape, fan_in, gain=1.0):
        return jax.random.normal(k, shape, f32) * (gain * fan_in ** -0.5)

    def gain(k, shape):
        return 1.0 + 0.05 * jax.random.normal(k, shape, f32)

    return {
        "x": jax.random.normal(ks[0], (BATCH, SEQ, D_MODEL), f32),
        "c": jax.random.normal(ks[1], (BATCH, D_MODEL), f32),
        "ctx": jax.random.normal(ks[2], (BATCH, CTX_LEN, D_MODEL), f32),
        "c_ctx": jax.random.normal(ks[3], (D_MODEL,), f32),
        "ada_w": w(ks[4], (DEPTH, D_MODEL, 3 * D_MODEL), D_MODEL, 0.5),
        "ada_b": 0.02 * jax.random.normal(ks[5], (DEPTH, 3 * D_MODEL), f32),
        "norm_g": gain(ks[6], (DEPTH, D_MODEL)),
        "ab_in_w": w(ks[7], (N_EVEN, D_MODEL, AB_IN), D_MODEL),
        "ab_out_w": w(ks[8], (N_EVEN, AB_MIX, D_MODEL), AB_MIX),
        "a_sink": jax.random.normal(ks[9], (N_EVEN, A_HEADS), f32),
        "b_q_norm_g": gain(ks[10], (N_EVEN, B_Q_LORA)),
        "b_w_uq": w(ks[11], (N_EVEN, B_Q_LORA, B_HEADS * (B_NOPE + B_ROPE)), B_Q_LORA),
        "b_kv_norm_g": gain(ks[12], (N_EVEN, B_KV_LORA)),
        "b_w_ukv": w(ks[13], (N_EVEN, B_KV_LORA, B_HEADS * (B_NOPE + B_V)), B_KV_LORA),
        "c_in_w": w(ks[14], (N_ODD, D_MODEL, C_IN), D_MODEL),
        "c_out_w": w(ks[15], (N_ODD, C_WIDTH, D_MODEL), C_WIDTH),
        "c_rpb": 0.5 * jax.random.normal(ks[16], (N_ODD, C_HEADS, 2 * C_KH - 1, 2 * C_KW - 1), f32),
        "final_g": gain(ks[17], (D_MODEL,)),
    }

def second_block(x, c, ctx, c_ctx, ada_w, ada_b, norm_g, ab_in_w, ab_out_w, a_sink,
              b_q_norm_g, b_w_uq, b_kv_norm_g, b_w_ukv, c_in_w, c_out_w, c_rpb, final_g):
    n_lat = x.shape[1]
    rope_a = axial_rope_angles(n_lat, HEAD_DIM)
    rope_b = axial_rope_angles(n_lat, B_ROPE)
    sc = jax.nn.silu(c)
    sc_ctx = jax.nn.silu(c_ctx)
    h, hc = x, ctx
    for layer in range(DEPTH):
        last = layer == DEPTH - 1
        mod = sc @ ada_w[layer] + ada_b[layer]
        shift, scale, gate = jnp.split(mod[:, None, :], 3, axis=-1)
        mod_c = sc_ctx @ ada_w[layer] + ada_b[layer]
        shift_c, scale_c, gate_c = jnp.split(mod_c, 3, axis=-1)
        u = rms_norm_2(h, norm_g[layer]) * (1 + scale) + shift
        uc = rms_norm_2(hc, norm_g[layer]) * (1 + scale_c) + shift_c
        if layer % 2 == 0:
            i = layer // 2
            y, yc = ab_mixer(u, uc, ab_in_w[i], ab_out_w[i], a_sink[i], b_q_norm_g[i], b_w_uq[i],
                             b_kv_norm_g[i], b_w_ukv[i], rope_a, rope_b, not last)
        else:
            i = layer // 2
            y, yc = c_mixer(u, uc, c_in_w[i], c_out_w[i], c_rpb[i], not last)
        h = h + gate * y
        if not last:
            hc = hc + gate_c * yc
    return rms_norm_2(h, final_g)


def setup_inputs(seed=0):
    out = dict(first_inputs(seed))
    for name, value in second_inputs(seed + 1).items():
        if name != "x":
            out[name + "_2"] = value
    return out


def reference(
    x, fox_w_in, fox_b_f, fox_w_out, ret_w_in, ret_gn_gain, ret_w_out, norm_mix, norm_ffn,
    router_group_w, router_group_b, router_expert_w, router_expert_b, expert_w_gu,
    expert_w_down, norm_final, c_2, ctx_2, c_ctx_2, ada_w_2, ada_b_2, norm_g_2, ab_in_w_2,
    ab_out_w_2, a_sink_2, b_q_norm_g_2, b_w_uq_2, b_kv_norm_g_2, b_w_ukv_2, c_in_w_2, c_out_w_2,
    c_rpb_2, final_g_2,
):
    x = first_block(
        x, fox_w_in, fox_b_f, fox_w_out, ret_w_in, ret_gn_gain, ret_w_out, norm_mix, norm_ffn,
        router_group_w, router_group_b, router_expert_w, router_expert_b, expert_w_gu,
        expert_w_down, norm_final,
    )
    return second_block(
        x, c_2, ctx_2, c_ctx_2, ada_w_2, ada_b_2, norm_g_2, ab_in_w_2, ab_out_w_2, a_sink_2,
        b_q_norm_g_2, b_w_uq_2, b_kv_norm_g_2, b_w_ukv_2, c_in_w_2, c_out_w_2, c_rpb_2,
        final_g_2,
    )


_drawn_inputs = setup_inputs


def setup_inputs(seed=0):
    import zlib

    import numpy as np

    out = dict(_drawn_inputs(seed))
    spreads = {}
    factors = {'ret_gn_gain': 5.112,
     'norm_mix': 3.351,
     'router_group_b': 4.847,
     'router_expert_b': 5.041,
     'norm_final': 2.852,
     'ctx_2': 2.843,
     'ada_b_2': 7.329,
     'norm_g_2': 8.0,
     'a_sink_2': 8.0,
     'b_q_norm_g_2': 8.0,
     'b_w_uq_2': 4.763,
     'b_kv_norm_g_2': 8.0,
     'c_rpb_2': 7.887}
    for name, (base, spread) in spreads.items():
        noise = np.random.default_rng([zlib.crc32(name.encode()), seed]).standard_normal(out[name].shape)
        drawn = base * np.exp(spread * noise) if base else spread * noise
        out[name] = __import__('jax').numpy.asarray(drawn.astype(out[name].dtype))
    for name, factor in factors.items():
        out[name] = (out[name] * factor).astype(out[name].dtype)
    return out
```

```python
from contextlib import ExitStack

import numpy as np

import concourse.bass as bass
from concourse import mybir

F32 = mybir.dt.float32
U32 = mybir.dt.uint32
ALU = mybir.AluOpType
ACT = mybir.ActivationFunctionType
AXX = mybir.AxisListType.X

P = 128
D = 1024
KC = D // P
SEQ, CTX = 512, 256
NT, NCT = SEQ // P, CTX // P
NTA = NT + NCT
BANK = 512
EPS = 1e-6
NEG = -1e30
FOX_H, DH = 16, 64
RET_H, RET_DK, RET_DV = 4, 256, 512
N_GROUPS, PER_GROUP = 4, 8
NE = N_GROUPS * PER_GROUP
NR = N_GROUPS + NE
FF = 512
EXTRA = 7
SLOTS = (NE + EXTRA) * P
B_NOPE, B_ROPE, B_V = 64, 32, 64
B_QK = B_NOPE + B_ROPE
Q_LORA, KV_LORA = 384, 256
GRID, KH, KW = 64, 8, 16
RING, SLOT = 3, 4096

C_ID, C_CAUSAL, C_ANTI, C_ONES, C_BEFORE = 0, 128, 256, 384, 512
C_IOTA, C_BASE, C_WIN = 640, 672, 704
C_COSA, C_SINA, C_COSB, C_SINB = 768, 896, 1024, 1088
C_ALL = 1152

V_MIX, V_FFN, V_NG, V_C, V_CC, V_GN, V_BQ, V_BKV = 0, 16, 32, 48, 56, 64, 80, 83
V_ALL = 85


def constants():
    f = np.float32
    c = np.zeros((P, C_ALL), f)
    i, j = np.arange(P)[:, None], np.arange(P)[None, :]
    c[:, C_ID:C_ID + P] = i == j
    c[:, C_CAUSAL:C_CAUSAL + P] = np.where(j <= i, 0, NEG)
    c[:, C_ANTI:C_ANTI + P] = np.where(j >= i, 0, NEG)
    c[:, C_ONES:C_ONES + P] = 1
    c[:, C_BEFORE:C_BEFORE + P] = i < j
    c[:, C_IOTA:C_IOTA + NE] = np.arange(NE)
    c[:, C_BASE:C_BASE + NE] = np.arange(NE) * P
    q, k = (np.arange(P) % GRID)[:, None], np.arange(GRID)[None, :]
    lo = np.clip(q - KW // 2, 0, GRID - KW)
    c[:, C_WIN:C_WIN + GRID] = np.where((k >= lo) & (k < lo + KW), 0, NEG)
    t = np.arange(SEQ)
    for at_cos, at_sin, rot in ((C_COSA, C_SINA, DH), (C_COSB, C_SINB, B_ROPE)):
        n = rot // 4
        inv = f(10000.0) ** (-np.arange(n, dtype=f) / f(n))
        ang = np.concatenate([(t // GRID).astype(f)[:, None] * inv, (t % GRID).astype(f)[:, None] * inv], 1)
        for at, fn in ((at_cos, np.cos), (at_sin, np.sin)):
            c[:, at:at + NT * 2 * n] = fn(ang).astype(f).reshape(NT, P, 2 * n).transpose(1, 0, 2).reshape(P, -1)
    half = RET_DK // 2
    inv = f(1.0) / (f(10000.0) ** np.linspace(0.0, 1.0, half, dtype=f))
    ang = np.arange(SEQ, dtype=f)[None, :] * inv[:, None].astype(f)
    rot = np.stack([np.cos(ang), np.sin(ang)], 1).astype(f)
    rel = (np.arange(SEQ)[None, :] - np.arange(P)[:, None]).astype(np.float64)
    decay = [np.where(rel >= 0, (1 - 2.0 ** (-5 - h)) ** np.maximum(rel, 0), 0) * RET_DK ** -0.5 for h in range(RET_H)]
    return c, rot, np.stack(decay, 1).astype(f)


def bands(rpb):
    h, rows, n = rpb.shape
    wide = np.zeros((h, rows, 2 * GRID - 1), rpb.dtype)
    at = GRID - 1 - n // 2
    wide[:, :, at:at + n] = rpb
    return np.stack([wide[:, :, GRID - 1 - q:2 * GRID - 1 - q] for q in range(GRID)], 1)


def build(nc, io, upto=99, dbg=None):
    ctx = ExitStack()
    with ctx:
        def sb(name, shape, dt=F32):
            return ctx.enter_context(nc.sbuf_tensor(name, shape, dt))

        sems = {}

        def sem(name):
            if name not in sems:
                sems[name] = ctx.enter_context(nc.semaphore(name))
            return sems[name]

        def dram(name, shape):
            return nc.dram_tensor(name, shape, F32, kind="Internal").ap()

        H = sb("H", [P, NT, D])
        HC = sb("HC", [P, NCT, D])
        XT = sb("XT", [P, KC, NTA * P])
        ring = sb("ring", [P, RING, SLOT])
        cst = sb("cst", [P, C_ALL])
        cols = sb("cols", [P, P])
        modc = sb("modc", [P, 2, 24, 2])
        amod = sb("amod", [P, 2, KC, 2])
        st = sb("st", [P, 4, 8])
        sm = sb("sm", [P, 4, 36])
        sinkb = sb("sinkb", [P, 8])
        rt = sb("rt", [P, 12, 128])
        rbias = sb("rbias", [P, NR])
        wr = sb("wr", [P, KC, NR])
        didx = sb("didx", [P, 2, NT], U32)
        gates = sb("gates", [P, 2, NT])
        top8 = sb("top8", [P, 4, NT, 8])
        top8i = sb("top8i", [P, 2, NT, 8], U32)
        ovn = sb("ovn", [1, 16], U32)
        arena_f = (nc.sbuf_usable_end - nc.sbuf_base) // 4 - 64
        arena_f = 26624
        arena = sb("arena", [P, arena_f])
        psum = ctx.enter_context(nc.psum_tensor("psum", [P, 8 * BANK], F32))

        xg_dram = dram("xg_dram", [SLOTS, D])
        y_dram = dram("y_dram", [SLOTS, D])

        ident = cst[:, C_ID:C_ID + P]
        ones = cst[:, C_ONES:C_ONES + P]

        def bank(i, n=BANK, p=P):
            return psum[0:p, i * BANK:i * BANK + n]

        def region(at, *shape):
            n = int(np.prod(shape))
            assert at + n <= arena_f, (at, shape)
            v = arena[:, at:at + n]
            names = "abcd"[:len(shape)]
            if len(shape) == 1:
                return v
            return v.rearrange(f"p ({' '.join(names)}) -> p {' '.join(names)}",
                               **{m: s for m, s in zip(names, shape)})

        class Count:

            def __init__(self, name):
                self.sem, self.n = sem(name), 0

            def on(self, ins):
                self.n += 1
                ins.then_inc(self.sem, 1)
                return self.n

            def then(self, eng, ins):
                self.on(ins)
                eng.wait_ge(self.sem, self.n)

        dve_step = Count("dve_step")
        act_step = Count("act_step")
        pool_step = Count("pool_step")

        w_ready = [sem(f"w_ready{i}") for i in range(RING)]

        class Weights:
            units, value, per, freed = [], [], [0] * RING, {}

            @classmethod
            def add(cls, *pieces):
                u = len(cls.units)
                cls.units.append(pieces)
                cls.per[u % RING] += 16 * len(pieces)
                cls.value.append(cls.per[u % RING])
                return u

            @classmethod
            def view(cls, u, at, k, n):
                return ring[:, u % RING, at:at + k * n].rearrange("p (k n) -> p k n", k=k)

            @classmethod
            def wait(cls, eng, u):
                eng.wait_ge(w_ready[u % RING], cls.value[u])

            @classmethod
            def load(cls, sp, u):
                if u >= RING:
                    sp.wait_ge(*cls.freed[u - RING])
                for at, k, n, src in cls.units[u]:
                    sp.dma_start(cls.view(u, at, k, n), src.rearrange("(k p) n -> p k n", p=P))\
                        .then_inc(w_ready[u % RING], 16)

        stages = []
        stage_done = sem("stage_done")

        class Stage:
            kind = None

            def __init__(self, tag):
                self.tag, self.earlier = tag, [x for x in stages if self.kind and x.kind == self.kind]
                stages.append(self)

            def s(self, name):
                return sem(f"{self.kind or self.tag}_{name}")

            def at(self, name):
                return sum(x.totals().get(name, 0) for x in self.earlier)

            def pe(self, pe): pass
            def act(self, act): pass
            def dve(self, dve): pass
            def pool(self, pool): pass
            def sp(self, sp): pass

        class Start(Stage):
            ROWS = region(0, P)
            ZERO = region(1024, D)

            def act(self, act):
                act.dma_start(cst[:, :], io["consts"]).then_inc(self.s("const"), 16)
                act.dma_start(H[:, :, :], io["x"][0].rearrange("(t p) d -> p t d", p=P)).then_inc(self.s("rows"), 16)
                act.dma_start(HC[:, :, :], io["ctx_2"][0].rearrange("(t p) d -> p t d", p=P)).then_inc(self.s("rows"), 16)

                def vec(at, ap):
                    n = ap.shape[0]
                    act.dma_start(self.ROWS[at:at + n, :], ap).then_inc(self.s("vec"), 16)

                act.wait_ge(self.s("clear"), 1)
                vec(V_MIX, io["norm_mix"].rearrange("l (c p) -> (l c) p", p=P))
                vec(V_FFN, io["norm_ffn"].rearrange("l (c p) -> (l c) p", p=P))
                vec(V_NG, io["norm_g_2"].rearrange("l (c p) -> (l c) p", p=P))
                vec(V_C, io["c_2"].rearrange("l (c p) -> (l c) p", p=P))
                vec(V_CC, io["c_ctx_2"].rearrange("(c p) -> c p", p=P))
                vec(V_GN, io["ret_gn_gain"].rearrange("l (c p) -> (l c) p", p=P))
                vec(V_BQ, io["b_q_norm_g_2"].rearrange("l (c p) -> (l c) p", p=P))
                vec(V_BKV, io["b_kv_norm_g_2"].rearrange("l (c p) -> (l c) p", p=P))
                act.dma_start(sinkb[:, :], io["a_sink_2"][0].partition_broadcast(P)).then_inc(self.s("vec"), 16)
                act.wait_ge(self.s("rows"), 32)
                act.wait_ge(self.s("vec"), 9 * 16)

            def dve(self, dve):
                dve.memset(self.ROWS[:, :], 0.0).then_inc(self.s("clear"), 1)
                dve.memset(self.ZERO[:, :], 0.0).then_inc(self.s("zero"), 1)
                dve.memset(top8[:, 0, :, :], NEG)
                dve.wait_ge(self.s("turned"), 1)
                dve.tensor_copy(cols[:, :], bank(0, P))
                dve.wait_ge(self.s("vec"), 9 * 16)
                dve.tensor_scalar(rt[:, 11, 0:8], sinkb[:, :], -1.0, None, ALU.mult)

            def pe(self, pe):
                pe.wait_ge(self.s("const"), 16)
                pe.wait_ge(self.s("vec"), 9 * 16)
                pe.wait_ge(self.s("clear"), 1)
                pe.transpose(bank(0, P), self.ROWS[:, :], ident).then_inc(self.s("turned"), 1)

            def pool(self, pool):
                pool.wait_ge(self.s("zero"), 1)
                for b in range(NE + EXTRA):
                    pool.dma_start(xg_dram[b * P:(b + 1) * P, :], self.ZERO).then_inc(self.s("cleared"), 16)
                for b in range(EXTRA):
                    pool.dma_start(y_dram[(NE + b) * P:(NE + b + 1) * P, :], self.ZERO).then_inc(self.s("cleared"), 16)
                pool.wait_ge(self.s("cleared"), 16 * (NE + 2 * EXTRA))

        def squares(stage, act, rows, junk):
            for t, r in enumerate(rows):
                i = act.activation(junk, r, ACT.Square, accum_out=st[:, 0, t:t + 1])
                if t < len(rows) - 1:
                    act_step.then(act, i)
            i.then_inc(stage.s("squares"), 1)
            roots(stage, act, len(rows))

        def roots(stage, act, n):
            act.wait_ge(stage.s("inv"), stage.at("inv") + 1)
            act.activation(st[:, 2, 0:n], st[:, 1, 0:n], ACT.Sqrt).then_inc(stage.s("root"), 1)

        def inverse_roots(stage, dve, n, width):
            ms, inv, y0, y = st[:, 0, 0:n], st[:, 1, 0:n], st[:, 2, 0:n], st[:, 3, 0:n]
            dve.wait_ge(stage.s("squares"), stage.at("squares") + 1)
            dve_step.then(dve, dve.tensor_scalar(ms, ms, 1.0 / width, EPS, ALU.mult, ALU.add))
            dve.reciprocal(inv, ms).then_inc(stage.s("inv"), 1)
            dve.wait_ge(stage.s("root"), stage.at("root") + 1)
            dve_step.then(dve, dve.tensor_tensor(y, y0, y0, ALU.mult))
            dve_step.then(dve, dve.tensor_tensor(y, y, ms, ALU.mult))
            dve_step.then(dve, dve.tensor_scalar(y, y, -0.5, 1.5, ALU.mult, ALU.add))
            dve.tensor_tensor(y, y, y0, ALU.mult).then_inc(stage.s("rstd"), 1)
            dve.wait_ge(stage.s("rstd"), stage.at("rstd") + 1)

        class Norm(Stage):
            kind = "norm"

            def totals(self):
                return dict(squares=1, inv=1, root=1, rstd=1, rows_a=(self.tiles + 1) // 2, rows_v=self.tiles // 2,
                            turned=self.chunks, out_a=(self.chunks + 1) // 2)

            def __init__(self, tag, rows, width, tiles, gain, shift, dst, tok0, scaled):
                super().__init__(tag)
                self.rows, self.width, self.tiles = rows, width, tiles
                self.gain, self.shift, self.dst, self.tok0, self.scaled = gain, shift, dst, tok0, scaled
                self.chunks = width // P

            def act(self, act):
                junk = region(arena_f - D, D)[:, 0:self.width]
                squares(self, act, [self.rows[:, t, :] for t in range(self.tiles)], junk)
                act.wait_ge(self.s("rstd"), self.at("rstd") + 1)
                for t in range(0, self.tiles, 2):
                    act.activation(self.scaled[:, t, :], self.rows[:, t, :], ACT.Copy, scale=st[:, 3, t:t + 1])\
                        .then_inc(self.s("rows_a"), 1)
                for c in range(0, self.chunks, 2):
                    act.wait_ge(self.s("turned"), self.at("turned") + c + 1)
                    act.activation(self.out(c), bank(c % 8, self.tiles * P), ACT.Identity,
                                   scale=self.gain(c), bias=self.shift(c) if self.shift else 0.0)\
                        .then_inc(self.s("out_a"), 1)

            def out(self, c):
                return self.dst[:, c, self.tok0:self.tok0 + self.tiles * P]

            def dve(self, dve):
                n = self.tiles
                inverse_roots(self, dve, n, self.width)
                for t in range(1, n, 2):
                    dve.tensor_scalar(self.scaled[:, t, :], self.rows[:, t, :], st[:, 3, t:t + 1], None, ALU.mult)\
                        .then_inc(self.s("rows_v"), 1)
                for c in range(1, self.chunks, 2):
                    dve.wait_ge(self.s("turned"), self.at("turned") + c + 1)
                    if self.shift:
                        i = dve.tensor_scalar(self.out(c), bank(c % 8, n * P), self.gain(c), self.shift(c), ALU.mult, ALU.add)
                    else:
                        i = dve.tensor_scalar(self.out(c), bank(c % 8, n * P), self.gain(c), None, ALU.mult)

            def pe(self, pe):
                pe.wait_ge(self.s("rows_a"), self.at("rows_a") + (self.tiles + 1) // 2)
                pe.wait_ge(self.s("rows_v"), self.at("rows_v") + self.tiles // 2)
                for c in range(self.chunks):
                    for t in range(self.tiles):
                        i = pe.transpose(bank(c % 8)[:, t * P:(t + 1) * P], self.scaled[:, t, c * P:(c + 1) * P], ident)
                    i.then_inc(self.s("turned"), 1)

        class Products(Stage):
            kind = "products"

            def totals(self):
                return dict(filled=len(self.jobs), taken_v=self.count["v"], taken_a=self.count["a"], small=self.small)

            small = 0

            def __init__(self, tag):
                super().__init__(tag)
                self.jobs, self.count, self.banks, self.holder = [], {"v": 0, "a": 0}, 0, {}

            def job(self, eng, fill, take, units=(), release=(), n_banks=1, after=(), scratch=False):
                self.count[eng] += 1
                if release:
                    Weights.freed[units[0]] = (self.s("filled"), self.at("filled") + len(self.jobs) + 1)
                bs = [(self.banks + i) % 8 for i in range(n_banks)]
                self.banks += n_banks
                j = dict(eng=eng, fill=fill, take=take, units=units, banks=bs,
                         k=self.count[eng], scratch=scratch, index=len(self.jobs) + 1,
                         after=[*after, *(self.holder[b] for b in bs if b in self.holder)])
                for b in bs:
                    self.holder[b] = j
                self.jobs.append(j)
                return j

            def taken(self, eng, j):
                eng.wait_ge(self.s("taken_" + j["eng"]), self.at("taken_" + j["eng"]) + j["k"])

            def pe(self, pe):
                for j in self.jobs:
                    for a in j["after"]:
                        self.taken(pe, a)
                    for u in j["units"]:
                        Weights.wait(pe, u)
                    i = j["fill"](pe, [bank(b) for b in j["banks"]])
                    i.then_inc(self.s("filled"), 1)

            def drains(self, eng, who):
                for j in self.jobs:
                    if j["eng"] == who:
                        eng.wait_ge(self.s("filled"), self.at("filled") + j["index"])
                        if j["scratch"] and j["k"] > 1:
                            eng.wait_ge(self.s("taken_" + who), self.at("taken_" + who) + j["k"] - 1)
                        j["take"](eng, [bank(b) for b in j["banks"]]).then_inc(self.s("taken_" + who), 1)

            def dve(self, dve):
                self.drains(dve, "v")

            def act(self, act):
                self.drains(act, "a")

        def mm_T(u, at, k, n, cols_, x, tok, ntok):
            def fill(pe, ps):
                w = Weights.view(u, at, k, n)
                for c in range(k):
                    i = pe.matmul(ps[0][0:cols_[1] - cols_[0], 0:ntok], w[:, c, cols_[0]:cols_[1]],
                                  x[:, c, tok:tok + ntok], start=(c == 0), stop=(c == k - 1))
                return i
            return fill

        def mm_R(u, at, k, n, c0, width, x, t):
            def fill(pe, ps):
                w = Weights.view(u, at, k, n)
                for c in range(k):
                    i = pe.matmul(ps[0][:, 0:width], x[:, c, t * P:(t + 1) * P], w[:, c, c0:c0 + width],
                                  start=(c == 0), stop=(c == k - 1))
                return i
            return fill

        def turn(srcs):
            def fill(pe, ps):
                for n, s in enumerate(srcs):
                    w = s.shape[-1]
                    i = pe.transpose(ps[0][0:w, n * P:(n + 1) * P], s, ident)
                return i
            return fill

        def copy_out(side, dst, scale=None):
            def take(eng, ps):
                src = ps[0][:, 0:dst.free_size()]
                if len(dst.shape) == 3:
                    src = src.rearrange("p (a b) -> p a b", a=dst.shape[1])
                if side == "a":
                    return eng.activation(dst, src, ACT.Copy, scale=1.0 if scale is None else scale)
                if scale is None:
                    return eng.tensor_copy(dst, src)
                return eng.tensor_scalar(dst, src, scale, None, ALU.mult)
            return take

        def act_out(dst, func):
            def take(eng, ps):
                return eng.activation(dst, ps[0][:, 0:dst.free_size()], func)
            return take

        def rope_rows(dst, src, cos, sin, heads, pairs, tmp):
            def emit(dve, ps):
                s = src(ps)
                c = cos.unsqueeze(1).broadcast_to([P, heads, pairs])
                n = sin.unsqueeze(1).broadcast_to([P, heads, pairs])
                x1, x2 = s[:, :, :, 0], s[:, :, :, 1]
                dve.tensor_tensor(tmp[0], x1, c, ALU.mult)
                dve.tensor_tensor(tmp[1], x2, n, ALU.mult)
                dve.tensor_tensor(tmp[2], x1, n, ALU.mult)
                dve_step.then(dve, dve.tensor_tensor(tmp[3], x2, c, ALU.mult))
                dve.tensor_tensor(dst[:, :, :, 0], tmp[0], tmp[1], ALU.subtract)
                return dve.tensor_tensor(dst[:, :, :, 1], tmp[2], tmp[3], ALU.add)
            return emit

        class OutProj(Stage):
            kind = "outproj"

            def totals(self):
                return dict(diag=len(self.gates()), spread=len(self.gates()), gate=len(self.gates()), filled=2 * self.tiles,
                            added=2 * self.tiles, summed=0 if self.layer is None else 2 * self.tiles)

            def __init__(self, tag, u, k, x, tiles, layer=None):
                super().__init__(tag)
                self.u, self.k, self.x, self.tiles, self.layer = u, k, x, tiles, layer
                self.gate = region(0, 2, D)
                self.tmp = region(2 * D, 2, BANK)
                self.diag = region(3 * D, KC, P)
                Weights.freed[u] = (self.s("filled"), self.at("filled") + 2 * tiles)

            def gates(self):
                return [] if self.layer is None else [0, 1] if self.tiles > NT else [0]

            def jobs(self):
                return [(t, half) for t in range(self.tiles) for half in range(2)]

            def row(self, t):
                return H[:, t, :] if t < NT else HC[:, t - NT, :]

            def pe(self, pe):
                for g in self.gates():
                    for half in range(2):
                        pe.wait_ge(self.s("diag"), self.at("diag") + g + 1)
                        for c in range(4):
                            i = pe.matmul(bank(6 + half)[:, c * P:(c + 1) * P], ones, self.diag[:, half * 4 + c, :],
                                          start=(c == 0), stop=(c == 3), skip_group_check=True)
                    i.then_inc(self.s("spread"), 1)
                    pe.wait_ge(self.s("gate"), self.at("gate") + g + 1)
                Weights.wait(pe, self.u)
                w = Weights.view(self.u, 0, self.k, D)
                for n, (t, half) in enumerate(self.jobs()):
                    if n >= 4:
                        pe.wait_ge(self.s("added"), self.at("added") + n - 3)
                    for c in range(self.k):
                        i = pe.matmul(bank(n % 4), self.x[:, c, t * P:(t + 1) * P],
                                      w[:, c, half * BANK:(half + 1) * BANK], start=(c == 0), stop=(c == self.k - 1))
                    i.then_inc(self.s("filled"), 1)

            def dve(self, dve):
                for g in self.gates():
                    if g:
                        dve.wait_ge(self.s("gate"), self.at("gate") + g)
                    for c in range(KC):
                        i = dve.tensor_scalar(self.diag[:, c, :], ident, modc[:, self.layer, 16 + c, g:g + 1], None, ALU.mult)
                    i.then_inc(self.s("diag"), 1)
                for n, (t, half) in enumerate(self.jobs()):
                    dve.wait_ge(self.s("filled"), self.at("filled") + n + 1)
                    dst = self.row(t)[:, half * BANK:(half + 1) * BANK]
                    if self.layer is None:
                        dve.tensor_tensor(dst, bank(n % 4), dst, ALU.add).then_inc(self.s("added"), 1)
                        continue
                    if n == 0:
                        dve.wait_ge(self.s("gate"), self.at("gate") + len(self.gates()))
                    if n >= 2:
                        dve.wait_ge(self.s("summed"), self.at("summed") + n - 1)
                    g = self.gate[:, int(t >= NT), half * BANK:(half + 1) * BANK]
                    dve.tensor_tensor(self.tmp[:, n % 2, :], bank(n % 4), g, ALU.mult).then_inc(self.s("added"), 1)

            def pool(self, pool):
                if self.layer is None:
                    return
                for n, (t, half) in enumerate(self.jobs()):
                    dst = self.row(t)[:, half * BANK:(half + 1) * BANK]
                    pool.wait_ge(self.s("added"), self.at("added") + n + 1)
                    pool.tensor_tensor(dst, self.tmp[:, n % 2, :], dst, ALU.add).then_inc(self.s("summed"), 1)

            def act(self, act):
                for g in self.gates():
                    act.wait_ge(self.s("spread"), self.at("spread") + g + 1)
                    act.activation(self.gate[:, g, :], psum[:, 6 * BANK:8 * BANK], ACT.Copy).then_inc(self.s("gate"), 1)

        class Attend(Stage):
            kind = "attend"

            def totals(self):
                return dict(scored=self.units, max=self.units, exp=self.units, recip=self.units, norm=self.units,
                            turned=self.items, weighed=self.items, pt_v=(self.items + 1) // 2,
                            pt_a=self.items // 2, out=self.heads // 2, bias0=16 * self.heads * self.table, bias1=16 * self.heads * self.table,
                            banded=self.heads * self.table)

            def __init__(self, tag, heads, nq, window, scores, keys, v, out, gate, add=None, sink=False):
                super().__init__(tag)
                self.heads, self.nq, self.window, self.scores = heads, nq, window, scores
                self.keys, self.v, self.out, self.gate = keys, v, out, gate
                self.add, self.sink = add, sink
                self.units, self.items = heads * nq, heads * len(keys)
                self.P = region(0, 2, 4, 768)
                self.PT = region(6144, 2, 6, BANK)

            def slots(self):
                n, m = self.nq - 1, len(self.keys)
                return [[]] + [list(range(m * i // n, m * (i + 1) // n)) for i in range(n)]

            def item(self, h, k):
                return h * len(self.keys) + k

            def side(self, m):
                return "a" if m % 2 else "v"

            def turned_out(self, eng, h, k):
                m = self.item(h, k)
                s = "pt_" + self.side(m)
                eng.wait_ge(self.s(s), self.at(s) + m // 2 + 1)

            def pe(self, pe):
                for h in range(self.heads + 1):
                    for i in range(self.nq):
                        if h < self.heads:
                            n = h * self.nq + i
                            if n >= 2:
                                pe.wait_ge(self.s("exp"), self.at("exp") + n - 1)
                            for c0, c1, lhsT, rhs in self.scores(h, i):
                                m = pe.matmul(psum[:, (n % 2) * 1024 + c0:(n % 2) * 1024 + c1], lhsT, rhs, start=True, stop=True)
                            m.then_inc(self.s("scored"), 1)
                        if h:
                            for k in self.slots()[i]:
                                self.turn_item(pe, h - 1, k)
                    if h:
                        self.weigh(pe, h - 1, len(self.keys) - 1)

            def turn_item(self, pe, h, k):
                m = self.item(h, k)
                _, qa, qb, at = self.keys[k]
                if k == 0:
                    pe.wait_ge(self.s("norm"), self.at("norm") + (h + 1) * self.nq)
                if m >= 2:
                    self.turned_out(pe, *divmod(m - 2, len(self.keys)))
                for i in range(qa, qb):
                    ins = pe.transpose(bank(4 + m % 2)[:, i * P:(i + 1) * P],
                                       self.P[:, h % 2, i, at[i]:at[i] + P], ident)
                ins.then_inc(self.s("turned"), 1)
                if k:
                    self.weigh(pe, h, k - 1)

            def weigh(self, pe, h, k):
                kt, qa, qb, _ = self.keys[k]
                self.turned_out(pe, h, k)
                if k == 0 and h % 2 == 0 and h >= 4:
                    pe.wait_ge(self.s("out"), self.at("out") + h // 2 - 1)
                b = (h % 2) * DH
                ins = pe.matmul(bank(6 + h // 2 % 2)[b:b + DH, qa * P:qb * P], self.v(h, kt),
                                self.PT[:, h % 2, k, qa * P:qb * P], start=(k == 0), stop=(k == len(self.keys) - 1))
                ins.then_inc(self.s("weighed"), 1)

            def take_items(self, eng, side, h, i):
                for k in self.slots()[i]:
                    m = self.item(h, k)
                    if self.side(m) != side:
                        continue
                    _, qa, qb, _ = self.keys[k]
                    eng.wait_ge(self.s("turned"), self.at("turned") + m + 1)
                    if h >= 2:
                        eng.wait_ge(self.s("weighed"), self.at("weighed") + self.item(h - 1, 0))
                    dst, src = self.PT[:, h % 2, k, qa * P:qb * P], bank(4 + m % 2)[:, qa * P:qb * P]
                    ins = eng.activation(dst, src, ACT.Copy) if side == "a" else eng.tensor_copy(dst, src)
                    ins.then_inc(self.s("pt_" + side), 1)

            def win(self, n, i):
                lo, hi = self.window(i)
                return psum[:, (n % 2) * 1024 + lo:(n % 2) * 1024 + hi]

            def dve(self, dve):
                for h in range(self.heads + 1):
                    for i in range(self.nq):
                        n = h * self.nq + i
                        if h < self.heads:
                            dve.wait_ge(self.s("scored"), self.at("scored") + n + 1)
                            adds = self.add(dve, h, i) if self.add else []
                            for c0, c1, a in adds:
                                x = psum[:, (n % 2) * 1024 + c0:(n % 2) * 1024 + c1]
                                ins = dve.tensor_tensor(x, x, a, ALU.add)
                            if adds:
                                dve_step.then(dve, ins)
                            ins = dve.tensor_reduce(sm[:, 0, n:n + 1], self.win(n, i), AXX, ALU.max, negate=True)
                            if self.sink:
                                dve_step.then(dve, ins)
                                ins = dve.tensor_tensor(sm[:, 0, n:n + 1], sm[:, 0, n:n + 1], self.nsink[:, h:h + 1], ALU.min)
                            ins.then_inc(self.s("max"), 1)
                        if 1 <= n <= self.heads * self.nq:
                            self.recip(dve, n - 1)
                        if h:
                            self.take_items(dve, "v", h - 1, i)
                    if h and h % 2 == 0:
                        dve.wait_ge(self.s("weighed"), self.at("weighed") + h * len(self.keys))
                        p = h // 2 - 1
                        dve.tensor_tensor(self.out(p), bank(6 + p % 2)[:, 0:self.nq * P], self.gate(p), ALU.mult)\
                            .then_inc(self.s("out"), 1)

            def recip(self, dve, n):
                dve.wait_ge(self.s("exp"), self.at("exp") + n + 1)
                rs = sm[:, 1, n:n + 1]
                if self.sink:
                    dve_step.then(dve, dve.tensor_tensor(rs, rs, sm[:, 3, n:n + 1], ALU.add))
                dve.reciprocal(sm[:, 2, n:n + 1], rs).then_inc(self.s("recip"), 1)

            def act(self, act):
                for h in range(self.heads + 1):
                    for i in range(self.nq):
                        n = h * self.nq + i
                        if h < self.heads:
                            act.wait_ge(self.s("max"), self.at("max") + n + 1)
                            if h >= 2:
                                act.wait_ge(self.s("turned"), self.at("turned") + self.item(h - 1, 0))
                            self.before_exp(act, h, i)
                            lo, hi = self.window(i)
                            if self.sink:
                                act.activation(sm[:, 3, n:n + 1], sinkb[:, h:h + 1], ACT.Exp, bias=sm[:, 0, n:n + 1])
                            act.activation(self.P[:, h % 2, i, 0:hi - lo], self.win(n, i), ACT.Exp,
                                           bias=sm[:, 0, n:n + 1], accum_out=sm[:, 1, n:n + 1]).then_inc(self.s("exp"), 1)
                        if h:
                            self.take_items(act, "a", h - 1, i)

            def before_exp(self, act, h, i):
                pass

            def pool(self, pool):
                for h in range(self.heads):
                    self.normalise(pool, h)

            def normalise(self, pool, h):
                for i in range(self.nq):
                    n = h * self.nq + i
                    lo, hi = self.window(i)
                    p = self.P[:, h % 2, i, 0:hi - lo]
                    pool.wait_ge(self.s("recip"), self.at("recip") + n + 1)
                    pool.tensor_scalar(p, p, sm[:, 2, n:n + 1], None, ALU.mult).then_inc(self.s("norm"), 1)

            table = 0
            nsink = rt[:, 11, 0:8]

        class RowNorm(Stage):
            kind = "rownorm"

            def totals(self):
                return dict(squares=1, inv=1, root=1, rstd=1, gain=16, made=NT)

            def __init__(self, tag, gain, out=None):
                super().__init__(tag)
                self.gain, self.out_ = gain, out
                self.g = region(0, D)
                self.y = region(1024, NT, D)

            def act(self, act):
                act.dma_start(self.g, self.gain.partition_broadcast(P)).then_inc(self.s("gain"), 16)
                squares(self, act, [H[:, t, :] for t in range(NT)], region(8192, D))
                if self.out_ is not None:
                    for t in range(NT):
                        act.wait_ge(self.s("made"), self.at("made") + t + 1)
                        act.dma_start(self.out_[0, t * P:(t + 1) * P, :], self.y[:, t, :]).then_inc(self.s("stored"), 16)
                    act.wait_ge(self.s("stored"), self.at("stored") + 16 * NT)

            def dve(self, dve):
                inverse_roots(self, dve, NT, D)
                dve.wait_ge(self.s("gain"), self.at("gain") + 16)
                for t in range(NT):
                    dst = H[:, t, :] if self.out_ is None else self.y[:, t, :]
                    dve.scalar_tensor_tensor(dst, H[:, t, :], st[:, 3, t:t + 1], self.g, ALU.mult, ALU.mult)\
                        .then_inc(self.s("made"), 1)

        def slot_view(i):
            return rt[:, i, :].rearrange("p (t e) -> p t e", t=NT)

        class Route(Stage):

            def __init__(self, tag, layer, rows):
                super().__init__(tag)
                self.l, self.rows = layer, rows

            def act(self, act):
                act.dma_start(wr[:, :, 0:N_GROUPS], io["router_group_w"][self.l].rearrange("(c p) g -> p c g", p=P))\
                    .then_inc(self.s("loaded"), 16)
                act.dma_start(wr[:, :, N_GROUPS:NR], io["router_expert_w"][self.l].rearrange("(c p) g -> p c g", p=P))\
                    .then_inc(self.s("loaded"), 16)
                act.dma_start(rbias[:, 0:N_GROUPS], io["router_group_b"][self.l].partition_broadcast(P)).then_inc(self.s("loaded"), 16)
                act.dma_start(rbias[:, N_GROUPS:NR], io["router_expert_b"][self.l].partition_broadcast(P)).then_inc(self.s("loaded"), 16)
                act.wait_ge(self.s("tops"), 1)
                for t in range(NT):
                    act.activation(top8[:, 3, t, :], top8[:, 0, t, :], ACT.Exp, bias=rt[:, 9, 8 + t:9 + t],
                                   accum_out=rt[:, 9, 16 + t:17 + t])
                act.activation(rt[:, 9, 20:24], rt[:, 9, 12:16], ACT.Exp).then_inc(self.s("exps"), 1)

            def pe(self, pe):
                pe.wait_ge(self.s("loaded"), 64)
                for t in range(NT):
                    for c in range(KC):
                        i = pe.matmul(bank(t, NR), XT[:, c, t * P:(t + 1) * P], wr[:, c, :], start=(c == 0), stop=(c == KC - 1))
                i.then_inc(self.s("logits"), 1)
                pe.wait_ge(self.s("mask"), 1)
                M = slot_view(4)
                for t in range(NT):
                    for u in range(t + 1):
                        lhs = ones if u < t else cst[:, C_BEFORE:C_BEFORE + P]
                        pe.matmul(bank(t, NE), lhs, M[:, u, :], start=(u == 0), stop=(u == t))
                for u in range(NT):
                    i = pe.matmul(bank(4, NE), ones, M[:, u, :], start=(u == 0), stop=(u == NT - 1))
                i.then_inc(self.s("ranked"), 1)

            def dve(self, dve):
                def step(i):
                    dve_step.then(dve, i)
                G, EL, MSK, DEST, TMP, OV = top8[:, 0], slot_view(0), slot_view(1), slot_view(5), slot_view(6), slot_view(7)
                A = [slot_view(2), slot_view(3)]
                gif, nmax, diff, gsum, e2 = (rt[:, 9, a:a + 4] for a in (0, 8, 12, 16, 20))
                eif = rt[:, 9, 24:32].rearrange("p (k t) -> p k t", k=2)
                pen = rt[:, 10, 0:16].rearrange("p (t g) -> p t g", t=NT)
                iota = cst[:, C_IOTA:C_IOTA + NE]
                dve.wait_ge(self.s("loaded"), 64)
                dve.wait_ge(self.s("logits"), 1)
                for t in range(NT):
                    dve.tensor_tensor(G[:, t, 0:N_GROUPS], bank(t)[:, 0:N_GROUPS], rbias[:, 0:N_GROUPS], ALU.add)
                    i = dve.tensor_tensor(EL[:, t, :], bank(t)[:, N_GROUPS:NR], rbias[:, N_GROUPS:NR], ALU.add)
                step(i)
                for t in range(NT):
                    i = dve.max(top8[:, 1, t, :], G[:, t, :])
                step(i)
                for t in range(NT):
                    i = dve.max_index(top8i[:, 0, t, :], top8[:, 1, t, :], G[:, t, :])
                step(i)
                step(dve.tensor_copy(gif, top8i[:, 0, :, 0]))
                for t in range(NT):
                    i = dve.tensor_scalar(pen[:, t, :], iota[:, 0:N_GROUPS], gif[:, t:t + 1], None, ALU.is_equal)
                step(i)
                step(dve.tensor_scalar(rt[:, 10, 0:16], rt[:, 10, 0:16], -NEG, NEG, ALU.mult, ALU.add))
                step(dve.tensor_tensor(rt[:, 1, :].rearrange("p (a e) -> p a e", e=PER_GROUP),
                                       rt[:, 0, :].rearrange("p (a e) -> p a e", e=PER_GROUP),
                                       rt[:, 10, 0:16].unsqueeze(2).broadcast_to([P, 16, PER_GROUP]), ALU.add))
                for t in range(NT):
                    i = dve.max(top8[:, 2, t, :], MSK[:, t, :])
                step(i)
                dve.tensor_scalar(nmax, top8[:, 1, :, 0], -1.0, None, ALU.mult)
                dve.tensor_tensor(diff, top8[:, 2, :, 1], top8[:, 2, :, 0], ALU.subtract).then_inc(self.s("tops"), 1)
                for t in range(NT):
                    i = dve.max_index(top8i[:, 1, t, :], top8[:, 2, t, :], MSK[:, t, :])
                step(i)
                for k in range(2):
                    i = dve.tensor_copy(eif[:, k, :], top8i[:, 1, :, k])
                step(i)
                for k in range(2):
                    for t in range(NT):
                        i = dve.tensor_scalar(A[k][:, t, :], iota, eif[:, k, t:t + 1], None, ALU.is_equal)
                step(i)
                dve.tensor_tensor(rt[:, 4, :], rt[:, 2, :], rt[:, 3, :], ALU.add).then_inc(self.s("mask"), 1)
                dve.wait_ge(self.s("exps"), 1)
                step(dve.scalar_tensor_tensor(gates[:, 0, :], e2, 1.0, gsum, ALU.add, ALU.mult))
                step(dve.reciprocal(gates[:, 0, :], gates[:, 0, :]))
                dve.tensor_tensor(gates[:, 1, :], gates[:, 0, :], e2, ALU.mult)
                dve.wait_ge(self.s("ranked"), 1)
                cnt, nov, incl, ob = (rt[:, 8, 32 * a:32 * a + 32] for a in range(4))
                step(dve.tensor_copy(cnt, bank(4)[:, 0:NE]))
                step(dve.tensor_scalar(nov, cnt, float(P), None, ALU.is_gt))
                step(dve.scalar_tensor_tensor(nov, cnt, 2.0 * P, nov, ALU.is_gt, ALU.add))
                step(dve.scalar_tensor_tensor(nov, cnt, 3.0 * P, nov, ALU.is_gt, ALU.add))
                step(dve.tensor_tensor_scan(incl, ones[:, 0:NE], nov, 0.0, ALU.mult, ALU.add))
                step(dve.tensor_tensor(ob, incl, nov, ALU.subtract))
                dlt = rt[:, 10, 32:64]
                step(dve.tensor_scalar(dlt, ob, float(NE - 1), float(P), ALU.add, ALU.mult))
                step(dve.tensor_tensor(dlt, dlt, cst[:, C_BASE:C_BASE + NE], ALU.subtract))
                for t in range(NT):
                    i = dve.tensor_copy(TMP[:, t, :], bank(t)[:, 0:NE])
                step(i)
                step(dve.tensor_scalar(rt[:, 7, :], rt[:, 6, :], float(P), None, ALU.is_ge))
                step(dve.tensor_tensor(OV, OV, dlt.unsqueeze(1).broadcast_to([P, NT, NE]), ALU.mult))
                step(dve.tensor_tensor(OV, OV, TMP, ALU.add))
                step(dve.tensor_tensor(DEST, OV, cst[:, C_BASE:C_BASE + NE].unsqueeze(1).broadcast_to([P, NT, NE]), ALU.add))
                for k in range(2):
                    step(dve.tensor_tensor(TMP, A[k], DEST, ALU.mult))
                    step(dve.tensor_reduce(rt[:, 10, 64 + 4 * k:68 + 4 * k], TMP, AXX, ALU.add))
                    i = dve.tensor_copy(didx[:, k, :], rt[:, 10, 64 + 4 * k:68 + 4 * k])
                i.then_inc(self.s("dest"), 1)
                big = [region(8192 + 256 * a, EXTRA, NE)[0:1] for a in range(2)]
                jb = cst[0:1, C_IOTA:C_IOTA + EXTRA].unsqueeze(2).broadcast_to([1, EXTRA, NE])
                over_j = lambda x: x[0:1].unsqueeze(1).broadcast_to([1, EXTRA, NE])
                dve.tensor_tensor(big[0], over_j(ob), jb, ALU.is_le)
                step(dve.tensor_tensor(big[1], over_j(incl), jb, ALU.is_gt))
                step(dve.tensor_tensor(big[0], big[0], big[1], ALU.mult))
                step(dve.tensor_tensor(big[0], big[0], over_j(iota), ALU.mult))
                step(dve.tensor_reduce(rt[0:1, 10, 80:80 + EXTRA], big[0], AXX, ALU.add))
                dve.tensor_copy(ovn[0:1, 1:1 + EXTRA], rt[0:1, 10, 80:80 + EXTRA])
                dve.tensor_copy(ovn[0:1, 0:1], incl[0:1, NE - 1:NE]).then_inc(self.s("extra"), 1)

            def pool(self, pool):
                pool.wait_ge(self.s("dest"), 1)
                for t in range(NT):
                    for k in range(2):
                        pool.indirect_dma_start(xg_dram, bass.IndirectOffsetOnAxis(ap=didx[:, k, t:t + 1], axis=0),
                                                self.rows[:, t, :], None).then_inc(self.s("scattered"), 16)
                pool.wait_ge(self.s("scattered"), 16 * 2 * NT)

        def is_at(e, n):
            return isinstance(e, int) and e == n

        class Experts(Stage):

            def __init__(self, tag, layer):
                super().__init__(tag)
                self.l = layer
                self.base, self.per = len(Weights.units), list(Weights.per)
                for v in range(3 * NE):
                    Weights.add((0, 0, 0, None))
                end = self.base + 3 * NE
                Weights.freed[end - 3] = (self.s("upped"), NE)
                Weights.freed[end - 2] = (self.s("downed"), NE - 1)
                Weights.freed[end - 1] = (self.s("downed"), NE)
                self.XG, self.XGT = region(0, D), region(1024, KC, P)
                self.SA, self.HR, self.HT, self.Y = region(2048, FF), region(2560, FF), region(3072, 4, P), region(4096, D)
                self.gu = io["expert_w_gu"][layer].rearrange("e (k p) n -> e p k n", p=P)
                self.dn = io["expert_w_down"][layer].rearrange("e (k p) n -> e p k n", p=P)
                self.xgb = xg_dram.rearrange("(b p) d -> b p d", p=P)
                self.yb = y_dram.rearrange("(b p) d -> b p d", p=P)

            def slot(self, v):
                return (self.base + v) % RING

            def unit_gu(self, e, half, first):
                s = self.slot(half if first else 2 + half)
                return s, self.per[s] + 16 * (1 if first else e + half)

            def unit_dn(self, e, last):
                s = self.slot(3 * NE - 1 if last else 4)
                return s, self.per[s] + 16 * (NE if last else e + 2)

            def loop(self, eng, body):
                body(0)
                body(1)
                with eng.Fori(2, NE - 2) as e:
                    body(e)
                body(NE - 2)
                body(NE - 1)

            def sp(self, sp):
                def load(slot, k, n, src):
                    sp.dma_start(ring[:, slot, :].rearrange("p (k n) -> p k n", k=k), src).then_inc(w_ready[slot], 16)

                def gu(e, half):
                    load(self.unit_gu(e, half, is_at(e, 0))[0], KC, BANK, self.gu[e, :, :, half * FF:(half + 1) * FF])

                def body(e):
                    if is_at(e, 0):
                        for half in range(2):
                            sp.wait_ge(*Weights.freed[self.base - RING + half])
                            gu(e, half)
                        return
                    if is_at(e, 1):
                        sp.wait_ge(*Weights.freed[self.base - 1])
                        gu(e, 0)
                        sp.wait_ge(self.s("gated"), 1)
                        gu(e, 1)
                        sp.wait_ge(self.s("upped"), 1)
                    else:
                        sp.wait_ge(self.s("gated"), e)
                        gu(e, 0)
                        sp.wait_ge(self.s("upped"), e)
                        gu(e, 1)
                        sp.wait_ge(self.s("downed"), e - 1)
                    load(self.unit_dn(e - 1, False)[0], 4, D, self.dn[e - 1])
                    if is_at(e, NE - 1):
                        sp.wait_ge(self.s("gated"), NE)
                        load(self.unit_dn(e, True)[0], 4, D, self.dn[e])
                self.loop(sp, body)
                sp.wait_ge(self.s("open"), 1)
                n = sp.value_load(ovn[0:1, 0:1], min_val=0, max_val=EXTRA)
                for j in range(EXTRA):
                    with sp.If(n > j):
                        if j == 0:
                            sp.wait_ge(self.s("downed"), NE)
                        e = sp.value_load(ovn[0:1, 1 + j:2 + j], min_val=0, max_val=NE - 1)
                        for half in range(2):
                            sp.dma_start(ring[:, half, :].rearrange("p (k n) -> p k n", k=KC),
                                         self.gu[e, :, :, half * FF:(half + 1) * FF]).then_inc(self.s("x_weights"), 16)
                        sp.dma_start(ring[:, 2, :].rearrange("p (k n) -> p k n", k=4), self.dn[e]).then_inc(self.s("x_weights"), 16)
                        sp.wait_ge(self.s("x_down"), j + 1)

            def turn_x(self, pe):
                for c in range(KC):
                    i = pe.transpose(psum[:, 2 * BANK + c * P:2 * BANK + (c + 1) * P], self.XG[:, c * P:(c + 1) * P], ident)
                return i

            def up(self, pe, slot, half):
                w = ring[:, slot, :].rearrange("p (k n) -> p k n", k=KC)
                for c in range(KC):
                    i = pe.matmul(bank(half), self.XGT[:, c, :], w[:, c, :], start=(c == 0), stop=(c == KC - 1))
                return i

            def turn_h(self, pe):
                for c in range(4):
                    i = pe.transpose(bank(4)[:, c * P:(c + 1) * P], self.HR[:, c * P:(c + 1) * P], ident)
                return i

            def down(self, pe, slot):
                w = ring[:, slot, :].rearrange("p (k n) -> p k n", k=4)
                for half in range(2):
                    for c in range(4):
                        i = pe.matmul(bank(5 + half), self.HT[:, c, :], w[:, c, half * BANK:(half + 1) * BANK],
                                      start=(c == 0), stop=(c == 3))
                return i

            def pe(self, pe):
                def down(e, last):
                    s, ready = self.unit_dn(e, last)
                    pe.wait_ge(w_ready[s], ready)
                    pe.wait_ge(self.s("ht"), e + 1)
                    if not is_at(e, 0):
                        pe.wait_ge(self.s("y"), e)
                    self.down(pe, s).then_inc(self.s("downed"), 1)

                def body(e):
                    first, last = is_at(e, 0), is_at(e, NE - 1)
                    if first:
                        pe.wait_ge(self.s("rows"), 16)
                        self.turn_x(pe).then_inc(self.s("turned"), 1)
                    pe.wait_ge(self.s("xt"), e + 1)
                    for half in range(2):
                        s, ready = self.unit_gu(e, half, first)
                        pe.wait_ge(w_ready[s], ready)
                        self.up(pe, s, half).then_inc(self.s(("gated", "upped")[half]), 1)
                    if not last:
                        pe.wait_ge(self.s("rows"), 16 * (e + 2))
                        self.turn_x(pe).then_inc(self.s("turned"), 1)
                    if not first:
                        down(e - 1, False)
                    pe.wait_ge(self.s("h"), e + 1)
                    self.turn_h(pe).then_inc(self.s("h_turned"), 1)
                    if last:
                        down(e, True)
                self.loop(pe, body)
                n = pe.value_load(ovn[0:1, 0:1], min_val=0, max_val=EXTRA)
                for j in range(EXTRA):
                    with pe.If(n > j):
                        pe.wait_ge(self.s("x_rows"), 16 * (j + 1))
                        self.turn_x(pe).then_inc(self.s("x_turned"), 1)
                        pe.wait_ge(self.s("x_xt"), j + 1)
                        pe.wait_ge(self.s("x_weights"), 48 * (j + 1))
                        self.up(pe, 0, 0)
                        self.up(pe, 1, 1).then_inc(self.s("x_upped"), 1)
                        pe.wait_ge(self.s("x_h"), j + 1)
                        self.turn_h(pe).then_inc(self.s("x_h_turned"), 1)
                        pe.wait_ge(self.s("x_ht"), j + 1)
                        self.down(pe, 2).then_inc(self.s("x_down"), 1)

            def gain(self):
                g = cols[:, V_FFN + KC * self.l:V_FFN + KC * (self.l + 1)]
                return g.unsqueeze(2).broadcast_to([P, KC, P])

            def take_x(self, dve):
                return dve.tensor_tensor(self.XGT, psum[:, 2 * BANK:4 * BANK].rearrange("p (c t) -> p c t", c=KC),
                                         self.gain(), ALU.mult)

            def take_ht(self, dve):
                return dve.tensor_copy(self.HT, bank(4).rearrange("p (c t) -> p c t", c=4))

            def dve(self, dve):
                def body(e):
                    first, last = is_at(e, 0), is_at(e, NE - 1)
                    if first:
                        dve.wait_ge(self.s("turned"), 1)
                        self.take_x(dve).then_inc(self.s("xt"), 1)
                    dve.wait_ge(self.s("silu"), e + 1)
                    dve.tensor_tensor(self.HR, self.SA, bank(1), ALU.mult).then_inc(self.s("h"), 1)
                    if not last:
                        dve.wait_ge(self.s("turned"), e + 2)
                        self.take_x(dve).then_inc(self.s("xt"), 1)
                    dve.wait_ge(self.s("h_turned"), e + 1)
                    self.take_ht(dve).then_inc(self.s("ht"), 1)
                self.loop(dve, body)
                n = dve.value_load(ovn[0:1, 0:1], min_val=0, max_val=EXTRA)
                for j in range(EXTRA):
                    with dve.If(n > j):
                        dve.wait_ge(self.s("x_turned"), j + 1)
                        self.take_x(dve).then_inc(self.s("x_xt"), 1)
                        dve.wait_ge(self.s("x_silu"), j + 1)
                        dve.tensor_tensor(self.HR, self.SA, bank(1), ALU.mult).then_inc(self.s("x_h"), 1)
                        dve.wait_ge(self.s("x_h_turned"), j + 1)
                        self.take_ht(dve).then_inc(self.s("x_ht"), 1)

            def act(self, act):
                def result(e):
                    act.wait_ge(self.s("downed"), e + 1)
                    if not is_at(e, 0):
                        act.wait_ge(self.s("stored"), 16 * e)
                    act.activation(self.Y, psum[:, 5 * BANK:7 * BANK], ACT.Copy).then_inc(self.s("y"), 1)
                    act.wait_ge(self.s("y"), e + 1)
                    act.dma_start(self.yb[e], self.Y).then_inc(self.s("stored"), 16)

                def body(e):
                    first, last = is_at(e, 0), is_at(e, NE - 1)
                    if first:
                        act.dma_start(self.XG, self.xgb[0]).then_inc(self.s("rows"), 16)
                        act.wait_ge(self.s("turned"), 1)
                        act.dma_start(self.XG, self.xgb[1]).then_inc(self.s("rows"), 16)
                    act.wait_ge(self.s("upped"), e + 1)
                    act.activation(self.SA, bank(0), ACT.Silu).then_inc(self.s("silu"), 1)
                    if not last and not is_at(e, NE - 2):
                        act.wait_ge(self.s("turned"), e + 2)
                        act.dma_start(self.XG, self.xgb[e + 2]).then_inc(self.s("rows"), 16)
                    if not first:
                        result(e - 1)
                    if last:
                        result(e)
                self.loop(act, body)
                act.wait_ge(self.s("stored"), 16 * NE)
                n = act.value_load(ovn[0:1, 0:1], min_val=0, max_val=EXTRA)
                for j in range(EXTRA):
                    with act.If(n > j):
                        act.dma_start(self.XG, self.xgb[NE + j]).then_inc(self.s("x_rows"), 16)
                        act.wait_ge(self.s("x_upped"), j + 1)
                        act.activation(self.SA, bank(0), ACT.Silu).then_inc(self.s("x_silu"), 1)
                        act.wait_ge(self.s("x_down"), j + 1)
                        act.activation(self.Y, psum[:, 5 * BANK:7 * BANK], ACT.Copy).then_inc(self.s("x_y"), 1)
                        act.wait_ge(self.s("x_y"), j + 1)
                        act.dma_start(self.yb[NE + j], self.Y).then_inc(self.s("x_stored"), 16)
                        act.wait_ge(self.s("x_stored"), 16 * (j + 1))

            def pool(self, pool):
                pool.nop().then_inc(self.s("open"), 1)

        class Combine(Stage):
            YG = region(0, 2, NT, D)

            def pool(self, pool):
                for t in range(NT):
                    for k in range(2):
                        pool.indirect_dma_start(self.YG[:, k, t, :], None, y_dram,
                                                bass.IndirectOffsetOnAxis(ap=didx[:, k, t:t + 1], axis=0))\
                            .then_inc(self.s(f"got{t}"), 16)

            def dve(self, dve):
                for t in range(NT):
                    dve.wait_ge(self.s(f"got{t}"), 32)
                    for k in range(2):
                        dve_step.then(dve, dve.scalar_tensor_tensor(H[:, t, :], self.YG[:, k, t, :], gates[:, k, t:t + 1],
                                                                    H[:, t, :], ALU.mult, ALU.add))

        class FoxDecay(Stage):

            def __init__(self, tag, z, c, nc_, tmp, QT, KT, half):
                super().__init__(tag)
                self.z, self.c, self.nc_, self.tmp, self.QT, self.KT, self.half = z, c, nc_, tmp, QT, KT, half

            def dve(self, dve):
                dve.memset(self.QT[64:66, :, :], 1.0)
                dve.memset(self.KT[64:66, :, :], 1.0).then_inc(self.s("ones"), 1)
                if self.half:
                    return
                z, c, tmp = self.z[0:FOX_H], self.c[0:FOX_H], self.tmp[0:FOX_H]
                dve.scalar_tensor_tensor(tmp, z, -1.0, z, ALU.mult, ALU.max).then_inc(self.s("abs"), 1)
                dve.wait_ge(self.s("log"), 2)
                dve_step.then(dve, dve.scalar_tensor_tensor(tmp, z, 0.0, tmp, ALU.min, ALU.subtract))
                dve_step.then(dve, dve.memset(z, 1.0))
                dve_step.then(dve, dve.tensor_tensor_scan(c, z, tmp, 0.0, ALU.mult, ALU.add))
                dve.tensor_scalar(self.nc_[0:FOX_H], c, -1.0, None, ALU.mult).then_inc(self.s("cum"), 1)

            def act(self, act):
                if not self.half:
                    tmp = self.tmp[0:FOX_H]
                    act.wait_ge(self.s("abs"), 1)
                    act.activation(tmp, tmp, ACT.Exp, scale=-1.0).then_inc(self.s("log"), 1)
                    act.wait_ge(self.s("log"), 1)
                    act.activation(tmp, tmp, ACT.Ln, bias=1.0).then_inc(self.s("log"), 1)
                    act.wait_ge(self.s("cum"), 1)
                act.wait_ge(self.s("ones"), 1)
                for h in range(8):
                    g = 8 * self.half + h
                    act.dma_start(self.QT[64:65, h, :], self.c[g:g + 1, :]).then_inc(self.s("laid"), 16)
                    act.dma_start(self.KT[65:66, h, :], self.nc_[g:g + 1, :]).then_inc(self.s("laid"), 16)
                act.wait_ge(self.s("laid"), 16 * 16)

        def use_units(stage, *us):
            def sp(eng):
                for u in us:
                    Weights.load(eng, u)
            stage.sp = sp

        def loads(stage, *pairs):
            def pool(eng):
                for dst, src in pairs:
                    eng.dma_start(dst, src).then_inc(stage.s("small"), 16)
                eng.wait_ge(stage.s("small"), stage.at("small") + 16 * len(pairs))
            stage.pool = pool
            stage.small = 16 * len(pairs)

        def gain_cols(at):
            return lambda c: cols[:, at + c:at + c + 1]

        def fox():
            QT, KT = region(12288, 8, SEQ), region(16384, 8, SEQ)
            V, GT = region(20480, NT, 512), region(22528, 4, SEQ)
            c, nc_, z, tmp = (region(24576 + 512 * i, SEQ) for i in range(4))
            bf = rt[:, 11, 16:17]
            Norm("n0", H, D, NT, gain_cols(V_MIX), None, XT, 0, region(0, NT, D))
            w = io["fox_w_in"][0]
            for g in range(2):
                p = Products(f"fox{g}")
                us = [Weights.add((0, KC, 512, w[:, D * i + 512 * g:D * i + 512 * (g + 1)])) for i in range(4)]
                use_units(p, *us)
                if g == 0:
                    loads(p, (wr[:, :, 0:FOX_H], w[:, 4 * D:4 * D + FOX_H].rearrange("(c p) g -> p c g", p=P)),
                          (bf[0:FOX_H], io["fox_b_f"][0].unsqueeze(1)))
                for i, (dst, scale) in enumerate(((QT, DH ** -0.5), (KT, 1.0))):
                    for n in range(4):
                        def take(eng, ps, dst=dst, n=n, scale=scale):
                            if n % 2:
                                eng.activation(dst[0:64, 2 * n, :], ps[0][0:64, :], ACT.Copy, scale=scale)
                                return eng.activation(dst[0:64, 2 * n + 1, :], ps[0][64:128, :], ACT.Copy, scale=scale)
                            eng.tensor_scalar(dst[0:64, 2 * n, :], ps[0][0:64, :], scale, None, ALU.mult)
                            return eng.tensor_scalar(dst[0:64, 2 * n + 1, :], ps[0][64:128, :], scale, None, ALU.mult)
                        p.job("va"[n % 2], mm_T(us[i], 0, KC, 512, (n * P, n * P + P), XT, 0, SEQ), take,
                              units=(us[i],), release=(1,) if n == 3 else ())
                for t in range(NT):
                    s = "va"[t % 2]
                    p.job(s, mm_R(us[2], 0, KC, 512, 0, 512, XT, t), copy_out(s, V[:, t, :]), units=(us[2],),
                          release=(1,) if t == 3 else ())
                for n in range(4):
                    p.job("a", mm_T(us[3], 0, KC, 512, (n * P, n * P + P), XT, 0, SEQ), act_out(GT[:, n, :], ACT.Sigmoid),
                          units=(us[3],), release=(1,) if n == 3 else ())
                if g == 0:
                    def fill(pe, ps, p=p):
                        pe.wait_ge(p.s("small"), p.at("small") + 32)
                        for k in range(KC):
                            i = pe.matmul(ps[0][0:FOX_H, :], wr[:, k, 0:FOX_H], XT[:, k, 0:SEQ], start=(k == 0), stop=(k == KC - 1))
                        return i
                    p.job("v", fill, lambda eng, ps: eng.tensor_scalar(z[0:FOX_H], ps[0][0:FOX_H, :], bf[0:FOX_H], None, ALU.add))
                FoxDecay(f"dec{g}", z, c, nc_, tmp, QT, KT, g)
                causal = cst[:, C_CAUSAL:C_CAUSAL + P]
                Attend(f"fa{g}", 8, NT, lambda i: (0, (i + 1) * P),
                       lambda h, i: [(0, (i + 1) * P, QT[0:66, h, i * P:(i + 1) * P], KT[0:66, h, 0:(i + 1) * P])],
                       [(k, k, NT, {i: k * P for i in range(NT)}) for k in range(NT)],
                       lambda h, kt: V[:, kt, h * DH:(h + 1) * DH], lambda q: GT[:, q, :], lambda q: GT[:, q, :],
                       add=lambda dve, h, i: [(i * P, (i + 1) * P, causal)])
                u = Weights.add((0, 4, D, io["fox_w_out"][0][512 * g:512 * (g + 1), :]))
                use_units(OutProj(f"fo{g}", u, 4, GT, NT), u)

        def moe(layer):
            rows = region(0, NT, D)
            Norm(f"nf{layer}", H, D, NT, gain_cols(V_FFN + KC * layer), None, XT, 0, rows)
            Route(f"rt{layer}", layer, rows)
            Experts(f"ex{layer}", layer)
            Combine(f"cb{layer}")

        R_ROT, R_DEC = region(20480, 2, SEQ), region(21504, RET_H, SEQ)
        R_Q, R_K, R_V, R_G = region(3072, 2, SEQ), region(4096, 2, SEQ), region(5120, NT, RET_DV), region(7168, NT, RET_DV)
        R_ST, R_Y, R_YT = region(9216, NT, SEQ), region(11264, NT, RET_DV), region(13312, 4, SEQ)
        R_TMP = region(15360, 2, 4, SEQ)
        R_BN, R_MV = region(24000, NT, 6), region(24064, NT, 2)

        class Retain(Stage):
            kind = "retain"

            def totals(self):
                return dict(scored=NT, decayed=NT, weighed=NT, squares=1, inv=1, root=1, rstd=1, normed=NT, gated=NT, turned=4)

            def __init__(self, tag, h):
                super().__init__(tag)
                self.h = h

            def pe(self, pe):
                for j in range(NT):
                    for c in range(2):
                        i = pe.matmul(bank(j, SEQ - j * P), R_K[:, c, j * P:(j + 1) * P], R_Q[:, c, j * P:SEQ],
                                      start=(c == 0), stop=(c == 1))
                    i.then_inc(self.s("scored"), 1)
                for i in range(NT):
                    pe.wait_ge(self.s("decayed"), self.at("decayed") + i + 1)
                    for j in range(i + 1):
                        m = pe.matmul(bank(4 + i), R_ST[:, j, (i - j) * P:(i - j + 1) * P], R_V[:, j, :],
                                      start=(j == 0), stop=(j == i))
                    m.then_inc(self.s("weighed"), 1)
                pe.wait_ge(self.s("gated"), self.at("gated") + NT)
                for c in range(4):
                    for i in range(NT):
                        m = pe.transpose(bank(c)[:, i * P:(i + 1) * P], R_Y[:, i, c * P:(c + 1) * P], ident)
                    m.then_inc(self.s("turned"), 1)

            def dve(self, dve):
                for j in range(NT):
                    dve.wait_ge(self.s("scored"), self.at("scored") + j + 1)
                    dve.tensor_tensor(R_ST[:, j, 0:SEQ - j * P], bank(j, SEQ - j * P), R_DEC[:, self.h, 0:SEQ - j * P], ALU.mult)\
                        .then_inc(self.s("decayed"), 1)
                for i in range(NT):
                    dve.wait_ge(self.s("weighed"), self.at("weighed") + i + 1)
                    dve_step.then(dve, dve.bn_stats(R_BN[:, i, :], bank(4 + i)))
                    ins = dve.bn_aggr(R_MV[:, i, :], R_BN[:, i, :])
                dve_step.then(dve, ins)
                dve.tensor_copy(st[:, 0, 0:NT], R_MV[:, :, 1]).then_inc(self.s("squares"), 1)
                inverse_roots(self, dve, NT, 1)
                for i in range(NT):
                    dve.tensor_scalar(R_Y[:, i, :], bank(4 + i), R_MV[:, i, 0:1], st[:, 3, i:i + 1], ALU.subtract, ALU.mult)\
                        .then_inc(self.s("normed"), 1)
                for c in range(0, 4, 2):
                    self.take(dve, c)

            def take(self, eng, c):
                eng.wait_ge(self.s("turned"), self.at("turned") + c + 1)
                at = V_GN + 4 * self.h + c
                if c % 2:
                    eng.activation(R_YT[:, c, :], bank(c), ACT.Copy, scale=cols[:, at:at + 1])
                else:
                    eng.tensor_scalar(R_YT[:, c, :], bank(c), cols[:, at:at + 1], None, ALU.mult)

            def pool(self, pool):
                for i in range(NT):
                    pool.wait_ge(self.s("normed"), self.at("normed") + i + 1)
                    pool.tensor_tensor(R_Y[:, i, :], R_Y[:, i, :], R_G[:, i, :], ALU.mult).then_inc(self.s("gated"), 1)

            def act(self, act):
                roots(self, act, NT)
                for c in range(1, 4, 2):
                    self.take(act, c)

        def retention():
            Norm("n1", H, D, NT, gain_cols(V_MIX + KC), None, XT, 0, region(0, NT, D))
            w = io["ret_w_in"][0]
            for h in range(RET_H):
                p = Products(f"ret{h}")
                qk = Weights.add((0, KC, 256, w[:, 256 * h:256 * (h + 1)]), (2048, KC, 256, w[:, D + 256 * h:D + 256 * (h + 1)]))
                uv = Weights.add((0, KC, 512, w[:, 2 * D + 512 * h:2 * D + 512 * (h + 1)]))
                ug = Weights.add((0, KC, 512, w[:, 4 * D + 512 * h:4 * D + 512 * (h + 1)]))
                use_units(p, qk, uv, ug)
                if h == 0:
                    loads(p, (R_ROT, io["rot"]), (R_DEC, io["decay"]))
                for i, dst in enumerate((R_Q, R_K)):
                    def fill(pe, ps, i=i, qk=qk):
                        wv = Weights.view(qk, 2048 * i, KC, 256)
                        for b in range(2):
                            for c in range(KC):
                                m = pe.matmul(ps[b], wv[:, c, b * P:(b + 1) * P], XT[:, c, 0:SEQ], start=(c == 0), stop=(c == KC - 1))
                        return m

                    def take(dve, ps, i=i, dst=dst, h=h, p=p):
                        cos, sin = R_ROT[:, 0, :], R_ROT[:, 1, :]
                        t = R_TMP[:, i]
                        if h == 0 and i == 0:
                            dve.wait_ge(p.s("small"), p.at("small") + 32)
                        dve.tensor_tensor(t[:, 0, :], ps[0], cos, ALU.mult)
                        dve.tensor_tensor(t[:, 1, :], ps[1], sin, ALU.mult)
                        dve.tensor_tensor(t[:, 2, :], ps[0], sin, ALU.mult)
                        dve_step.then(dve, dve.tensor_tensor(t[:, 3, :], ps[1], cos, ALU.mult))
                        dve.tensor_tensor(dst[:, 0, :], t[:, 0, :], t[:, 1, :], ALU.subtract)
                        return dve.tensor_tensor(dst[:, 1, :], t[:, 2, :], t[:, 3, :], ALU.add)
                    p.job("v", fill, take, units=(qk,), release=(1,) if i else (), n_banks=2)
                for t in range(NT):
                    p.job("a", mm_R(uv, 0, KC, 512, 0, 512, XT, t), act_out(R_V[:, t, :], ACT.Copy), units=(uv,),
                          release=(1,) if t == 3 else ())
                for t in range(NT):
                    p.job("a", mm_R(ug, 0, KC, 512, 0, 512, XT, t), act_out(R_G[:, t, :], ACT.Silu), units=(ug,),
                          release=(1,) if t == 3 else ())
                Retain(f"rn{h}", h)
                u = Weights.add((0, 4, D, io["ret_w_out"][0][512 * h:512 * (h + 1), :]))
                use_units(OutProj(f"ro{h}", u, 4, R_YT, NT), u)

        A_ROWS, A_B, A_SC = region(0, P), region(128, 48), region(256, KC, 2)

        class AdaPrep(Stage):
            def act(self, act):
                act.wait_ge(self.s("clear"), 1)
                act.dma_start(A_ROWS[0:48, :], io["ada_b_2"].rearrange("l (c p) -> (l c) p", p=P)).then_inc(self.s("rows"), 16)
                act.activation(A_SC[:, :, 0], cols[:, V_C:V_C + KC], ACT.Silu)
                act.activation(A_SC[:, :, 1], cols[:, V_CC:V_CC + KC], ACT.Silu)

            def dve(self, dve):
                dve.memset(A_ROWS, 0.0).then_inc(self.s("clear"), 1)
                dve.wait_ge(self.s("turned"), 1)
                dve.tensor_copy(A_B, bank(0, 48))

            def pe(self, pe):
                pe.wait_ge(self.s("rows"), 16)
                pe.transpose(bank(0, P), A_ROWS, ident).then_inc(self.s("turned"), 1)

        def modulation():
            AdaPrep("ap")
            p = Products("ada")
            us = []
            for layer in range(2):
                for q in range(6):
                    u = Weights.add((0, KC, 512, io["ada_w_2"][layer][:, 512 * q:512 * (q + 1)]))
                    us.append(u)

                    def fill(pe, ps, u=u):
                        w = Weights.view(u, 0, KC, 512)
                        for n in range(4):
                            for c in range(KC):
                                i = pe.matmul(ps[0][:, 2 * n:2 * n + 2], w[:, c, n * P:(n + 1) * P], A_SC[:, c, :],
                                              start=(c == 0), stop=(c == KC - 1))
                        return i

                    def take(dve, ps, layer=layer, q=q):
                        b = A_B[:, 24 * layer + 4 * q:24 * layer + 4 * q + 4].unsqueeze(2).broadcast_to([P, 4, 2])
                        m = dve.tensor_tensor(modc[:, layer, 4 * q:4 * q + 4, :], ps[0][:, 0:8].rearrange("p (n g) -> p n g", g=2), b, ALU.add)
                        if q != 3:
                            return m
                        dve_step.then(dve, m)
                        g = cols[:, V_NG + KC * layer:V_NG + KC * (layer + 1)].unsqueeze(2).broadcast_to([P, KC, 2])
                        return dve.scalar_tensor_tensor(amod[:, layer], modc[:, layer, 8:16, :], 1.0, g, ALU.add, ALU.mult)
                    p.job("v", fill, take, units=(u,), release=(1,))
            use_units(p, *us)

        def mod_norms(layer):
            for g, (rows, tiles, tok0) in enumerate(((H, NT, 0), (HC, NCT, SEQ))):
                Norm(f"m{layer}{g}", rows, D, tiles, lambda c, g=g: amod[:, layer, c, g:g + 1],
                     lambda c, g=g: modc[:, layer, c, g:g + 1], XT, tok0, region(0, NT, D))

        def tok_T(p, us, at, k, n, cs, x, dst, take_of, eng, ctx_too=True, release=False):
            p.job(eng, mm_T(us, at, k, n, cs, x, 0, SEQ), take_of(dst[:, 0:SEQ]), units=(us,),
                  release=(1,) if release and not ctx_too else ())
            if ctx_too:
                p.job(eng, mm_T(us, at, k, n, cs, x, SEQ, CTX), take_of(dst[:, SEQ:SEQ + CTX]), units=(us,),
                      release=(1,) if release else ())

        FULL_KEYS = lambda tiles, nq: [(k, 0, nq, {i: n * P for i in range(nq)}) for n, k in enumerate(tiles)]

        def pair_q(x, h, t):
            b = (h % 2) * DH
            return x[b:b + DH, h // 2, t * P:(t + 1) * P]

        def mixer_a():
            QT, KT = region(12288, 4, NTA * P), region(15360, 2, NTA * P)
            V, ZT = region(16896, NTA, P), region(17664, 4, NTA * P)
            QR, KR = region(20736, 2, 512), region(21760, 2, 2, 2, DH)
            TMP = region(22272, 4, 256)
            w = io["ab_in_w_2"][0]
            p = Products("pa")
            uq = Weights.add((0, KC, 512, w[:, 0:512]))
            uk = Weights.add((0, KC, 256, w[:, 512:768]))
            uz = Weights.add((0, KC, 512, w[:, 768:1280]))
            use_units(p, uq, uk, uz)
            turned = [None, None]
            pend = []

            def flush(n):
                while len(pend) > n:
                    f = pend.pop(0)
                    turned[f[0] % 2] = f[1]()
            for t in range(NTA):
                cos = cst[:, C_COSA + 32 * t:C_COSA + 32 * (t + 1)]
                sin = cst[:, C_SINA + 32 * t:C_SINA + 32 * (t + 1)]
                buf = QR[:, t % 2, :]
                if t < NT:
                    take = rope_rows(buf.rearrange("p (h i two) -> p h i two", h=8, two=2),
                                     lambda ps: ps[0][:, 0:512].rearrange("p (h i two) -> p h i two", h=8, two=2),
                                     cos, sin, 8, 32, [TMP[:, i, :].rearrange("p (h i) -> p h i", h=8) for i in range(4)])
                else:
                    take = copy_out("v", buf)
                made = p.job("v", mm_R(uq, 0, KC, 512, 0, 512, XT, t), take, units=(uq,), release=(1,) if t == NTA - 1 else (),
                             after=[turned[t % 2]] if turned[t % 2] else [], scratch=True)

                def later(t=t, buf=buf, made=made):
                    return p.job("a", turn([buf[:, c * P:(c + 1) * P] for c in range(4)]),
                                 copy_out("a", QT[:, :, t * P:(t + 1) * P], DH ** -0.5), after=[made])
                pend.append((t, later))
                flush(1)
            flush(0)
            turned = [None, None]
            for t in range(NTA):
                cos = cst[:, C_COSA + 32 * t:C_COSA + 32 * (t + 1)]
                sin = cst[:, C_SINA + 32 * t:C_SINA + 32 * (t + 1)]
                kr = KR[:, t % 2]

                def take(dve, ps, t=t, kr=kr, cos=cos, sin=sin):
                    first = kr[:, :, 0, :]
                    if t < NT:
                        i = rope_rows(first.rearrange("p h (i two) -> p h i two", two=2),
                                      lambda ps: ps[0][:, 0:P].rearrange("p (h i two) -> p h i two", h=2, two=2),
                                      cos, sin, 2, 32, [TMP[:, j, 0:64].rearrange("p (h i) -> p h i", h=2) for j in range(4)])(dve, ps)
                    else:
                        i = dve.tensor_copy(first, ps[0][:, 0:P].rearrange("p (h d) -> p h d", h=2))
                    dve_step.then(dve, i)
                    dve.tensor_copy(kr[:, :, 1, :], first)
                    return dve.tensor_copy(V[:, t, :], ps[0][:, P:2 * P])
                made = p.job("v", mm_R(uk, 0, KC, 256, 0, 256, XT, t), take, units=(uk,), release=(1,) if t == NTA - 1 else (),
                             after=[turned[t % 2]] if turned[t % 2] else [], scratch=True)

                def later(t=t, kr=kr, made=made):
                    return p.job("a", turn([kr[:, g].rearrange("p c d -> p (c d)") for g in range(2)]),
                                 copy_out("a", KT[:, :, t * P:(t + 1) * P]), after=[made])
                pend.append((t, later))
                flush(1)
            flush(0)
            for n in range(4):
                tok_T(p, uz, 0, KC, 512, (n * P, n * P + P), XT, ZT[:, n, :], lambda d: act_out(d, ACT.Silu), "a", release=n == 3)

            anti, causal = cst[:, C_ANTI:C_ANTI + P], cst[:, C_CAUSAL:C_CAUSAL + P]
            lo = lambda i: max(0, i - 1)
            hi = lambda i: min(NT, i + 2)
            width = lambda i: (hi(i) - lo(i)) * P

            def kT(h, a, b):
                g, base = h // 4, (h % 2) * DH
                return KT[base:base + DH, g, a * P:b * P]

            def adds(dve, h, i):
                r = []
                if i > 0:
                    r.append((512 - width(i), 512 - width(i) + P, anti))
                if i < NT - 1:
                    r.append((512 - P, 512, causal))
                return r
            local = [(k, lo(k), hi(k), {i: (k - lo(i)) * P for i in range(lo(k), hi(k))}) for k in range(NT)]
            ctxk = [(NT + c, 0, NT, {i: width(i) + c * P for i in range(NT)}) for c in range(NCT)]
            a = Attend("aa", 8, NT, lambda i: (512 - width(i), 768),
                       lambda h, i: [(512 - width(i), 512, pair_q(QT, h, i), kT(h, lo(i), hi(i))),
                                     (512, 768, pair_q(QT, h, i), kT(h, NT, NTA))],
                       ctxk + local, lambda h, kt: V[:, kt, (h // 4) * DH:(h // 4 + 1) * DH],
                       lambda q: ZT[:, q, 0:SEQ], lambda q: ZT[:, q, 0:SEQ], add=adds, sink=True)
            Attend("ac", 8, NCT, lambda i: (0, CTX),
                   lambda h, i: [(0, CTX, pair_q(QT, h, NT + i), kT(h, NT, NTA))],
                   FULL_KEYS([NT, NT + 1], NCT), lambda h, kt: V[:, kt, (h // 4) * DH:(h // 4 + 1) * DH],
                   lambda q: ZT[:, q, SEQ:SEQ + CTX], lambda q: ZT[:, q, SEQ:SEQ + CTX], sink=True)
            u = Weights.add((0, 4, D, io["ab_out_w_2"][0][0:512, :]))
            use_units(OutProj("oa", u, 4, ZT, NTA, 0), u)

        def mixer_b():
            cqT, ckvT, KR = region(12288, 3, NTA * P), region(14592, 2, NTA * P), region(16128, NTA, B_ROPE)
            QT, KT = region(16320, 4, NTA * P), region(19392, 4, NTA * P)
            V, ZT = region(22464, NTA, 256), region(24000, 2, NTA * P)
            CQ, CKV = region(0, NTA, Q_LORA), region(2304, NTA, KV_LORA)
            TMP = region(4096, 4, 64)
            w = io["ab_in_w_2"][0]
            p = Products("pb")
            u1 = Weights.add((0, KC, 384, w[:, 1280:1664]))
            u2 = Weights.add((0, KC, 288, w[:, 1664:1952]))
            use_units(p, u1, u2)
            for t in range(NTA):
                s = "va"[t % 2]
                p.job(s, mm_R(u1, 0, KC, 384, 0, 384, XT, t), copy_out(s, CQ[:, t, :]), units=(u1,),
                      release=(1,) if t == NTA - 1 else ())

            def tabs(t):
                return cst[:, C_COSB + 16 * t:C_COSB + 16 * (t + 1)], cst[:, C_SINB + 16 * t:C_SINB + 16 * (t + 1)]
            for t in range(NTA):
                def take(dve, ps, t=t):
                    dve.tensor_copy(CKV[:, t, :], ps[0][:, 0:256])
                    kr = ps[0][:, 256:288]
                    if t >= NT:
                        return dve.tensor_copy(KR[:, t, :], kr)
                    cos, sin = tabs(t)
                    return rope_rows(KR[:, t, :].rearrange("p (h i two) -> p h i two", h=1, two=2),
                                     lambda ps: kr.rearrange("p (h i two) -> p h i two", h=1, two=2),
                                     cos, sin, 1, 16, [TMP[:, j, 0:16].rearrange("p (h i) -> p h i", h=1) for j in range(4)])(dve, ps)
                p.job("v", mm_R(u2, 0, KC, 288, 0, 288, XT, t), take, units=(u2,), release=(1,) if t == NTA - 1 else (), scratch=True)
            for nm, rows, width, at, dst in (("q", CQ, Q_LORA, V_BQ, cqT), ("k", CKV, KV_LORA, V_BKV, ckvT)):
                Norm(f"b{nm}l", rows[:, 0:NT, :], width, NT, gain_cols(at), None, dst, 0, rows[:, 0:NT, :])
                Norm(f"b{nm}c", rows[:, NT:NTA, :], width, NCT, gain_cols(at), None, dst, SEQ, rows[:, NT:NTA, :])
            QR, KRW = region(0, 2, 4, B_QK), region(768, 2, 4, B_QK)
            TQ = region(2048, 4, 64)
            scale = B_QK ** -0.5
            for g in range(2):
                p = Products(f"pb{g}")
                uq = Weights.add((0, 3, 384, io["b_w_uq_2"][0][:, 384 * g:384 * (g + 1)]),
                                 (1152, 2, 512, io["b_w_ukv_2"][0][:, 512 * g:512 * (g + 1)]))
                uz = Weights.add((0, KC, 256, w[:, 1952 + 256 * g:1952 + 256 * (g + 1)]))
                use_units(p, uq, uz)
                turned, pend = [[None, None], [None, None]], []

                def flush(n):
                    while len(pend) > n:
                        which, t, f = pend.pop(0)
                        turned[which][t % 2] = f()
                for t in range(NTA):
                    def takeq(dve, ps, t=t):
                        src = ps[0][:, 0:384].rearrange("p (h d) -> p h d", h=4)
                        dst = QR[:, t % 2]
                        i = dve.tensor_copy(dst[:, :, 0:B_NOPE], src[:, :, 0:B_NOPE])
                        if t >= NT:
                            return dve.tensor_copy(dst[:, :, B_NOPE:B_QK], src[:, :, B_NOPE:B_QK])
                        cos, sin = tabs(t)
                        return rope_rows(dst[:, :, B_NOPE:B_QK].rearrange("p h (i two) -> p h i two", two=2),
                                         lambda ps: src[:, :, B_NOPE:B_QK].rearrange("p h (i two) -> p h i two", two=2),
                                         cos, sin, 4, 16, [TQ[:, j, :].rearrange("p (h i) -> p h i", h=4) for j in range(4)])(dve, ps)

                    def takek(dve, ps, t=t):
                        src = ps[0].rearrange("p (h d) -> p h d", h=4)
                        dst = KRW[:, t % 2]
                        dve.tensor_copy(dst[:, :, 0:B_NOPE], src[:, :, 0:B_NOPE])
                        dve.tensor_copy(V[:, t, :].rearrange("p (h d) -> p h d", h=4), src[:, :, B_NOPE:B_NOPE + B_V])
                        return dve.tensor_copy(dst[:, :, B_NOPE:B_QK], KR[:, t, :].unsqueeze(1).broadcast_to([P, 4, B_ROPE]))
                    for which, fill, take, buf, dst, sc in (
                            (0, mm_R(uq, 0, 3, 384, 0, 384, cqT, t), takeq, QR, QT, scale),
                            (1, mm_R(uq, 1152, 2, 512, 0, 512, ckvT, t), takek, KRW, KT, None)):
                        made = p.job("v", fill, take, units=(uq,), release=(1,) if which and t == NTA - 1 else (),
                                     after=[turned[which][t % 2]] if turned[which][t % 2] else [], scratch=True)

                        def later(t=t, buf=buf, dst=dst, sc=sc, made=made):
                            def take(eng, ps):
                                src = ps[0][0:B_QK, :].rearrange("p (h t) -> p h t", h=4)
                                return eng.activation(dst[0:B_QK, :, t * P:(t + 1) * P], src, ACT.Copy, scale=sc or 1.0)
                            return p.job("a", turn([buf[:, t % 2, h, :] for h in range(4)]), take, after=[made])
                        pend.append((which, t, later))
                        flush(2)
                flush(0)
                for n in range(2):
                    tok_T(p, uz, 0, KC, 256, (n * P, n * P + P), XT, ZT[:, n, :], lambda d: act_out(d, ACT.Silu), "a", release=n == 1)
                q = lambda h, t: QT[0:B_QK, h, t * P:(t + 1) * P]
                v = lambda h, kt: V[:, kt, h * DH:(h + 1) * DH]
                Attend(f"ba{g}", 4, NT, lambda i: (0, 768),
                       lambda h, i: [(0, 512, q(h, i), KT[0:B_QK, h, 0:SEQ]), (512, 768, q(h, i), KT[0:B_QK, h, SEQ:SEQ + CTX])],
                       FULL_KEYS(range(NTA), NT), v, lambda r: ZT[:, r, 0:SEQ], lambda r: ZT[:, r, 0:SEQ])
                Attend(f"bc{g}", 4, NCT, lambda i: (0, CTX),
                       lambda h, i: [(0, CTX, q(h, NT + i), KT[0:B_QK, h, SEQ:SEQ + CTX])],
                       FULL_KEYS([NT, NT + 1], NCT), v, lambda r: ZT[:, r, SEQ:SEQ + CTX], lambda r: ZT[:, r, SEQ:SEQ + CTX])
                u = Weights.add((0, 2, D, io["ab_out_w_2"][0][512 + 256 * g:512 + 256 * (g + 1), :]))
                use_units(OutProj(f"ob{g}", u, 2, ZT, NTA, 0), u)

        class Neighbours(Attend):
            table = 1
            TT = region(22528, 2, 14, GRID)

            def load(self, act, h):
                for j0, p0 in ((1, 0), (0, GRID)):
                    act.dma_start(self.TT[p0:p0 + GRID, h % 2], io["bands"][self.h0 + h, :, j0:j0 + 14, :])\
                        .then_inc(self.s(f"bias{h % 2}"), 16)

            def act(self, act):
                self.load(act, 0)
                self.load(act, 1)
                super().act(act)

            def before_exp(self, act, h, i):
                if i == 0 and 1 <= h < self.heads - 1:
                    act.wait_ge(self.s("max"), self.at("max") + h * self.nq)
                    self.load(act, h + 1)

            def pool(self, pool):
                def band(h):
                    x = self.TT[:, h % 2]
                    s = f"bias{h % 2}"
                    pool.wait_ge(self.s(s), self.at(s) + 32 * (h // 2 + 1))
                    pool.tensor_tensor(x, x, cst[:, C_WIN:C_WIN + GRID].unsqueeze(1).broadcast_to([P, 14, GRID]), ALU.add)\
                        .then_inc(self.s("banded"), 1)
                band(0)
                for h in range(self.heads):
                    if h + 1 < self.heads:
                        band(h + 1)
                    self.normalise(pool, h)

        def mixer_c():
            w = io["c_in_w_2"][0]
            for g in range(2):
                QT, KT = region(12288, 4, SEQ), region(14336, 4, NTA * P)
                V, ZT = region(17408, NTA, 512), region(20480, 4, SEQ)
                p = Products(f"pc{g}")
                us = [Weights.add((0, KC, 512, w[:, D * i + 512 * g:D * i + 512 * (g + 1)])) for i in range(4)]
                use_units(p, *us)
                for n in range(4):
                    cs = (n * P, n * P + P)
                    tok_T(p, us[0], 0, KC, 512, cs, XT, QT[:, n, :], lambda d: copy_out("v", d, DH ** -0.5), "v", False, n == 3)
                for n in range(4):
                    tok_T(p, us[1], 0, KC, 512, (n * P, n * P + P), XT, KT[:, n, :], lambda d: copy_out("a", d), "a", True, n == 3)
                for t in range(NTA):
                    s = "va"[t % 2]
                    p.job(s, mm_R(us[2], 0, KC, 512, 0, 512, XT, t), copy_out(s, V[:, t, :]), units=(us[2],),
                          release=(1,) if t == NTA - 1 else ())
                for n in range(4):
                    tok_T(p, us[3], 0, KC, 512, (n * P, n * P + P), XT, ZT[:, n, :], lambda d: act_out(d, ACT.Silu), "a", False, n == 3)

                def kT(h, a, b):
                    base = (h % 2) * DH
                    return KT[base:base + DH, h // 2, a:b]

                def adds(dve, h, i, at=(None,)):
                    if i == 0:
                        dve.wait_ge(at[0].s("banded"), at[0].at("banded") + h + 1)
                    tt = Neighbours.TT[:, h % 2].rearrange("p j k -> p (j k)")
                    s = (6 - 2 * i) * GRID
                    return [(0, SEQ, tt[:, s:s + SEQ])]
                a = Neighbours(f"na{g}", 8, NT, lambda i: (0, 768),
                               lambda h, i, QT=QT, kT=kT: [(0, 512, pair_q(QT, h, i), kT(h, 0, 512)), (512, 768, pair_q(QT, h, i), kT(h, 512, 768))],
                               FULL_KEYS(range(NTA), NT), lambda h, kt, V=V: V[:, kt, h * DH:(h + 1) * DH],
                               lambda r, ZT=ZT: ZT[:, r, :], lambda r, ZT=ZT: ZT[:, r, :])
                a.add = lambda dve, h, i, a=a: adds(dve, h, i, (a,))
                a.h0 = 8 * g
                u = Weights.add((0, 4, D, io["c_out_w_2"][0][512 * g:512 * (g + 1), :]))
                use_units(OutProj(f"oc{g}", u, 4, ZT, NT, 1), u)

        parts = [lambda: Start("start"), fox, lambda: moe(0), retention, lambda: moe(1),
                 lambda: RowNorm("nfin", io["norm_final"]), modulation, lambda: mod_norms(0), mixer_a, mixer_b,
                 lambda: mod_norms(1), mixer_c, lambda: RowNorm("last", io["final_g_2"], io["out"])]
        for part in parts[:upto]:
            part()

        block = ctx.enter_context(nc.Block())
        n_stage = len(stages)

        def run(eng, what):
            for k, stage in enumerate(stages):
                if k:
                    eng.wait_ge(stage_done, 4 * k)
                getattr_free(stage, what)(eng)
                eng.drain().then_inc(stage_done, 1)

        def getattr_free(stage, what):
            return {"pe": stage.pe, "act": stage.act, "dve": stage.dve, "pool": stage.pool}[what]

        @block.sync
        def _(sp):
            for stage in stages:
                stage.sp(sp)
            sp.wait_ge(stage_done, 4 * n_stage)
            if dbg:
                for n, (name, ap) in enumerate(dbg(dict(H=H,HC=HC,XT=XT,modc=modc,region=region,gates=gates,didx=didx,rt=rt,cols=cols,ovn=ovn,psum=psum))):
                    sp.dma_start(io[name], ap).then_inc(sem("dbg"), 16)
                    sp.wait_ge(sem("dbg"), 16 * (n + 1))

        @block.tensor
        def _(pe):
            run(pe, "pe")

        @block.scalar
        def _(act):
            run(act, "act")

        @block.vector
        def _(dve):
            run(dve, "dve")

        @block.gpsimd
        def _(pool):
            run(pool, "pool")
        print("semaphores", len(sems), "stages", n_stage)


_OUT = ((1, SEQ, D), "float32")


def kernel(**inputs):
    import concourse.bacc as bacc
    from concourse.bass_utils import run_bass_kernel_spmd

    nc = bacc.Bacc("TRN2", target_bir_lowering=False, num_devices=1, dynamic_dma_scratch_size=8192)
    consts, rot, decay = constants()
    arrays = {f"in_{k}": np.ascontiguousarray(v) for k, v in inputs.items()}
    arrays |= {"in_consts": consts, "in_rot": rot, "in_decay": decay, "in_bands": bands(np.asarray(inputs["c_rpb_2"])[0])}
    io = {k[3:]: nc.dram_tensor(k, a.shape, mybir.dt.from_np(a.dtype), kind="ExternalInput").ap() for k, a in arrays.items()}
    io["out"] = nc.dram_tensor("out", _OUT[0], F32, kind="ExternalOutput").ap()
    build(nc, io)
    r = run_bass_kernel_spmd(nc, [arrays], core_ids=[0])
    return r.results[0]["out"]
```

```python
from contextlib import ExitStack

import numpy as np

import concourse.bass as bass
from concourse import mybir

F32 = mybir.dt.float32
U32 = mybir.dt.uint32
ALU = mybir.AluOpType
ACT = mybir.ActivationFunctionType
AXX = mybir.AxisListType.X

P = 128
D = 1024
KC = D // P
SEQ, CTX = 512, 256
NT, NCT = SEQ // P, CTX // P
NTA = NT + NCT
BANK = 512
EPS = 1e-6
NEG = -1e30
FOX_H, DH = 16, 64
RET_H, RET_DK, RET_DV = 4, 256, 512
N_GROUPS, PER_GROUP = 4, 8
NE = N_GROUPS * PER_GROUP
NR = N_GROUPS + NE
FF = 512
BR = 64
EXTRA = (2 * SEQ - 2) // BR
SLOTS = (NE + EXTRA) * BR
B_NOPE, B_ROPE, B_V = 64, 32, 64
B_QK = B_NOPE + B_ROPE
Q_LORA, KV_LORA = 384, 256
GRID, KH, KW = 64, 8, 16
RING, SLOT = 3, 4096

C_ID, C_CAUSAL, C_ANTI, C_ONES, C_BEFORE = 0, 128, 256, 384, 512
C_IOTA, C_BASE, C_WIN = 640, 672, 704
C_COSA, C_SINA, C_COSB, C_SINB = 768, 896, 1024, 1088
C_ALL = 1152

V_MIX, V_FFN, V_NG, V_C, V_CC, V_GN, V_BQ, V_BKV = 0, 16, 32, 48, 56, 64, 80, 83
V_ALL = 85


def constants():
    f = np.float32
    c = np.zeros((P, C_ALL), f)
    i, j = np.arange(P)[:, None], np.arange(P)[None, :]
    c[:, C_ID:C_ID + P] = i == j
    c[:, C_CAUSAL:C_CAUSAL + P] = np.where(j <= i, 0, NEG)
    c[:, C_ANTI:C_ANTI + P] = np.where(j >= i, 0, NEG)
    c[:, C_ONES:C_ONES + P] = 1
    c[:, C_BEFORE:C_BEFORE + P] = i < j
    c[:, C_IOTA:C_IOTA + NE] = np.arange(NE)
    c[:, C_BASE:C_BASE + NE] = np.arange(NE) * BR
    q, k = (np.arange(P) % GRID)[:, None], np.arange(GRID)[None, :]
    lo = np.clip(q - KW // 2, 0, GRID - KW)
    c[:, C_WIN:C_WIN + GRID] = np.where((k >= lo) & (k < lo + KW), 0, NEG)
    t = np.arange(SEQ)
    for at_cos, at_sin, rot in ((C_COSA, C_SINA, DH), (C_COSB, C_SINB, B_ROPE)):
        n = rot // 4
        inv = f(10000.0) ** (-np.arange(n, dtype=f) / f(n))
        ang = np.concatenate([(t // GRID).astype(f)[:, None] * inv, (t % GRID).astype(f)[:, None] * inv], 1)
        for at, fn in ((at_cos, np.cos), (at_sin, np.sin)):
            c[:, at:at + NT * 2 * n] = fn(ang).astype(f).reshape(NT, P, 2 * n).transpose(1, 0, 2).reshape(P, -1)
    half = RET_DK // 2
    inv = f(1.0) / (f(10000.0) ** np.linspace(0.0, 1.0, half, dtype=f))
    ang = np.arange(SEQ, dtype=f)[None, :] * inv[:, None].astype(f)
    rot = np.stack([np.cos(ang), np.sin(ang)], 1).astype(f)
    rel = (np.arange(SEQ)[None, :] - np.arange(P)[:, None]).astype(np.float64)
    decay = [np.where(rel >= 0, (1 - 2.0 ** (-5 - h)) ** np.maximum(rel, 0), 0) * RET_DK ** -0.5 for h in range(RET_H)]
    return c, rot, np.stack(decay, 1).astype(f)


def bands(rpb):
    h, rows, n = rpb.shape
    wide = np.zeros((h, rows, 2 * GRID - 1), rpb.dtype)
    at = GRID - 1 - n // 2
    wide[:, :, at:at + n] = rpb
    return np.stack([wide[:, :, GRID - 1 - q:2 * GRID - 1 - q] for q in range(GRID)], 1)


def build(nc, io):
    ctx = ExitStack()
    with ctx:
        def sb(name, shape, dt=F32):
            return ctx.enter_context(nc.sbuf_tensor(name, shape, dt))

        sems = {}

        def sem(name):
            if name not in sems:
                sems[name] = ctx.enter_context(nc.semaphore(name))
            return sems[name]

        def dram(name, shape):
            return nc.dram_tensor(name, shape, F32, kind="Internal").ap()

        H = sb("H", [P, NT, D])
        HC = sb("HC", [P, NCT, D])
        XT = sb("XT", [P, KC, NTA * P])
        ring = sb("ring", [P, RING, SLOT])
        cst = sb("cst", [P, C_ALL])
        cols = sb("cols", [P, P])
        modc = sb("modc", [P, 2, 24, 2])
        amod = sb("amod", [P, 2, KC, 2])
        st = sb("st", [P, 4, 8])
        sm = sb("sm", [P, 4, 36])
        cmod = sb("cmod", [P, KC, 32])
        adab = sb("adab", [P, 48])
        sinkb = sb("sinkb", [P, 8])
        rt = sb("rt", [P, 12, 128])
        rbias = sb("rbias", [P, NR])
        wr = sb("wr", [P, KC, NR])
        didx = sb("didx", [P, 2, NT], U32)
        gates = sb("gates", [P, 2, NT])
        top8 = sb("top8", [P, 4, NT, 8])
        top8i = sb("top8i", [P, 2, NT, 8], U32)
        ovn = sb("ovn", [1, 16], U32)
        arena_f = 26624
        arena = sb("arena", [P, arena_f])
        psum = ctx.enter_context(nc.psum_tensor("psum", [P, 8 * BANK], F32))

        xg_dram = dram("xg_dram", [SLOTS, D])
        y_dram = dram("y_dram", [SLOTS, D])

        ident = cst[:, C_ID:C_ID + P]
        ones = cst[:, C_ONES:C_ONES + P]

        def bank(i, n=BANK, p=P):
            return psum[0:p, i * BANK:i * BANK + n]

        def region(at, *shape):
            n = int(np.prod(shape))
            assert at + n <= arena_f, (at, shape)
            v = arena[:, at:at + n]
            names = "abcd"[:len(shape)]
            if len(shape) == 1:
                return v
            return v.rearrange(f"p ({' '.join(names)}) -> p {' '.join(names)}",
                               **{m: s for m, s in zip(names, shape)})

        class Count:

            def __init__(self, name):
                self.sem, self.n = sem(name), 0

            def on(self, ins):
                self.n += 1
                ins.then_inc(self.sem, 1)
                return self.n

            def then(self, eng, ins):
                self.on(ins)
                eng.wait_ge(self.sem, self.n)

        dve_step = Count("dve_step")
        act_step = Count("act_step")
        pool_step = Count("pool_step")

        w_ready = [sem(f"w_ready{i}") for i in range(RING)]

        class Weights:
            units, value, per, freed = [], [], [0] * RING, {}

            @classmethod
            def add(cls, *pieces):
                u = len(cls.units)
                cls.units.append(pieces)
                cls.per[u % RING] += 16 * len(pieces)
                cls.value.append(cls.per[u % RING])
                return u

            @classmethod
            def view(cls, u, at, k, n):
                return ring[:, u % RING, at:at + k * n].rearrange("p (k n) -> p k n", k=k)

            @classmethod
            def wait(cls, eng, u):
                eng.wait_ge(w_ready[u % RING], cls.value[u])

            @classmethod
            def load(cls, sp, u):
                if u >= RING:
                    sp.wait_ge(*cls.freed[u - RING])
                for at, k, n, src in cls.units[u]:
                    sp.dma_start(cls.view(u, at, k, n), src.rearrange("(k p) n -> p k n", p=P))\
                        .then_inc(w_ready[u % RING], 16)

        stages = []
        stage_done = sem("stage_done")

        class Stage:
            kind = None

            def __init__(self, tag):
                self.tag, self.earlier = tag, [x for x in stages if self.kind and x.kind == self.kind]
                stages.append(self)

            def s(self, name):
                return sem(f"{self.kind or self.tag}_{name}")

            def at(self, name):
                return sum(x.totals().get(name, 0) for x in self.earlier)

            def pe(self, pe): pass
            def act(self, act): pass
            def dve(self, dve): pass
            def pool(self, pool): pass
            def sp(self, sp): pass

        class Start(Stage):
            ROWS = region(0, P)
            BIAS = region(128, P)
            ZERO = rt[:, 0:8, :].rearrange("p a b -> p (a b)")

            def act(self, act):
                act.dma_start(cst[:, :], io["consts"]).then_inc(self.s("const"), 16)
                act.dma_start(H[:, :, :], io["x"][0].rearrange("(t p) d -> p t d", p=P)).then_inc(self.s("rows"), 16)

                def vec(at, ap):
                    n = ap.shape[0]
                    act.dma_start(self.ROWS[at:at + n, :], ap).then_inc(self.s("vec"), 16)

                act.wait_ge(self.s("clear"), 1)
                vec(V_MIX, io["norm_mix"].rearrange("l (c p) -> (l c) p", p=P))
                vec(V_FFN, io["norm_ffn"].rearrange("l (c p) -> (l c) p", p=P))
                vec(V_NG, io["norm_g_2"].rearrange("l (c p) -> (l c) p", p=P))
                vec(V_C, io["c_2"].rearrange("l (c p) -> (l c) p", p=P))
                vec(V_CC, io["c_ctx_2"].rearrange("(c p) -> c p", p=P))
                vec(V_GN, io["ret_gn_gain"].rearrange("l (c p) -> (l c) p", p=P))
                vec(V_BQ, io["b_q_norm_g_2"].rearrange("l (c p) -> (l c) p", p=P))
                vec(V_BKV, io["b_kv_norm_g_2"].rearrange("l (c p) -> (l c) p", p=P))
                act.dma_start(self.BIAS[0:48, :], io["ada_b_2"].rearrange("l (c p) -> (l c) p", p=P)).then_inc(self.s("vec"), 16)
                act.dma_start(sinkb[:, :], io["a_sink_2"][0].partition_broadcast(P)).then_inc(self.s("vec"), 16)
                act.wait_ge(self.s("rows"), 16)
                act.wait_ge(self.s("cols"), 1)
                for g, at in enumerate((V_C, V_CC)):
                    act.activation(cmod[:, :, g], cols[:, at:at + KC], ACT.Silu)

            def dve(self, dve):
                dve.memset(region(0, 2 * P), 0.0).then_inc(self.s("clear"), 1)
                dve.memset(cmod[:, :, :], 0.0)
                dve.memset(self.ZERO[:, :], 0.0).then_inc(self.s("zero"), 1)
                dve.memset(top8[:, 0, :, :], NEG)
                dve.wait_ge(self.s("turned"), 1)
                dve.tensor_copy(adab[:, :], bank(1, 48))
                dve.tensor_copy(cols[:, :], bank(0, P)).then_inc(self.s("cols"), 1)
                dve.wait_ge(self.s("vec"), 10 * 16)
                dve.tensor_scalar(rt[:, 11, 0:8], sinkb[:, :], -1.0, None, ALU.mult)

            def pe(self, pe):
                pe.wait_ge(self.s("const"), 16)
                pe.wait_ge(self.s("vec"), 10 * 16)
                pe.wait_ge(self.s("clear"), 1)
                pe.transpose(bank(0, P), self.ROWS[:, :], ident)
                pe.transpose(bank(1, P), self.BIAS[:, :], ident).then_inc(self.s("turned"), 1)

            def sp(self, sp):
                sp.wait_ge(self.s("rows"), 16)
                sp.wait_ge(self.s("vec"), 10 * 16)

        def clear_blocks(sp):
            sp.dma_start(HC[:, :, :], io["ctx_2"][0].rearrange("(t p) d -> p t d", p=P)).then_inc(sem("start_context"), 16)
            sp.wait_ge(sem("start_zero"), 1)
            for x, b0, b1 in ((xg_dram, 0, NE + EXTRA), (y_dram, NE, NE + EXTRA)):
                x = x[b0 * BR:b1 * BR, :]
                n = x.shape[0] // P * P
                sp.dma_start(x[0:n].rearrange("(n p) d -> p n d", p=P),
                             Start.ZERO.unsqueeze(1).broadcast_to([P, n // P, D])).then_inc(sem("start_cleared"), 16)
                if n < x.shape[0]:
                    sp.dma_start(x[n:], Start.ZERO[0:x.shape[0] - n, :]).then_inc(sem("start_cleared"), 16)

        def blocks_cleared(eng):
            eng.wait_ge(sem("start_context"), 16)
            eng.wait_ge(sem("start_cleared"), 16 * 4)

        def squares(stage, act, rows, junk):
            for t, r in enumerate(rows):
                i = act.activation(junk, r, ACT.Square, accum_out=st[:, 0, t:t + 1])
                if t < len(rows) - 1:
                    act_step.then(act, i)
            i.then_inc(stage.s("squares"), 1)
            roots(stage, act, len(rows))

        def roots(stage, act, n):
            act.wait_ge(stage.s("inv"), stage.at("inv") + 1)
            act.activation(st[:, 2, 0:n], st[:, 1, 0:n], ACT.Sqrt).then_inc(stage.s("root"), 1)

        def inverse_roots(stage, dve, n, width):
            ms, inv, y0, y = st[:, 0, 0:n], st[:, 1, 0:n], st[:, 2, 0:n], st[:, 3, 0:n]
            dve.wait_ge(stage.s("squares"), stage.at("squares") + 1)
            dve_step.then(dve, dve.tensor_scalar(ms, ms, 1.0 / width, EPS, ALU.mult, ALU.add))
            dve.reciprocal(inv, ms).then_inc(stage.s("inv"), 1)
            dve.wait_ge(stage.s("root"), stage.at("root") + 1)
            dve_step.then(dve, dve.tensor_tensor(y, y0, y0, ALU.mult))
            dve_step.then(dve, dve.tensor_tensor(y, y, ms, ALU.mult))
            dve_step.then(dve, dve.tensor_scalar(y, y, -0.5, 1.5, ALU.mult, ALU.add))
            dve.tensor_tensor(y, y, y0, ALU.mult).then_inc(stage.s("rstd"), 1)
            dve.wait_ge(stage.s("rstd"), stage.at("rstd") + 1)

        class Norm(Stage):
            kind = "norm"

            def totals(self):
                return dict(squares=1, inv=1, root=1, rstd=1, rows_a=(self.tiles + 1) // 2, rows_v=self.tiles // 2,
                            turned=self.chunks, out_a=(self.chunks + 1) // 2)

            def __init__(self, tag, rows, width, tiles, gain, shift, dst, tok0, scaled):
                super().__init__(tag)
                self.rows, self.width, self.tiles = rows, width, tiles
                self.gain, self.shift, self.dst, self.tok0, self.scaled = gain, shift, dst, tok0, scaled
                self.chunks = width // P

            def act(self, act):
                junk = region(arena_f - D, D)[:, 0:self.width]
                squares(self, act, [self.rows[:, t, :] for t in range(self.tiles)], junk)
                act.wait_ge(self.s("rstd"), self.at("rstd") + 1)
                for t in range(0, self.tiles, 2):
                    act.activation(self.scaled[:, t, :], self.rows[:, t, :], ACT.Copy, scale=st[:, 3, t:t + 1])\
                        .then_inc(self.s("rows_a"), 1)
                for c in range(0, self.chunks, 2):
                    act.wait_ge(self.s("turned"), self.at("turned") + c + 1)
                    act.activation(self.out(c), bank(c % 8, self.tiles * P), ACT.Identity,
                                   scale=self.gain(c), bias=self.shift(c) if self.shift else 0.0)\
                        .then_inc(self.s("out_a"), 1)

            def out(self, c):
                return self.dst[:, c, self.tok0:self.tok0 + self.tiles * P]

            def dve(self, dve):
                n = self.tiles
                inverse_roots(self, dve, n, self.width)
                for t in range(1, n, 2):
                    dve.tensor_scalar(self.scaled[:, t, :], self.rows[:, t, :], st[:, 3, t:t + 1], None, ALU.mult)\
                        .then_inc(self.s("rows_v"), 1)
                for c in range(1, self.chunks, 2):
                    dve.wait_ge(self.s("turned"), self.at("turned") + c + 1)
                    if self.shift:
                        i = dve.tensor_scalar(self.out(c), bank(c % 8, n * P), self.gain(c), self.shift(c), ALU.mult, ALU.add)
                    else:
                        i = dve.tensor_scalar(self.out(c), bank(c % 8, n * P), self.gain(c), None, ALU.mult)

            def pe(self, pe):
                pe.wait_ge(self.s("rows_a"), self.at("rows_a") + (self.tiles + 1) // 2)
                pe.wait_ge(self.s("rows_v"), self.at("rows_v") + self.tiles // 2)
                for c in range(self.chunks):
                    for t in range(self.tiles):
                        i = pe.transpose(bank(c % 8)[:, t * P:(t + 1) * P], self.scaled[:, t, c * P:(c + 1) * P], ident)
                    i.then_inc(self.s("turned"), 1)

        class Products(Stage):
            kind = "products"

            def totals(self):
                return dict(filled=len(self.jobs), taken_v=self.count["v"], taken_a=self.count["a"], small=self.small)

            small = 0

            def __init__(self, tag):
                super().__init__(tag)
                self.jobs, self.count, self.banks, self.holder = [], {"v": 0, "a": 0}, 0, {}

            def job(self, eng, fill, take, units=(), release=(), n_banks=1, after=(), scratch=False):
                self.count[eng] += 1
                if release:
                    Weights.freed[units[0]] = (self.s("filled"), self.at("filled") + len(self.jobs) + 1)
                bs = [(self.banks + i) % 8 for i in range(n_banks)]
                self.banks += n_banks
                j = dict(eng=eng, fill=fill, take=take, units=units, banks=bs,
                         k=self.count[eng], scratch=scratch, index=len(self.jobs) + 1,
                         after=[*after, *(self.holder[b] for b in bs if b in self.holder)])
                for b in bs:
                    self.holder[b] = j
                self.jobs.append(j)
                return j

            def taken(self, eng, j):
                eng.wait_ge(self.s("taken_" + j["eng"]), self.at("taken_" + j["eng"]) + j["k"])

            def pe(self, pe):
                for j in self.jobs:
                    for a in j["after"]:
                        self.taken(pe, a)
                    for u in j["units"]:
                        Weights.wait(pe, u)
                    i = j["fill"](pe, [bank(b) for b in j["banks"]])
                    i.then_inc(self.s("filled"), 1)

            def drains(self, eng, who):
                for j in self.jobs:
                    if j["eng"] == who:
                        eng.wait_ge(self.s("filled"), self.at("filled") + j["index"])
                        if j["scratch"] and j["k"] > 1:
                            eng.wait_ge(self.s("taken_" + who), self.at("taken_" + who) + j["k"] - 1)
                        j["take"](eng, [bank(b) for b in j["banks"]]).then_inc(self.s("taken_" + who), 1)

            def dve(self, dve):
                self.drains(dve, "v")

            def act(self, act):
                self.drains(act, "a")

        def mm_T(u, at, k, n, cols_, x, tok, ntok):
            def fill(pe, ps):
                w = Weights.view(u, at, k, n)
                for c in range(k):
                    i = pe.matmul(ps[0][0:cols_[1] - cols_[0], 0:ntok], w[:, c, cols_[0]:cols_[1]],
                                  x[:, c, tok:tok + ntok], start=(c == 0), stop=(c == k - 1))
                return i
            return fill

        def mm_R(u, at, k, n, c0, width, x, t):
            def fill(pe, ps):
                w = Weights.view(u, at, k, n)
                for c in range(k):
                    i = pe.matmul(ps[0][:, 0:width], x[:, c, t * P:(t + 1) * P], w[:, c, c0:c0 + width],
                                  start=(c == 0), stop=(c == k - 1))
                return i
            return fill

        def turn(srcs):
            def fill(pe, ps):
                for n, s in enumerate(srcs):
                    w = s.shape[-1]
                    i = pe.transpose(ps[0][0:w, n * P:(n + 1) * P], s, ident)
                return i
            return fill

        def copy_out(side, dst, scale=None):
            def take(eng, ps):
                src = ps[0][:, 0:dst.free_size()]
                if len(dst.shape) == 3:
                    src = src.rearrange("p (a b) -> p a b", a=dst.shape[1])
                if side == "a":
                    return eng.activation(dst, src, ACT.Copy, scale=1.0 if scale is None else scale)
                if scale is None:
                    return eng.tensor_copy(dst, src)
                return eng.tensor_scalar(dst, src, scale, None, ALU.mult)
            return take

        def act_out(dst, func):
            def take(eng, ps):
                return eng.activation(dst, ps[0][:, 0:dst.free_size()], func)
            return take

        def rope_rows(dst, src, cos, sin, heads, pairs, tmp):
            def emit(dve, ps):
                s = src(ps)
                c = cos.unsqueeze(1).broadcast_to([P, heads, pairs])
                n = sin.unsqueeze(1).broadcast_to([P, heads, pairs])
                x1, x2 = s[:, :, :, 0], s[:, :, :, 1]
                dve.tensor_tensor(tmp[0], x1, c, ALU.mult)
                dve.tensor_tensor(tmp[1], x2, n, ALU.mult)
                dve.tensor_tensor(tmp[2], x1, n, ALU.mult)
                dve_step.then(dve, dve.tensor_tensor(tmp[3], x2, c, ALU.mult))
                dve.tensor_tensor(dst[:, :, :, 0], tmp[0], tmp[1], ALU.subtract)
                return dve.tensor_tensor(dst[:, :, :, 1], tmp[2], tmp[3], ALU.add)
            return emit

        class OutProj(Stage):
            kind = "outproj"

            def totals(self):
                return dict(diag=len(self.gates()), spread=len(self.gates()), gate=len(self.gates()), filled=2 * self.tiles,
                            added=2 * self.tiles, summed=0 if self.layer is None else 2 * self.tiles)

            def __init__(self, tag, u, k, x, tiles, layer=None):
                super().__init__(tag)
                self.u, self.k, self.x, self.tiles, self.layer = u, k, x, tiles, layer
                self.gate = region(0, 2, D)
                self.tmp = region(2 * D, 2, BANK)
                self.diag = region(3 * D, KC, P)
                Weights.freed[u] = (self.s("filled"), self.at("filled") + 2 * tiles)

            def gates(self):
                return [] if self.layer is None else [0, 1] if self.tiles > NT else [0]

            def jobs(self):
                return [(t, half) for t in range(self.tiles) for half in range(2)]

            def row(self, t):
                return H[:, t, :] if t < NT else HC[:, t - NT, :]

            def pe(self, pe):
                for g in self.gates():
                    for half in range(2):
                        pe.wait_ge(self.s("diag"), self.at("diag") + g + 1)
                        for c in range(4):
                            i = pe.matmul(bank(6 + half)[:, c * P:(c + 1) * P], ones, self.diag[:, half * 4 + c, :],
                                          start=(c == 0), stop=(c == 3), skip_group_check=True)
                    i.then_inc(self.s("spread"), 1)
                    pe.wait_ge(self.s("gate"), self.at("gate") + g + 1)
                Weights.wait(pe, self.u)
                w = Weights.view(self.u, 0, self.k, D)
                for n, (t, half) in enumerate(self.jobs()):
                    if n >= 4:
                        pe.wait_ge(self.s("added"), self.at("added") + n - 3)
                    for c in range(self.k):
                        i = pe.matmul(bank(n % 4), self.x[:, c, t * P:(t + 1) * P],
                                      w[:, c, half * BANK:(half + 1) * BANK], start=(c == 0), stop=(c == self.k - 1))
                    i.then_inc(self.s("filled"), 1)

            def dve(self, dve):
                for g in self.gates():
                    if g:
                        dve.wait_ge(self.s("gate"), self.at("gate") + g)
                    for c in range(KC):
                        i = dve.tensor_scalar(self.diag[:, c, :], ident, modc[:, self.layer, 16 + c, g:g + 1], None, ALU.mult)
                    i.then_inc(self.s("diag"), 1)
                for n, (t, half) in enumerate(self.jobs()):
                    dve.wait_ge(self.s("filled"), self.at("filled") + n + 1)
                    dst = self.row(t)[:, half * BANK:(half + 1) * BANK]
                    if self.layer is None:
                        dve.tensor_tensor(dst, bank(n % 4), dst, ALU.add).then_inc(self.s("added"), 1)
                        continue
                    if n == 0:
                        dve.wait_ge(self.s("gate"), self.at("gate") + len(self.gates()))
                    if n >= 2:
                        dve.wait_ge(self.s("summed"), self.at("summed") + n - 1)
                    g = self.gate[:, int(t >= NT), half * BANK:(half + 1) * BANK]
                    dve.tensor_tensor(self.tmp[:, n % 2, :], bank(n % 4), g, ALU.mult).then_inc(self.s("added"), 1)

            def pool(self, pool):
                if self.layer is None:
                    return
                for n, (t, half) in enumerate(self.jobs()):
                    dst = self.row(t)[:, half * BANK:(half + 1) * BANK]
                    pool.wait_ge(self.s("added"), self.at("added") + n + 1)
                    pool.tensor_tensor(dst, self.tmp[:, n % 2, :], dst, ALU.add).then_inc(self.s("summed"), 1)

            def act(self, act):
                for g in self.gates():
                    act.wait_ge(self.s("spread"), self.at("spread") + g + 1)
                    act.activation(self.gate[:, g, :], psum[:, 6 * BANK:8 * BANK], ACT.Copy).then_inc(self.s("gate"), 1)

        class Attend(Stage):
            kind = "attend"
            LAG = 3
            table = 0
            nsink = rt[:, 11, 0:8]

            def __init__(self, tag, heads, nq, window, scores, keys, v, out, gate, add=None, sink=False, masks_on_pe=False):
                super().__init__(tag)
                self.heads, self.nq, self.window, self.scores = heads, nq, window, scores
                self.keys, self.v, self.out, self.gate = keys, v, out, gate
                self.add, self.sink, self.masks_on_pe = add, sink, masks_on_pe
                self.units = heads * nq
                self.depth = 4 if all(window(i)[1] <= BANK for i in range(nq)) else 2
                self.P = region(0, 4, 768)
                self.PT = region(3072, 2, 2, 6, P)
                self.first = [0]
                for n in range(self.units):
                    self.first.append(self.first[-1] + (len(keys(self.at_unit(n)[1])) + 3) // 4)

            def totals(self):
                return dict(scored=self.units, max=self.units, exp=self.units, norm=self.units,
                            turned=self.first[-1], pt=self.first[-1], weighed=self.units // 2,
                            out=self.heads // 2, bias0=16 * self.heads * self.table,
                            bias1=16 * self.heads * self.table, banded=self.heads * self.table)

            def at_unit(self, n):
                pair, r = divmod(n, 2 * self.nq)
                return 2 * pair + r % 2, r // 2

            def groups(self, n):
                k = len(self.keys(self.at_unit(n)[1]))
                return [(self.first[n] + g, 4 + g, 4 * g, min(4, k - 4 * g)) for g in range((k + 3) // 4)]

            def steps(self):
                return range(self.units + self.LAG + 3)

            def s_at(self, n, c0, c1):
                at = n % self.depth * (4 * BANK // self.depth)
                return psum[:, at + c0:at + c1]

            def pe(self, pe):
                for n in self.steps():
                    if n < self.units:
                        if n >= self.depth:
                            pe.wait_ge(self.s("exp"), self.at("exp") + n - self.depth + 1)
                        masks = self.add(self.at_unit(n)[1]) if self.add and self.masks_on_pe else []
                        for c0, c1, lhsT, rhs in self.scores(*self.at_unit(n)):
                            here = [a for a in masks if c0 <= a[0] < c1]
                            i = pe.matmul(self.s_at(n, c0, c1), lhsT, rhs, start=True, stop=True)
                            for m0, m1, mask in here:
                                i = pe.matmul(self.s_at(n, m0, m1), ident, mask, start=False, stop=True,
                                              skip_group_check=True)
                        i.then_inc(self.s("scored"), 1)
                    u = n - self.LAG
                    if 0 <= u < self.units:
                        self.turn(pe, u)
                    if u >= 2 and u % 2 == 0 and u <= self.units:
                        self.weigh(pe, u // 2 - 1)

            def turn(self, pe, u):
                pe.wait_ge(self.s("norm"), self.at("norm") + u + 1)
                for item, b, k0, k in self.groups(u):
                    earlier = [g[0] for w in (u - 1, u - 2) if w >= 0 for g in self.groups(w) if g[1] == b]
                    if earlier:
                        pe.wait_ge(self.s("pt"), self.at("pt") + earlier[0] + 1)
                    for j in range(k):
                        i = pe.transpose(bank(b)[:, j * P:(j + 1) * P], self.P[:, u % 4, (k0 + j) * P:(k0 + j + 1) * P], ident)
                    i.then_inc(self.s("turned"), 1)

            def weigh(self, pe, m):
                h, i = self.at_unit(2 * m)
                keys, pair = self.keys(i), h // 2
                pe.wait_ge(self.s("pt"), self.at("pt") + self.first[2 * m + 2])
                if i == 0 and pair >= 2:
                    pe.wait_ge(self.s("out"), self.at("out") + pair - 1)
                for n, kt in enumerate(keys):
                    for hh in range(2):
                        ins = pe.matmul(psum[hh * DH:(hh + 1) * DH, (6 + pair % 2) * BANK + i * P:(6 + pair % 2) * BANK + (i + 1) * P],
                                        self.v(h + hh, kt), self.PT[:, m % 2, hh, n, :], start=(n == 0), stop=(n == len(keys) - 1))
                ins.then_inc(self.s("weighed"), 1)

            def act(self, act):
                for n in self.steps():
                    u = n - self.LAG
                    if 0 <= u < self.units:
                        m = u // 2
                        if m >= 2:
                            act.wait_ge(self.s("weighed"), self.at("weighed") + m - 1)
                        for item, b, k0, k in self.groups(u):
                            act.wait_ge(self.s("turned"), self.at("turned") + item + 1)
                            act.activation(self.PT[:, m % 2, u % 2, k0:k0 + k, :],
                                           bank(b)[:, 0:k * P].rearrange("p (k q) -> p k q", k=k), ACT.Copy)\
                                .then_inc(self.s("pt"), 1)
                    if n < self.units:
                        h, i = self.at_unit(n)
                        self.before_exp(act, n)
                        act.wait_ge(self.s("max"), self.at("max") + n + 1)
                        if n >= 4:
                            act.wait_ge(self.s("turned"), self.at("turned") + self.first[n - 3])
                        lo, hi = self.window(i)
                        if self.sink:
                            act.activation(sm[:, 3, n:n + 1], sinkb[:, h:h + 1], ACT.Exp, bias=sm[:, 0, n:n + 1])
                        act.activation(self.P[:, n % 4, 0:hi - lo], self.s_at(n, lo, hi), ACT.Exp,
                                       bias=sm[:, 0, n:n + 1], accum_out=sm[:, 1, n:n + 1]).then_inc(self.s("exp"), 1)

            def before_exp(self, act, n):
                pass

            def maximum(self, dve, n):
                h, i = self.at_unit(n)
                adds = self.add(i) if self.add and not self.masks_on_pe else []
                for c0, c1, a in adds:
                    ins = dve.tensor_tensor(self.s_at(n, c0, c1), self.s_at(n, c0, c1), a, ALU.add)
                if adds:
                    dve_step.then(dve, ins)
                ins = dve.tensor_reduce(sm[:, 0, n:n + 1], self.s_at(n, *self.window(i)), AXX, ALU.max, negate=True)
                if self.sink:
                    dve_step.then(dve, ins)
                    ins = dve.tensor_tensor(sm[:, 0, n:n + 1], sm[:, 0, n:n + 1], self.nsink[:, h:h + 1], ALU.min)
                return ins

            def dve(self, dve):
                for n in self.steps():
                    if n < self.units:
                        dve.wait_ge(self.s("scored"), self.at("scored") + n + 1)
                        self.maximum(dve, n).then_inc(self.s("max"), 1)
                    if 1 <= n <= self.units:
                        self.normalise(dve, n - 1)
                    u = n - self.LAG - 1
                    if u >= 0 and u % (2 * self.nq) == 0 and 0 < u <= self.units:
                        pair = u // (2 * self.nq) - 1
                        dve.wait_ge(self.s("weighed"), self.at("weighed") + (pair + 1) * self.nq)
                        dve.tensor_tensor(self.out(pair), bank(6 + pair % 2)[:, 0:self.nq * P], self.gate(pair), ALU.mult)\
                            .then_inc(self.s("out"), 1)

            def normalise(self, dve, n):
                lo, hi = self.window(self.at_unit(n)[1])
                dve.wait_ge(self.s("exp"), self.at("exp") + n + 1)
                rs = sm[:, 1, n:n + 1]
                if self.sink:
                    dve_step.then(dve, dve.tensor_tensor(rs, rs, sm[:, 3, n:n + 1], ALU.add))
                dve_step.then(dve, dve.reciprocal(sm[:, 2, n:n + 1], rs))
                p = self.P[:, n % 4, 0:hi - lo]
                dve.tensor_scalar(p, p, sm[:, 2, n:n + 1], None, ALU.mult).then_inc(self.s("norm"), 1)

        class RowNorm(Stage):
            kind = "rownorm"

            def totals(self):
                return dict(squares=1, inv=1, root=1, rstd=1, gain=16, made=NT)

            def __init__(self, tag, gain, out=None):
                super().__init__(tag)
                self.gain, self.out_ = gain, out
                self.g = region(0, D)
                self.y = region(1024, NT, D)

            def act(self, act):
                act.dma_start(self.g, self.gain.partition_broadcast(P)).then_inc(self.s("gain"), 16)
                squares(self, act, [H[:, t, :] for t in range(NT)], region(8192, D))
                if self.out_ is not None:
                    for t in range(NT):
                        act.wait_ge(self.s("made"), self.at("made") + t + 1)
                        act.dma_start(self.out_[0, t * P:(t + 1) * P, :], self.y[:, t, :]).then_inc(self.s("stored"), 16)
                    act.wait_ge(self.s("stored"), self.at("stored") + 16 * NT)

            def dve(self, dve):
                inverse_roots(self, dve, NT, D)
                dve.wait_ge(self.s("gain"), self.at("gain") + 16)
                for t in range(NT):
                    dst = H[:, t, :] if self.out_ is None else self.y[:, t, :]
                    dve.scalar_tensor_tensor(dst, H[:, t, :], st[:, 3, t:t + 1], self.g, ALU.mult, ALU.mult)\
                        .then_inc(self.s("made"), 1)

        def slot_view(i):
            return rt[:, i, :].rearrange("p (t e) -> p t e", t=NT)

        class Route(Stage):

            def __init__(self, tag, layer, rows):
                super().__init__(tag)
                self.l, self.rows = layer, rows

            def load(self, pool):
                pool.dma_start(wr[:, :, 0:N_GROUPS], io["router_group_w"][self.l].rearrange("(c p) g -> p c g", p=P))\
                    .then_inc(self.s("loaded"), 16)
                pool.dma_start(wr[:, :, N_GROUPS:NR], io["router_expert_w"][self.l].rearrange("(c p) g -> p c g", p=P))\
                    .then_inc(self.s("loaded"), 16)
                pool.dma_start(rbias[:, 0:N_GROUPS], io["router_group_b"][self.l].partition_broadcast(P)).then_inc(self.s("loaded"), 16)
                pool.dma_start(rbias[:, N_GROUPS:NR], io["router_expert_b"][self.l].partition_broadcast(P)).then_inc(self.s("loaded"), 16)

            def act(self, act):
                act.wait_ge(self.s("tops"), 1)
                for t in range(NT):
                    act.activation(top8[:, 3, t, :], top8[:, 0, t, :], ACT.Exp, bias=rt[:, 9, 8 + t:9 + t],
                                   accum_out=rt[:, 9, 16 + t:17 + t])
                act.activation(rt[:, 9, 20:24], rt[:, 9, 12:16], ACT.Exp).then_inc(self.s("exps"), 1)

            def pe(self, pe):
                pe.wait_ge(self.s("loaded"), 64)
                for t in range(NT):
                    for c in range(KC):
                        i = pe.matmul(bank(t, NR), XT[:, c, t * P:(t + 1) * P], wr[:, c, :], start=(c == 0), stop=(c == KC - 1))
                i.then_inc(self.s("logits"), 1)
                pe.wait_ge(self.s("mask"), 1)
                M = slot_view(4)
                for t in range(NT):
                    for u in range(t + 1):
                        lhs = ones if u < t else cst[:, C_BEFORE:C_BEFORE + P]
                        pe.matmul(bank(t, NE), lhs, M[:, u, :], start=(u == 0), stop=(u == t))
                for u in range(NT):
                    i = pe.matmul(bank(4, NE), ones, M[:, u, :], start=(u == 0), stop=(u == NT - 1))
                i.then_inc(self.s("ranked"), 1)

            def dve(self, dve):
                def step(i):
                    dve_step.then(dve, i)
                G, EL, MSK, DEST, TMP, OV = top8[:, 0], slot_view(0), slot_view(1), slot_view(5), slot_view(6), slot_view(7)
                A = [slot_view(2), slot_view(3)]
                gif, nmax, diff, gsum, e2 = (rt[:, 9, a:a + 4] for a in (0, 8, 12, 16, 20))
                eif = rt[:, 9, 24:32].rearrange("p (k t) -> p k t", k=2)
                pen = rt[:, 10, 0:16].rearrange("p (t g) -> p t g", t=NT)
                iota = cst[:, C_IOTA:C_IOTA + NE]
                if self.l == 0:
                    blocks_cleared(dve)
                dve.wait_ge(self.s("loaded"), 64)
                dve.wait_ge(self.s("logits"), 1)
                for t in range(NT):
                    dve.tensor_tensor(G[:, t, 0:N_GROUPS], bank(t)[:, 0:N_GROUPS], rbias[:, 0:N_GROUPS], ALU.add)
                    i = dve.tensor_tensor(EL[:, t, :], bank(t)[:, N_GROUPS:NR], rbias[:, N_GROUPS:NR], ALU.add)
                step(i)
                for t in range(NT):
                    i = dve.max(top8[:, 1, t, :], G[:, t, :])
                step(i)
                for t in range(NT):
                    i = dve.max_index(top8i[:, 0, t, :], top8[:, 1, t, :], G[:, t, :])
                step(i)
                step(dve.tensor_copy(gif, top8i[:, 0, :, 0]))
                for t in range(NT):
                    i = dve.tensor_scalar(pen[:, t, :], iota[:, 0:N_GROUPS], gif[:, t:t + 1], None, ALU.is_equal)
                step(i)
                step(dve.tensor_scalar(rt[:, 10, 0:16], rt[:, 10, 0:16], -NEG, NEG, ALU.mult, ALU.add))
                step(dve.tensor_tensor(rt[:, 1, :].rearrange("p (a e) -> p a e", e=PER_GROUP),
                                       rt[:, 0, :].rearrange("p (a e) -> p a e", e=PER_GROUP),
                                       rt[:, 10, 0:16].unsqueeze(2).broadcast_to([P, 16, PER_GROUP]), ALU.add))
                for t in range(NT):
                    i = dve.max(top8[:, 2, t, :], MSK[:, t, :])
                step(i)
                dve.tensor_scalar(nmax, top8[:, 1, :, 0], -1.0, None, ALU.mult)
                dve.tensor_tensor(diff, top8[:, 2, :, 1], top8[:, 2, :, 0], ALU.subtract).then_inc(self.s("tops"), 1)
                for t in range(NT):
                    i = dve.max_index(top8i[:, 1, t, :], top8[:, 2, t, :], MSK[:, t, :])
                step(i)
                for k in range(2):
                    i = dve.tensor_copy(eif[:, k, :], top8i[:, 1, :, k])
                step(i)
                for k in range(2):
                    for t in range(NT):
                        i = dve.tensor_scalar(A[k][:, t, :], iota, eif[:, k, t:t + 1], None, ALU.is_equal)
                step(i)
                dve.tensor_tensor(rt[:, 4, :], rt[:, 2, :], rt[:, 3, :], ALU.add).then_inc(self.s("mask"), 1)
                dve.wait_ge(self.s("exps"), 1)
                step(dve.scalar_tensor_tensor(gates[:, 0, :], e2, 1.0, gsum, ALU.add, ALU.mult))
                step(dve.reciprocal(gates[:, 0, :], gates[:, 0, :]))
                dve.tensor_tensor(gates[:, 1, :], gates[:, 0, :], e2, ALU.mult)
                dve.wait_ge(self.s("ranked"), 1)
                cnt, nov, incl, ob = (rt[:, 8, 32 * a:32 * a + 32] for a in range(4))
                step(dve.tensor_copy(cnt, bank(4)[:, 0:NE]))
                step(dve.tensor_scalar(nov, cnt, float(BR), None, ALU.is_gt))
                for m in range(2, SEQ // BR):
                    step(dve.scalar_tensor_tensor(nov, cnt, float(m * BR), nov, ALU.is_gt, ALU.add))
                step(dve.tensor_tensor_scan(incl, ones[:, 0:NE], nov, 0.0, ALU.mult, ALU.add))
                step(dve.tensor_tensor(ob, incl, nov, ALU.subtract))
                dlt = rt[:, 10, 32:64]
                step(dve.tensor_scalar(dlt, ob, float(NE - 1), float(BR), ALU.add, ALU.mult))
                step(dve.tensor_tensor(dlt, dlt, cst[:, C_BASE:C_BASE + NE], ALU.subtract))
                for t in range(NT):
                    i = dve.tensor_copy(TMP[:, t, :], bank(t)[:, 0:NE])
                step(i)
                step(dve.tensor_scalar(rt[:, 7, :], rt[:, 6, :], float(BR), None, ALU.is_ge))
                step(dve.tensor_tensor(OV, OV, dlt.unsqueeze(1).broadcast_to([P, NT, NE]), ALU.mult))
                step(dve.tensor_tensor(OV, OV, TMP, ALU.add))
                step(dve.tensor_tensor(DEST, OV, cst[:, C_BASE:C_BASE + NE].unsqueeze(1).broadcast_to([P, NT, NE]), ALU.add))
                for k in range(2):
                    step(dve.tensor_tensor(TMP, A[k], DEST, ALU.mult))
                    step(dve.tensor_reduce(rt[:, 10, 64 + 4 * k:68 + 4 * k], TMP, AXX, ALU.add))
                    i = dve.tensor_copy(didx[:, k, :], rt[:, 10, 64 + 4 * k:68 + 4 * k])
                i.then_inc(self.s("dest"), 1)
                big = [region(8192 + 512 * a, EXTRA, NE)[0:1] for a in range(2)]
                jb = cst[0:1, C_IOTA:C_IOTA + EXTRA].unsqueeze(2).broadcast_to([1, EXTRA, NE])
                over_j = lambda x: x[0:1].unsqueeze(1).broadcast_to([1, EXTRA, NE])
                dve.tensor_tensor(big[0], over_j(ob), jb, ALU.is_le)
                step(dve.tensor_tensor(big[1], over_j(incl), jb, ALU.is_gt))
                step(dve.tensor_tensor(big[0], big[0], big[1], ALU.mult))
                step(dve.tensor_tensor(big[0], big[0], over_j(iota), ALU.mult))
                step(dve.tensor_reduce(rt[0:1, 10, 80:80 + EXTRA], big[0], AXX, ALU.add))
                dve.tensor_copy(ovn[0:1, 1:1 + EXTRA], rt[0:1, 10, 80:80 + EXTRA])
                dve.tensor_copy(ovn[0:1, 0:1], incl[0:1, NE - 1:NE]).then_inc(self.s("extra"), 1)

            def pool(self, pool):
                if self.l == 0:
                    blocks_cleared(pool)
                pool.wait_ge(self.s("dest"), 1)
                for t in range(NT):
                    for k in range(2):
                        pool.indirect_dma_start(xg_dram, bass.IndirectOffsetOnAxis(ap=didx[:, k, t:t + 1], axis=0),
                                                self.rows[:, t, :], None).then_inc(self.s("scattered"), 16)
                pool.wait_ge(self.s("scattered"), 16 * 2 * NT)

        def is_at(e, n):
            return isinstance(e, int) and e == n

        class Experts(Stage):

            def __init__(self, tag, layer):
                super().__init__(tag)
                self.l = layer
                self.base, self.per = len(Weights.units), list(Weights.per)
                for v in range(3 * NE):
                    Weights.add((0, 0, 0, None))
                end = self.base + 3 * NE
                Weights.freed[end - 3] = (self.s("upped"), NE)
                Weights.freed[end - 2] = (self.s("downed"), NE - 1)
                Weights.freed[end - 1] = (self.s("downed"), NE)
                self.XG, self.XGT = region(0, D), region(1024, KC, BR)
                self.SA, self.HR = region(2048, FF)[P - BR:P], region(2560, FF)
                self.HT, self.Y = region(3072, 4, BR), region(4096, BANK)
                self.gu = io["expert_w_gu"][layer].rearrange("e (k p) n -> e p k n", p=P)
                self.dn = io["expert_w_down"][layer].rearrange("e (k p) n -> e p k n", p=P)
                self.xgb = xg_dram.rearrange("(b p) d -> b p d", p=BR)
                self.yb = y_dram.rearrange("(b p) (h n) -> b h p n", p=BR, h=2)

            def slot(self, v):
                return (self.base + v) % RING

            def unit_gu(self, e, half, first):
                s = self.slot(half if first else 2 + half)
                return s, self.per[s] + 16 * (1 if first else e + half)

            def unit_dn(self, e, last):
                s = self.slot(3 * NE - 1 if last else 4)
                return s, self.per[s] + 16 * (NE if last else e + 2)

            def loop(self, eng, body):
                body(0)
                body(1)
                with eng.Fori(2, NE - 2) as e:
                    body(e)
                body(NE - 2)
                body(NE - 1)

            def sp(self, sp):
                def load(slot, k, n, src):
                    sp.dma_start(ring[:, slot, :].rearrange("p (k n) -> p k n", k=k), src).then_inc(w_ready[slot], 16)

                def gu(e, half):
                    load(self.unit_gu(e, half, is_at(e, 0))[0], 4, 2 * FF, self.gu[e, :, 4 * half:4 * half + 4, :])

                def body(e):
                    if is_at(e, 0):
                        for half in range(2):
                            sp.wait_ge(*Weights.freed[self.base - RING + half])
                            gu(e, half)
                        return
                    if is_at(e, 1):
                        sp.wait_ge(*Weights.freed[self.base - 1])
                        gu(e, 0)
                        sp.wait_ge(self.s("gated"), 1)
                        gu(e, 1)
                        sp.wait_ge(self.s("upped"), 1)
                    else:
                        sp.wait_ge(self.s("gated"), e)
                        gu(e, 0)
                        sp.wait_ge(self.s("upped"), e)
                        gu(e, 1)
                        sp.wait_ge(self.s("downed"), e - 1)
                    load(self.unit_dn(e - 1, False)[0], 4, D, self.dn[e - 1])
                    if is_at(e, NE - 1):
                        sp.wait_ge(self.s("gated"), NE)
                        load(self.unit_dn(e, True)[0], 4, D, self.dn[e])
                self.loop(sp, body)
                sp.wait_ge(self.s("open"), 1)
                n = sp.value_load(ovn[0:1, 0:1], min_val=0, max_val=EXTRA)
                with sp.If(n > 0):
                    for j in range(EXTRA):
                        with sp.If(n > j):
                            if j == 0:
                                sp.wait_ge(self.s("downed"), NE)
                            e = sp.value_load(ovn[0:1, 1 + j:2 + j], min_val=0, max_val=NE - 1)
                            for half in range(2):
                                sp.dma_start(ring[:, half, :].rearrange("p (k n) -> p k n", k=4),
                                             self.gu[e, :, 4 * half:4 * half + 4, :]).then_inc(self.s("x_weights"), 16)
                            sp.dma_start(ring[:, 2, :].rearrange("p (k n) -> p k n", k=4), self.dn[e]).then_inc(self.s("x_weights"), 16)
                            sp.wait_ge(self.s("x_down"), j + 1)

            def turn_x(self, pe):
                for c in range(KC):
                    i = pe.transpose(psum[:, 2 * BANK + c * P:2 * BANK + (c + 1) * P], self.XG[:, c * P:(c + 1) * P], ident)
                return i

            def up(self, pe, slot, part):
                w = ring[:, slot, :].rearrange("p (k n) -> p k n", k=4)
                for c in range(4):
                    for side in range(2):
                        i = pe.matmul(psum[side * BR:(side + 1) * BR, 0:FF], self.XGT[:, 4 * part + c, :],
                                      w[:, c, side * FF:(side + 1) * FF], start=(part == 0 and c == 0), stop=(part == 1 and c == 3))
                return i

            def turn_h(self, pe):
                for c in range(4):
                    i = pe.transpose(bank(4)[:, c * P:(c + 1) * P], self.HR[:, c * P:(c + 1) * P], ident)
                return i

            def down(self, pe, slot):
                w = ring[:, slot, :].rearrange("p (k n) -> p k n", k=4)
                for c in range(4):
                    for half in range(2):
                        i = pe.matmul(psum[half * BR:(half + 1) * BR, 5 * BANK:6 * BANK], self.HT[:, c, :],
                                      w[:, c, half * BANK:(half + 1) * BANK], start=(c == 0), stop=(c == 3))
                return i

            def pe(self, pe):
                def down(e, last):
                    s, ready = self.unit_dn(e, last)
                    pe.wait_ge(w_ready[s], ready)
                    pe.wait_ge(self.s("ht"), e + 1)
                    if not is_at(e, 0):
                        pe.wait_ge(self.s("y"), e)
                    self.down(pe, s).then_inc(self.s("downed"), 1)

                def body(e):
                    first, last = is_at(e, 0), is_at(e, NE - 1)
                    if first:
                        pe.wait_ge(self.s("padded"), 2)
                        pe.wait_ge(self.s("rows"), 16)
                        self.turn_x(pe).then_inc(self.s("turned"), 1)
                    pe.wait_ge(self.s("xt"), e + 1)
                    for half in range(2):
                        s, ready = self.unit_gu(e, half, first)
                        pe.wait_ge(w_ready[s], ready)
                        self.up(pe, s, half).then_inc(self.s(("gated", "upped")[half]), 1)
                    if not last:
                        pe.wait_ge(self.s("rows"), 16 * (e + 2))
                        self.turn_x(pe).then_inc(self.s("turned"), 1)
                    if not first:
                        down(e - 1, False)
                    pe.wait_ge(self.s("h"), e + 1)
                    self.turn_h(pe).then_inc(self.s("h_turned"), 1)
                    if last:
                        down(e, True)
                self.loop(pe, body)
                n = pe.value_load(ovn[0:1, 0:1], min_val=0, max_val=EXTRA)
                with pe.If(n > 0):
                    for j in range(EXTRA):
                        with pe.If(n > j):
                            pe.wait_ge(self.s("x_rows"), 16 * (j + 1))
                            self.turn_x(pe).then_inc(self.s("x_turned"), 1)
                            pe.wait_ge(self.s("x_xt"), j + 1)
                            pe.wait_ge(self.s("x_weights"), 48 * (j + 1))
                            self.up(pe, 0, 0)
                            self.up(pe, 1, 1).then_inc(self.s("x_upped"), 1)
                            pe.wait_ge(self.s("x_h"), j + 1)
                            self.turn_h(pe).then_inc(self.s("x_h_turned"), 1)
                            pe.wait_ge(self.s("x_ht"), j + 1)
                            self.down(pe, 2).then_inc(self.s("x_down"), 1)

            def gain(self):
                g = cols[:, V_FFN + KC * self.l:V_FFN + KC * (self.l + 1)]
                return g.unsqueeze(2).broadcast_to([P, KC, BR])

            def take_x(self, dve):
                return dve.tensor_tensor(self.XGT, psum[:, 2 * BANK:4 * BANK].rearrange("p (c t) -> p c t", c=KC)[:, :, 0:BR],
                                         self.gain(), ALU.mult)

            def take_ht(self, dve):
                return dve.tensor_copy(self.HT, bank(4).rearrange("p (c t) -> p c t", c=4)[:, :, 0:BR])

            def hidden(self, dve):
                return dve.tensor_tensor(self.HR[0:BR], self.SA, psum[P - BR:P, 0:FF], ALU.mult)

            def silu(self, act):
                return act.activation(self.SA, psum[0:BR, 0:FF], ACT.Silu)

            def store(self, act, b, done):
                for half in range(2):
                    act.dma_start(self.yb[b, half], self.Y[half * BR:(half + 1) * BR, :]).then_inc(done, 16)

            def dve(self, dve):
                def body(e):
                    first, last = is_at(e, 0), is_at(e, NE - 1)
                    if first:
                        dve.wait_ge(self.s("turned"), 1)
                        self.take_x(dve).then_inc(self.s("xt"), 1)
                    dve.wait_ge(self.s("silu"), e + 1)
                    self.hidden(dve).then_inc(self.s("h"), 1)
                    if not last:
                        dve.wait_ge(self.s("turned"), e + 2)
                        self.take_x(dve).then_inc(self.s("xt"), 1)
                    dve.wait_ge(self.s("h_turned"), e + 1)
                    self.take_ht(dve).then_inc(self.s("ht"), 1)
                self.loop(dve, body)
                n = dve.value_load(ovn[0:1, 0:1], min_val=0, max_val=EXTRA)
                with dve.If(n > 0):
                    for j in range(EXTRA):
                        with dve.If(n > j):
                            dve.wait_ge(self.s("x_turned"), j + 1)
                            self.take_x(dve).then_inc(self.s("x_xt"), 1)
                            dve.wait_ge(self.s("x_silu"), j + 1)
                            self.hidden(dve).then_inc(self.s("x_h"), 1)
                            dve.wait_ge(self.s("x_h_turned"), j + 1)
                            self.take_ht(dve).then_inc(self.s("x_ht"), 1)

            def act(self, act):
                def result(e):
                    act.wait_ge(self.s("downed"), e + 1)
                    if not is_at(e, 0):
                        act.wait_ge(self.s("stored"), 32 * e)
                    act.activation(self.Y, bank(5), ACT.Copy).then_inc(self.s("y"), 1)
                    act.wait_ge(self.s("y"), e + 1)
                    self.store(act, e, self.s("stored"))

                def body(e):
                    first, last = is_at(e, 0), is_at(e, NE - 1)
                    if first:
                        act.dma_start(self.XG[0:BR], self.xgb[0]).then_inc(self.s("rows"), 16)
                        act.wait_ge(self.s("turned"), 1)
                        act.dma_start(self.XG[0:BR], self.xgb[1]).then_inc(self.s("rows"), 16)
                    act.wait_ge(self.s("upped"), e + 1)
                    self.silu(act).then_inc(self.s("silu"), 1)
                    if not last and not is_at(e, NE - 2):
                        act.wait_ge(self.s("turned"), e + 2)
                        act.dma_start(self.XG[0:BR], self.xgb[e + 2]).then_inc(self.s("rows"), 16)
                    if not first:
                        result(e - 1)
                    if last:
                        result(e)
                self.loop(act, body)
                act.wait_ge(self.s("stored"), 32 * NE)
                n = act.value_load(ovn[0:1, 0:1], min_val=0, max_val=EXTRA)
                with act.If(n > 0):
                    for j in range(EXTRA):
                        with act.If(n > j):
                            act.dma_start(self.XG[0:BR], self.xgb[NE + j]).then_inc(self.s("x_rows"), 16)
                            act.wait_ge(self.s("x_upped"), j + 1)
                            self.silu(act).then_inc(self.s("x_silu"), 1)
                            act.wait_ge(self.s("x_down"), j + 1)
                            act.activation(self.Y, bank(5), ACT.Copy).then_inc(self.s("x_y"), 1)
                            act.wait_ge(self.s("x_y"), j + 1)
                            self.store(act, NE + j, self.s("x_stored"))
                            act.wait_ge(self.s("x_stored"), 32 * (j + 1))

            def pool(self, pool):
                pool.memset(self.XG[BR:P], 0.0).then_inc(self.s("padded"), 1)
                pool.memset(self.HR[BR:P], 0.0).then_inc(self.s("padded"), 1)
                pool.nop().then_inc(self.s("open"), 1)

        class Combine(Stage):
            YG = region(0, 2, NT, D)

            def sp(self, sp):
                for t in range(NT):
                    sp.wait_ge(self.s(f"got{t}"), 32)

            def pool(self, pool):
                for t in range(NT):
                    for k in range(2):
                        pool.indirect_dma_start(self.YG[:, k, t, :], None, y_dram,
                                                bass.IndirectOffsetOnAxis(ap=didx[:, k, t:t + 1], axis=0))\
                            .then_inc(self.s(f"got{t}"), 16)

            def dve(self, dve):
                for t in range(NT):
                    dve.wait_ge(self.s(f"got{t}"), 32)
                    for k in range(2):
                        dve_step.then(dve, dve.scalar_tensor_tensor(H[:, t, :], self.YG[:, k, t, :], gates[:, k, t:t + 1],
                                                                    H[:, t, :], ALU.mult, ALU.add))

        class FoxDecay(Stage):

            def __init__(self, tag, z, c, nc_, tmp, QT, KT, half):
                super().__init__(tag)
                self.z, self.c, self.nc_, self.tmp, self.QT, self.KT, self.half = z, c, nc_, tmp, QT, KT, half

            def sp(self, sp):
                if not self.half:
                    clear_blocks(sp)

            def dve(self, dve):
                dve.memset(self.QT[64:66, :, :], 1.0)
                dve.memset(self.KT[64:66, :, :], 1.0).then_inc(self.s("ones"), 1)
                if self.half:
                    return
                z, c, tmp = self.z[0:FOX_H], self.c[0:FOX_H], self.tmp[0:FOX_H]
                dve.scalar_tensor_tensor(tmp, z, -1.0, z, ALU.mult, ALU.max).then_inc(self.s("abs"), 1)
                dve.wait_ge(self.s("log"), 2)
                dve_step.then(dve, dve.scalar_tensor_tensor(tmp, z, 0.0, tmp, ALU.min, ALU.subtract))
                dve_step.then(dve, dve.memset(z, 1.0))
                dve_step.then(dve, dve.tensor_tensor_scan(c, z, tmp, 0.0, ALU.mult, ALU.add))
                dve.tensor_scalar(self.nc_[0:FOX_H], c, -1.0, None, ALU.mult).then_inc(self.s("cum"), 1)

            def act(self, act):
                if not self.half:
                    tmp = self.tmp[0:FOX_H]
                    act.wait_ge(self.s("abs"), 1)
                    act.activation(tmp, tmp, ACT.Exp, scale=-1.0).then_inc(self.s("log"), 1)
                    act.wait_ge(self.s("log"), 1)
                    act.activation(tmp, tmp, ACT.Ln, bias=1.0).then_inc(self.s("log"), 1)
                    act.wait_ge(self.s("cum"), 1)
                act.wait_ge(self.s("ones"), 1)
                for h in range(8):
                    g = 8 * self.half + h
                    act.dma_start(self.QT[64:65, h, :], self.c[g:g + 1, :]).then_inc(self.s("laid"), 16)
                    act.dma_start(self.KT[65:66, h, :], self.nc_[g:g + 1, :]).then_inc(self.s("laid"), 16)
                act.wait_ge(self.s("laid"), 16 * 16)

        def use_units(stage, *us):
            def sp(eng):
                for u in us:
                    Weights.load(eng, u)
            stage.sp = sp

        def loads(stage, *pairs):
            def pool(eng):
                for dst, src in pairs:
                    eng.dma_start(dst, src).then_inc(stage.s("small"), 16)
                eng.wait_ge(stage.s("small"), stage.at("small") + 16 * len(pairs))
            stage.pool = pool
            stage.small = 16 * len(pairs)

        def zeros(stage, *parts):
            def pool(eng):
                for x in parts:
                    eng.memset(x, 0.0)
            stage.pool = pool

        def gain_cols(at):
            return lambda c: cols[:, at + c:at + c + 1]

        def fox():
            QT, KT = region(12288, 8, SEQ), region(16384, 8, SEQ)
            V, GT = region(20480, NT, 512), region(22528, 4, SEQ)
            c, nc_, z, tmp = (region(24576 + 512 * i, SEQ) for i in range(4))
            bf = rt[:, 11, 16:17]
            Norm("n0", H, D, NT, gain_cols(V_MIX), None, XT, 0, region(0, NT, D))
            w = io["fox_w_in"][0]
            for g in range(2):
                p = Products(f"fox{g}")
                us = [Weights.add((0, KC, 512, w[:, D * i + 512 * g:D * i + 512 * (g + 1)])) for i in range(4)]
                use_units(p, *us)
                if g == 0:
                    loads(p, (wr[:, :, 0:FOX_H], w[:, 4 * D:4 * D + FOX_H].rearrange("(c p) g -> p c g", p=P)),
                          (bf[0:FOX_H], io["fox_b_f"][0].unsqueeze(1)))
                for i, (dst, scale) in enumerate(((QT, DH ** -0.5), (KT, 1.0))):
                    for n in range(4):
                        def take(eng, ps, dst=dst, n=n, scale=scale):
                            if n % 2:
                                eng.activation(dst[0:64, 2 * n, :], ps[0][0:64, :], ACT.Copy, scale=scale)
                                return eng.activation(dst[0:64, 2 * n + 1, :], ps[0][64:128, :], ACT.Copy, scale=scale)
                            eng.tensor_scalar(dst[0:64, 2 * n, :], ps[0][0:64, :], scale, None, ALU.mult)
                            return eng.tensor_scalar(dst[0:64, 2 * n + 1, :], ps[0][64:128, :], scale, None, ALU.mult)
                        p.job("va"[n % 2], mm_T(us[i], 0, KC, 512, (n * P, n * P + P), XT, 0, SEQ), take,
                              units=(us[i],), release=(1,) if n == 3 else ())
                for t in range(NT):
                    s = "va"[t % 2]
                    p.job(s, mm_R(us[2], 0, KC, 512, 0, 512, XT, t), copy_out(s, V[:, t, :]), units=(us[2],),
                          release=(1,) if t == 3 else ())
                for n in range(4):
                    p.job("a", mm_T(us[3], 0, KC, 512, (n * P, n * P + P), XT, 0, SEQ), act_out(GT[:, n, :], ACT.Sigmoid),
                          units=(us[3],), release=(1,) if n == 3 else ())
                if g == 0:
                    def fill(pe, ps, p=p):
                        pe.wait_ge(p.s("small"), p.at("small") + 32)
                        for k in range(KC):
                            i = pe.matmul(ps[0][0:FOX_H, :], wr[:, k, 0:FOX_H], XT[:, k, 0:SEQ], start=(k == 0), stop=(k == KC - 1))
                        return i
                    p.job("v", fill, lambda eng, ps: eng.tensor_scalar(z[0:FOX_H], ps[0][0:FOX_H, :], bf[0:FOX_H], None, ALU.add))
                FoxDecay(f"dec{g}", z, c, nc_, tmp, QT, KT, g)
                causal = cst[:, C_CAUSAL:C_CAUSAL + P]
                Attend(f"fa{g}", 8, NT, lambda i: (0, (i + 1) * P),
                       lambda h, i: [(0, (i + 1) * P, QT[0:66, h, i * P:(i + 1) * P], KT[0:66, h, 0:(i + 1) * P])],
                       lambda i: range(i + 1),
                       lambda h, kt: V[:, kt, h * DH:(h + 1) * DH], lambda q: GT[:, q, :], lambda q: GT[:, q, :],
                       add=lambda i: [(i * P, (i + 1) * P, causal)], masks_on_pe=True)
                u = Weights.add((0, 4, D, io["fox_w_out"][0][512 * g:512 * (g + 1), :]))
                use_units(OutProj(f"fo{g}", u, 4, GT, NT), u)

        def moe(layer):
            rows = region(0, NT, D)
            norm = Norm(f"nf{layer}", H, D, NT, gain_cols(V_FFN + KC * layer), None, XT, 0, rows)
            norm.pool = Route(f"rt{layer}", layer, rows).load
            Experts(f"ex{layer}", layer)
            Combine(f"cb{layer}")

        R_ROT, R_DEC = region(20480, 2, SEQ), region(21504, RET_H, SEQ)
        R_Q, R_K, R_V, R_G = region(3072, 2, SEQ), region(4096, 2, SEQ), region(5120, NT, RET_DV), region(7168, NT, RET_DV)
        R_ST, R_Y, R_YT = region(9216, NT, SEQ), region(11264, NT, RET_DV), region(13312, 4, SEQ)
        R_TMP = region(15360, 2, 4, SEQ)
        R_BN, R_MV = region(24000, NT, 6), region(24064, NT, 2)

        class Retain(Stage):
            kind = "retain"

            def totals(self):
                return dict(scored=NT, decayed=NT, weighed=NT, squares=1, inv=1, root=1, rstd=1, normed=NT, gated=NT, turned=4)

            def __init__(self, tag, h):
                super().__init__(tag)
                self.h = h

            def pe(self, pe):
                for j in range(NT):
                    for c in range(2):
                        i = pe.matmul(bank(j, SEQ - j * P), R_K[:, c, j * P:(j + 1) * P], R_Q[:, c, j * P:SEQ],
                                      start=(c == 0), stop=(c == 1))
                    i.then_inc(self.s("scored"), 1)
                for i in range(NT):
                    pe.wait_ge(self.s("decayed"), self.at("decayed") + i + 1)
                    for j in range(i + 1):
                        m = pe.matmul(bank(4 + i), R_ST[:, j, (i - j) * P:(i - j + 1) * P], R_V[:, j, :],
                                      start=(j == 0), stop=(j == i))
                    m.then_inc(self.s("weighed"), 1)
                pe.wait_ge(self.s("gated"), self.at("gated") + NT)
                for c in range(4):
                    for i in range(NT):
                        m = pe.transpose(bank(c)[:, i * P:(i + 1) * P], R_Y[:, i, c * P:(c + 1) * P], ident)
                    m.then_inc(self.s("turned"), 1)

            def dve(self, dve):
                for j in range(NT):
                    dve.wait_ge(self.s("scored"), self.at("scored") + j + 1)
                    dve.tensor_tensor(R_ST[:, j, 0:SEQ - j * P], bank(j, SEQ - j * P), R_DEC[:, self.h, 0:SEQ - j * P], ALU.mult)\
                        .then_inc(self.s("decayed"), 1)
                for i in range(NT):
                    dve.wait_ge(self.s("weighed"), self.at("weighed") + i + 1)
                    dve_step.then(dve, dve.bn_stats(R_BN[:, i, :], bank(4 + i)))
                    ins = dve.bn_aggr(R_MV[:, i, :], R_BN[:, i, :])
                dve_step.then(dve, ins)
                dve.tensor_copy(st[:, 0, 0:NT], R_MV[:, :, 1]).then_inc(self.s("squares"), 1)
                inverse_roots(self, dve, NT, 1)
                for i in range(NT):
                    dve.tensor_scalar(R_Y[:, i, :], bank(4 + i), R_MV[:, i, 0:1], st[:, 3, i:i + 1], ALU.subtract, ALU.mult)\
                        .then_inc(self.s("normed"), 1)
                for c in range(0, 4, 2):
                    self.take(dve, c)

            def take(self, eng, c):
                eng.wait_ge(self.s("turned"), self.at("turned") + c + 1)
                at = V_GN + 4 * self.h + c
                if c % 2:
                    eng.activation(R_YT[:, c, :], bank(c), ACT.Copy, scale=cols[:, at:at + 1])
                else:
                    eng.tensor_scalar(R_YT[:, c, :], bank(c), cols[:, at:at + 1], None, ALU.mult)

            def pool(self, pool):
                for i in range(NT):
                    pool.wait_ge(self.s("normed"), self.at("normed") + i + 1)
                    pool.tensor_tensor(R_Y[:, i, :], R_Y[:, i, :], R_G[:, i, :], ALU.mult).then_inc(self.s("gated"), 1)

            def act(self, act):
                roots(self, act, NT)
                for c in range(1, 4, 2):
                    self.take(act, c)

        M_ROWS = region(24128, 2, P)

        def modulation(p, unit, layer, q):
            x = M_ROWS[:, q % 2, :]

            def fill(pe, ps):
                w = Weights.view(unit, 0, KC, 512)
                for c in range(KC):
                    for g in range(4):
                        i = pe.matmul(ps[0][32 * g:32 * g + 32, 0:P], cmod[:, c, :], w[:, c, g * P:(g + 1) * P],
                                      start=(c == 0), stop=(c == KC - 1))
                return i
            rows = p.job("v", fill, lambda dve, ps: dve.tensor_copy(x, ps[0][:, 0:P]), units=(unit,), release=(1,))

            def take(dve, ps):
                b = adab[:, 24 * layer + 4 * q:24 * layer + 4 * q + 4].unsqueeze(2).broadcast_to([P, 4, 2])
                both = ps[0][:, 0:P].rearrange("p (g r) -> p g r", g=4)[:, :, 0:2]
                m = dve.tensor_tensor(modc[:, layer, 4 * q:4 * q + 4, :], both, b, ALU.add)
                if q != 3:
                    return m
                dve_step.then(dve, m)
                g = cols[:, V_NG + KC * layer:V_NG + KC * (layer + 1)].unsqueeze(2).broadcast_to([P, KC, 2])
                return dve.scalar_tensor_tensor(amod[:, layer], modc[:, layer, 8:16, :], 1.0, g, ALU.add, ALU.mult)
            return lambda: p.job("v", turn([x]), take, after=[rows])

        def retention():
            Norm("n1", H, D, NT, gain_cols(V_MIX + KC), None, XT, 0, region(0, NT, D))
            w = io["ret_w_in"][0]
            for h in range(RET_H):
                p = Products(f"ret{h}")
                columns = [divmod(n, 6) for n in range(3 * h, 3 * h + 3)]

                def modulation_unit(n):
                    layer, q = columns[n]
                    return Weights.add((0, KC, 512, io["ada_w_2"][layer][:, 512 * q:512 * (q + 1)]))
                qk = Weights.add((0, KC, 256, w[:, 256 * h:256 * (h + 1)]), (2048, KC, 256, w[:, D + 256 * h:D + 256 * (h + 1)]))
                m0 = modulation_unit(0)
                uv = Weights.add((0, KC, 512, w[:, 2 * D + 512 * h:2 * D + 512 * (h + 1)]))
                m1 = modulation_unit(1)
                ug = Weights.add((0, KC, 512, w[:, 4 * D + 512 * h:4 * D + 512 * (h + 1)]))
                m2 = modulation_unit(2)
                use_units(p, qk, m0, uv, m1, ug, m2)
                if h == 0:
                    loads(p, (R_ROT, io["rot"]), (R_DEC, io["decay"]))
                for i, dst in enumerate((R_Q, R_K)):
                    def fill(pe, ps, i=i, qk=qk):
                        wv = Weights.view(qk, 2048 * i, KC, 256)
                        for b in range(2):
                            for c in range(KC):
                                m = pe.matmul(ps[b], wv[:, c, b * P:(b + 1) * P], XT[:, c, 0:SEQ], start=(c == 0), stop=(c == KC - 1))
                        return m

                    def take(dve, ps, i=i, dst=dst, h=h, p=p):
                        cos, sin = R_ROT[:, 0, :], R_ROT[:, 1, :]
                        t = R_TMP[:, i]
                        if h == 0 and i == 0:
                            dve.wait_ge(p.s("small"), p.at("small") + 32)
                        dve.tensor_tensor(t[:, 0, :], ps[0], cos, ALU.mult)
                        dve.tensor_tensor(t[:, 1, :], ps[1], sin, ALU.mult)
                        dve.tensor_tensor(t[:, 2, :], ps[0], sin, ALU.mult)
                        dve_step.then(dve, dve.tensor_tensor(t[:, 3, :], ps[1], cos, ALU.mult))
                        dve.tensor_tensor(dst[:, 0, :], t[:, 0, :], t[:, 1, :], ALU.subtract)
                        return dve.tensor_tensor(dst[:, 1, :], t[:, 2, :], t[:, 3, :], ALU.add)
                    p.job("v", fill, take, units=(qk,), release=(1,) if i else (), n_banks=2)
                turned = modulation(p, m0, *columns[0])
                for t in range(NT):
                    p.job("a", mm_R(uv, 0, KC, 512, 0, 512, XT, t), act_out(R_V[:, t, :], ACT.Copy), units=(uv,),
                          release=(1,) if t == 3 else ())
                turned()
                turned = modulation(p, m1, *columns[1])
                for t in range(NT):
                    p.job("a", mm_R(ug, 0, KC, 512, 0, 512, XT, t), act_out(R_G[:, t, :], ACT.Silu), units=(ug,),
                          release=(1,) if t == 3 else ())
                turned()
                modulation(p, m2, *columns[2])()
                Retain(f"rn{h}", h)
                u = Weights.add((0, 4, D, io["ret_w_out"][0][512 * h:512 * (h + 1), :]))
                use_units(OutProj(f"ro{h}", u, 4, R_YT, NT), u)

        def mod_norms(layer):
            for g, (rows, tiles, tok0) in enumerate(((H, NT, 0), (HC, NCT, SEQ))):
                Norm(f"m{layer}{g}", rows, D, tiles, lambda c, g=g: amod[:, layer, c, g:g + 1],
                     lambda c, g=g: modc[:, layer, c, g:g + 1], XT, tok0, region(0, NT, D))

        def tok_T(p, us, at, k, n, cs, x, dst, take_of, eng, ctx_too=True, release=False):
            p.job(eng, mm_T(us, at, k, n, cs, x, 0, SEQ), take_of(dst[:, 0:SEQ]), units=(us,),
                  release=(1,) if release and not ctx_too else ())
            if ctx_too:
                p.job(eng, mm_T(us, at, k, n, cs, x, SEQ, CTX), take_of(dst[:, SEQ:SEQ + CTX]), units=(us,),
                      release=(1,) if release else ())

        def mixer_a():
            QT, KT = region(12288, 8, NTA * P), region(18432, NTA * P)
            V, ZT = region(19968, NTA, P), region(20736, 4, NTA * P)
            QR, KR, TMP = region(0, 2, 512), region(1024, 2, P), region(1536, 4, 256)
            w = io["ab_in_w_2"][0]
            p = Products("pa")
            uq = Weights.add((0, KC, 512, w[:, 0:512]))
            uk = Weights.add((0, KC, 256, w[:, 512:768]))
            uz = Weights.add((0, KC, 512, w[:, 768:1280]))
            use_units(p, uq, uk, uz)
            zeros(p, *(QT[(1 - g) * DH:(2 - g) * DH, 4 * g:4 * g + 4, :] for g in range(2)))
            turned = [None, None]
            pend = []

            def flush(n):
                while len(pend) > n:
                    f = pend.pop(0)
                    turned[f[0] % 2] = f[1]()
            for t in range(NTA):
                cos = cst[:, C_COSA + 32 * t:C_COSA + 32 * (t + 1)]
                sin = cst[:, C_SINA + 32 * t:C_SINA + 32 * (t + 1)]
                buf = QR[:, t % 2, :]
                if t < NT:
                    take = rope_rows(buf.rearrange("p (h i two) -> p h i two", h=8, two=2),
                                     lambda ps: ps[0][:, 0:512].rearrange("p (h i two) -> p h i two", h=8, two=2),
                                     cos, sin, 8, 32, [TMP[:, i, :].rearrange("p (h i) -> p h i", h=8) for i in range(4)])
                else:
                    take = copy_out("v", buf)
                made = p.job("v", mm_R(uq, 0, KC, 512, 0, 512, XT, t), take, units=(uq,), release=(1,) if t == NTA - 1 else (),
                             after=[turned[t % 2]] if turned[t % 2] else [], scratch=True)

                def later(t=t, buf=buf, made=made):
                    def take(eng, ps):
                        for g in range(2):
                            for hh in range(2):
                                src = ps[0][hh * DH:(hh + 1) * DH, g * 2 * P:(g + 1) * 2 * P].rearrange("p (c t) -> p c t", c=2)
                                i = eng.activation(QT[g * DH:(g + 1) * DH, 4 * g + hh:4 * g + 4:2, t * P:(t + 1) * P],
                                                   src, ACT.Copy, scale=DH ** -0.5)
                        return i
                    return p.job("a", turn([buf[:, c * P:(c + 1) * P] for c in range(4)]), take, after=[made])
                pend.append((t, later))
                flush(1)
            flush(0)
            turned = [None, None]
            for t in range(NTA):
                cos = cst[:, C_COSA + 32 * t:C_COSA + 32 * (t + 1)]
                sin = cst[:, C_SINA + 32 * t:C_SINA + 32 * (t + 1)]
                kr = KR[:, t % 2, :]

                def take(dve, ps, t=t, kr=kr, cos=cos, sin=sin):
                    dve.tensor_copy(V[:, t, :], ps[0][:, P:2 * P])
                    if t >= NT:
                        return dve.tensor_copy(kr, ps[0][:, 0:P])
                    return rope_rows(kr.rearrange("p (h i two) -> p h i two", h=2, two=2),
                                     lambda ps: ps[0][:, 0:P].rearrange("p (h i two) -> p h i two", h=2, two=2),
                                     cos, sin, 2, 32, [TMP[:, j, 0:64].rearrange("p (h i) -> p h i", h=2) for j in range(4)])(dve, ps)
                made = p.job("v", mm_R(uk, 0, KC, 256, 0, 256, XT, t), take, units=(uk,), release=(1,) if t == NTA - 1 else (),
                             after=[turned[t % 2]] if turned[t % 2] else [], scratch=True)

                def later(t=t, kr=kr, made=made):
                    return p.job("a", turn([kr]), copy_out("a", KT[:, t * P:(t + 1) * P]), after=[made])
                pend.append((t, later))
                flush(1)
            flush(0)
            for n in range(4):
                tok_T(p, uz, 0, KC, 512, (n * P, n * P + P), XT, ZT[:, n, :], lambda d: act_out(d, ACT.Silu), "a", release=n == 3)

            anti, causal = cst[:, C_ANTI:C_ANTI + P], cst[:, C_CAUSAL:C_CAUSAL + P]
            lo = lambda i: max(0, i - 1)
            hi = lambda i: min(NT, i + 2)
            width = lambda i: (hi(i) - lo(i)) * P

            def kT(a, b):
                return KT[:, a * P:b * P]

            def adds(i):
                r = []
                if i > 0:
                    r.append((512 - width(i), 512 - width(i) + P, anti))
                if i < NT - 1:
                    r.append((512 - P, 512, causal))
                return r
            Attend("aa", 8, NT, lambda i: (512 - width(i), 768),
                   lambda h, i: [(512 - width(i), 512, QT[:, h, i * P:(i + 1) * P], kT(lo(i), hi(i))),
                                 (512, 768, QT[:, h, i * P:(i + 1) * P], kT(NT, NTA))],
                   lambda i: [*range(lo(i), hi(i)), NT, NT + 1], lambda h, kt: V[:, kt, (h // 4) * DH:(h // 4 + 1) * DH],
                   lambda q: ZT[:, q, 0:SEQ], lambda q: ZT[:, q, 0:SEQ], add=adds, sink=True)
            Attend("ac", 8, NCT, lambda i: (0, CTX),
                   lambda h, i: [(0, CTX, QT[:, h, (NT + i) * P:(NT + i + 1) * P], kT(NT, NTA))],
                   lambda i: [NT, NT + 1], lambda h, kt: V[:, kt, (h // 4) * DH:(h // 4 + 1) * DH],
                   lambda q: ZT[:, q, SEQ:SEQ + CTX], lambda q: ZT[:, q, SEQ:SEQ + CTX], sink=True)
            u = Weights.add((0, 4, D, io["ab_out_w_2"][0][0:512, :]))
            use_units(OutProj("oa", u, 4, ZT, NTA, 0), u)

        def mixer_b():
            cqT, ckvT, KR = region(12288, 3, NTA * P), region(14592, 2, NTA * P), region(16128, NTA, B_ROPE)
            QT, KT = region(16320, 4, NTA * P), region(19392, 4, NTA * P)
            V, ZT = region(22464, NTA, 256), region(24000, 2, NTA * P)
            CQ, CKV = region(0, NTA, Q_LORA), region(2304, NTA, KV_LORA)
            TMP = region(4096, 4, 64)
            w = io["ab_in_w_2"][0]
            p = Products("pb")
            u1 = Weights.add((0, KC, 384, w[:, 1280:1664]))
            u2 = Weights.add((0, KC, 288, w[:, 1664:1952]))
            use_units(p, u1, u2)
            for t in range(NTA):
                s = "va"[t % 2]
                p.job(s, mm_R(u1, 0, KC, 384, 0, 384, XT, t), copy_out(s, CQ[:, t, :]), units=(u1,),
                      release=(1,) if t == NTA - 1 else ())

            def tabs(t):
                return cst[:, C_COSB + 16 * t:C_COSB + 16 * (t + 1)], cst[:, C_SINB + 16 * t:C_SINB + 16 * (t + 1)]
            for t in range(NTA):
                def take(dve, ps, t=t):
                    dve.tensor_copy(CKV[:, t, :], ps[0][:, 0:256])
                    kr = ps[0][:, 256:288]
                    if t >= NT:
                        return dve.tensor_copy(KR[:, t, :], kr)
                    cos, sin = tabs(t)
                    return rope_rows(KR[:, t, :].rearrange("p (h i two) -> p h i two", h=1, two=2),
                                     lambda ps: kr.rearrange("p (h i two) -> p h i two", h=1, two=2),
                                     cos, sin, 1, 16, [TMP[:, j, 0:16].rearrange("p (h i) -> p h i", h=1) for j in range(4)])(dve, ps)
                p.job("v", mm_R(u2, 0, KC, 288, 0, 288, XT, t), take, units=(u2,), release=(1,) if t == NTA - 1 else (), scratch=True)
            for nm, rows, width, at, dst in (("q", CQ, Q_LORA, V_BQ, cqT), ("k", CKV, KV_LORA, V_BKV, ckvT)):
                Norm(f"b{nm}l", rows[:, 0:NT, :], width, NT, gain_cols(at), None, dst, 0, rows[:, 0:NT, :])
                Norm(f"b{nm}c", rows[:, NT:NTA, :], width, NCT, gain_cols(at), None, dst, SEQ, rows[:, NT:NTA, :])
            QR, KRW = region(0, 2, 4, B_QK), region(768, 2, 4, B_QK)
            TQ = region(2048, 4, 64)
            scale = B_QK ** -0.5
            for g in range(2):
                p = Products(f"pb{g}")
                uq = Weights.add((0, 3, 384, io["b_w_uq_2"][0][:, 384 * g:384 * (g + 1)]),
                                 (1152, 2, 512, io["b_w_ukv_2"][0][:, 512 * g:512 * (g + 1)]))
                uz = Weights.add((0, KC, 256, w[:, 1952 + 256 * g:1952 + 256 * (g + 1)]))
                use_units(p, uq, uz)
                turned, pend = [[None, None], [None, None]], []

                def flush(n):
                    while len(pend) > n:
                        which, t, f = pend.pop(0)
                        turned[which][t % 2] = f()
                for t in range(NTA):
                    def takeq(dve, ps, t=t):
                        src = ps[0][:, 0:384].rearrange("p (h d) -> p h d", h=4)
                        dst = QR[:, t % 2]
                        i = dve.tensor_copy(dst[:, :, 0:B_NOPE], src[:, :, 0:B_NOPE])
                        if t >= NT:
                            return dve.tensor_copy(dst[:, :, B_NOPE:B_QK], src[:, :, B_NOPE:B_QK])
                        cos, sin = tabs(t)
                        return rope_rows(dst[:, :, B_NOPE:B_QK].rearrange("p h (i two) -> p h i two", two=2),
                                         lambda ps: src[:, :, B_NOPE:B_QK].rearrange("p h (i two) -> p h i two", two=2),
                                         cos, sin, 4, 16, [TQ[:, j, :].rearrange("p (h i) -> p h i", h=4) for j in range(4)])(dve, ps)

                    def takek(dve, ps, t=t):
                        src = ps[0].rearrange("p (h d) -> p h d", h=4)
                        dst = KRW[:, t % 2]
                        dve.tensor_copy(dst[:, :, 0:B_NOPE], src[:, :, 0:B_NOPE])
                        dve.tensor_copy(V[:, t, :].rearrange("p (h d) -> p h d", h=4), src[:, :, B_NOPE:B_NOPE + B_V])
                        return dve.tensor_copy(dst[:, :, B_NOPE:B_QK], KR[:, t, :].unsqueeze(1).broadcast_to([P, 4, B_ROPE]))
                    for which, fill, take, buf, dst, sc in (
                            (0, mm_R(uq, 0, 3, 384, 0, 384, cqT, t), takeq, QR, QT, scale),
                            (1, mm_R(uq, 1152, 2, 512, 0, 512, ckvT, t), takek, KRW, KT, None)):
                        made = p.job("v", fill, take, units=(uq,), release=(1,) if which and t == NTA - 1 else (),
                                     after=[turned[which][t % 2]] if turned[which][t % 2] else [], scratch=True)

                        def later(t=t, buf=buf, dst=dst, sc=sc, made=made):
                            def take(eng, ps):
                                src = ps[0][0:B_QK, :].rearrange("p (h t) -> p h t", h=4)
                                return eng.activation(dst[0:B_QK, :, t * P:(t + 1) * P], src, ACT.Copy, scale=sc or 1.0)
                            return p.job("a", turn([buf[:, t % 2, h, :] for h in range(4)]), take, after=[made])
                        pend.append((which, t, later))
                        flush(2)
                flush(0)
                for n in range(2):
                    tok_T(p, uz, 0, KC, 256, (n * P, n * P + P), XT, ZT[:, n, :], lambda d: act_out(d, ACT.Silu), "a", release=n == 1)
                q = lambda h, t: QT[0:B_QK, h, t * P:(t + 1) * P]
                v = lambda h, kt: V[:, kt, h * DH:(h + 1) * DH]
                Attend(f"ba{g}", 4, NT, lambda i: (0, 768),
                       lambda h, i: [(0, 512, q(h, i), KT[0:B_QK, h, 0:SEQ]), (512, 768, q(h, i), KT[0:B_QK, h, SEQ:SEQ + CTX])],
                       lambda i: range(NTA), v, lambda r: ZT[:, r, 0:SEQ], lambda r: ZT[:, r, 0:SEQ])
                Attend(f"bc{g}", 4, NCT, lambda i: (0, CTX),
                       lambda h, i: [(0, CTX, q(h, NT + i), KT[0:B_QK, h, SEQ:SEQ + CTX])],
                       lambda i: [NT, NT + 1], v, lambda r: ZT[:, r, SEQ:SEQ + CTX], lambda r: ZT[:, r, SEQ:SEQ + CTX])
                u = Weights.add((0, 2, D, io["ab_out_w_2"][0][512 + 256 * g:512 + 256 * (g + 1), :]))
                use_units(OutProj(f"ob{g}", u, 2, ZT, NTA, 0), u)

        class Neighbours(Attend):
            table = 1
            TT = region(22528, 2, 2, 14, GRID)

            def load(self, act, h):
                for j0, p0 in ((1, 0), (0, GRID)):
                    act.dma_start(self.TT[p0:p0 + GRID, h // 2 % 2, h % 2], io["bands"][self.h0 + h, :, j0:j0 + 14, :])\
                        .then_inc(self.s(f"bias{h // 2 % 2}"), 16)

            def act(self, act):
                for h in range(4):
                    self.load(act, h)
                super().act(act)

            def before_exp(self, act, n):
                pair, r = divmod(n, 2 * self.nq)
                if r == 0 and 1 <= pair < self.heads // 2 - 1:
                    act.wait_ge(self.s("max"), self.at("max") + n)
                    for h in range(2 * pair + 2, 2 * pair + 4):
                        self.load(act, h)

            def maximum(self, dve, n):
                h, i = self.at_unit(n)
                if i == 0:
                    dve.wait_ge(self.s("banded"), self.at("banded") + h + 1)
                tt = self.TT[:, h // 2 % 2, h % 2].rearrange("p j k -> p (j k)")
                at = (6 - 2 * i) * GRID
                m, x = sm[:, 0, n:n + 1], self.s_at(n, 0, SEQ)
                dve_step.then(dve, dve.tensor_reduce(m, self.s_at(n, SEQ, SEQ + CTX), AXX, ALU.max))
                dve_step.then(dve, dve.tensor_tensor_reduce(x, x, tt[:, at:at + SEQ], 1.0, m, ALU.add, ALU.max, m))
                return dve.tensor_scalar(m, m, -1.0, None, ALU.mult)

            def pool(self, pool):
                for h in range(self.heads):
                    x, s = self.TT[:, h // 2 % 2, h % 2], f"bias{h // 2 % 2}"
                    pool.wait_ge(self.s(s), self.at(s) + 64 * (h // 4 + 1))
                    pool.tensor_tensor(x, x, cst[:, C_WIN:C_WIN + GRID].unsqueeze(1).broadcast_to([P, 14, GRID]), ALU.add)\
                        .then_inc(self.s("banded"), 1)

        def mixer_c():
            w = io["c_in_w_2"][0]
            for g in range(2):
                QT, KT = region(6144, 2, 4, SEQ), region(10240, 4, NTA * P)
                V, ZT = region(13312, NTA, 512), region(16384, 4, SEQ)
                p = Products(f"pc{g}")
                us = [Weights.add((0, KC, 512, w[:, D * i + 512 * g:D * i + 512 * (g + 1)])) for i in range(4)]
                use_units(p, *us)
                zeros(p, *(QT[(1 - hh) * DH:(2 - hh) * DH, hh] for hh in range(2)))
                for n in range(4):
                    def take(dve, ps, n=n, QT=QT):
                        for hh in range(2):
                            r = slice(hh * DH, (hh + 1) * DH)
                            i = dve.tensor_scalar(QT[r, hh, n, :], ps[0][r, :], DH ** -0.5, None, ALU.mult)
                        return i
                    p.job("v", mm_T(us[0], 0, KC, 512, (n * P, n * P + P), XT, 0, SEQ), take, units=(us[0],),
                          release=(1,) if n == 3 else ())
                for n in range(4):
                    tok_T(p, us[1], 0, KC, 512, (n * P, n * P + P), XT, KT[:, n, :], lambda d: copy_out("a", d), "a", True, n == 3)
                for t in range(NTA):
                    s = "va"[t % 2]
                    p.job(s, mm_R(us[2], 0, KC, 512, 0, 512, XT, t), copy_out(s, V[:, t, :]), units=(us[2],),
                          release=(1,) if t == NTA - 1 else ())
                for n in range(4):
                    tok_T(p, us[3], 0, KC, 512, (n * P, n * P + P), XT, ZT[:, n, :], lambda d: act_out(d, ACT.Silu), "a", False, n == 3)

                def scores(h, i, QT=QT, KT=KT):
                    q = QT[:, h % 2, h // 2, i * P:(i + 1) * P]
                    return [(0, SEQ, q, KT[:, h // 2, 0:SEQ]), (SEQ, SEQ + CTX, q, KT[:, h // 2, SEQ:SEQ + CTX])]
                a = Neighbours(f"na{g}", 8, NT, lambda i: (0, 768), scores,
                               lambda i: range(NTA), lambda h, kt, V=V: V[:, kt, h * DH:(h + 1) * DH],
                               lambda r, ZT=ZT: ZT[:, r, :], lambda r, ZT=ZT: ZT[:, r, :])
                a.h0 = 8 * g
                u = Weights.add((0, 4, D, io["c_out_w_2"][0][512 * g:512 * (g + 1), :]))
                use_units(OutProj(f"oc{g}", u, 4, ZT, NT, 1), u)

        parts = [lambda: Start("start"), fox, lambda: moe(0), retention, lambda: moe(1),
                 lambda: RowNorm("nfin", io["norm_final"]), lambda: mod_norms(0), mixer_a, mixer_b,
                 lambda: mod_norms(1), mixer_c, lambda: RowNorm("last", io["final_g_2"], io["out"])]
        for part in parts:
            part()

        block = ctx.enter_context(nc.Block())
        n_stage = len(stages)

        def run(eng, what):
            for k, stage in enumerate(stages):
                if k:
                    eng.wait_ge(stage_done, 4 * k)
                dict(pe=stage.pe, act=stage.act, dve=stage.dve, pool=stage.pool)[what](eng)
                eng.drain().then_inc(stage_done, 1)

        @block.sync
        def _(sp):
            for stage in stages:
                stage.sp(sp)
            sp.wait_ge(stage_done, 4 * n_stage)

        @block.tensor
        def _(pe):
            run(pe, "pe")

        @block.scalar
        def _(act):
            run(act, "act")

        @block.vector
        def _(dve):
            run(dve, "dve")

        @block.gpsimd
        def _(pool):
            run(pool, "pool")




def kernel(**inputs):
    import concourse.bacc as bacc
    from concourse.bass_utils import run_bass_kernel_spmd

    nc = bacc.Bacc("TRN2", target_bir_lowering=False, num_devices=1, dynamic_dma_scratch_size=8192)
    consts, rot, decay = constants()
    arrays = {f"in_{k}": np.ascontiguousarray(v) for k, v in inputs.items()}
    arrays |= {"in_consts": consts, "in_rot": rot, "in_decay": decay, "in_bands": bands(np.asarray(inputs["c_rpb_2"])[0])}
    io = {k[3:]: nc.dram_tensor(k, a.shape, mybir.dt.from_np(a.dtype), kind="ExternalInput").ap() for k, a in arrays.items()}
    io["out"] = nc.dram_tensor("out", (1, SEQ, D), F32, kind="ExternalOutput").ap()
    build(nc, io)
    r = run_bass_kernel_spmd(nc, [arrays], core_ids=[0])
    return r.results[0]["out"]
```
